# Optimizing a Trainium2 kernel written in Bass

```python
import jax, jax.numpy as jnp
from jax import lax
import numpy as np

D_MODEL = 1024
BATCH = 1
SEQ = 512
DEPTH = 1

GRID_W = 64
CTX_LEN = 256
D_MIX = D_MODEL
D_REC = D_MIX // 2
D_ATT = D_MIX - D_REC
HEAD_DIM = 64
N_ATT_HEADS = D_ATT // HEAD_DIM
N_REC_BLOCKS = 8
REC_BLOCK = D_REC // N_REC_BLOCKS
CONV_W = 4
CONV_PAD_LEFT = 2
LRU_C = 8.0
WIN_ROWS = 8
WIN_COLS = 16
D_FF = 2816
N_MOD = 9
RES_W_FFN = 0.5
EPS = 1e-6
NEG_INF = -1e30
C_RG = D_REC
C_Q = 2 * D_REC
C_K = C_Q + D_ATT
C_V = C_K + D_ATT
D_IN = C_V + D_ATT

kernel_name = "hybrid_rglru_natten_macaron_dit_layer"

def rmsnorm(x, g):
    xf = x.astype(jnp.float32)
    y = xf * lax.rsqrt(jnp.mean(xf * xf, axis=-1, keepdims=True) + EPS)
    return (y * g.astype(jnp.float32)).astype(x.dtype)

def modulated_norm(x, g, mod, idx):
    shift = mod[:, 3 * idx][:, None]
    scale = mod[:, 3 * idx + 1][:, None]
    return rmsnorm(x, g) * (1.0 + scale) + shift

def gated_residual(x, y, g, mod, idx, res_w):
    gate = mod[:, 3 * idx + 2][:, None]
    return x + res_w * gate * rmsnorm(y, g)

def sublayer(x, mod, idx, g_pre, g_post, fn, res_w):
    return gated_residual(x, fn(modulated_norm(x, g_pre, mod, idx)), g_post, mod, idx, res_w)

def swiglu(h, w_gu, w_down):
    g, u = jnp.split(h @ w_gu, 2, axis=-1)
    return (jax.nn.silu(g) * u) @ w_down

def centred_dwconv(x, w, b):
    y = lax.conv_general_dilated(
        x, w[:, None, :], window_strides=(1,),
        padding=[(CONV_PAD_LEFT, CONV_W - 1 - CONV_PAD_LEFT)],
        dimension_numbers=("NWC", "WIO", "NWC"), feature_group_count=x.shape[-1])
    return y + b

def linear_scan(a, u, h0, reverse):
    def combine(left, right):
        a_l, b_l = left
        a_r, b_r = right
        return a_l * a_r, a_r * b_l + b_r
    a_cum, b_cum = lax.associative_scan(combine, (a, u), reverse=reverse, axis=1)
    return a_cum * h0[:, None] + b_cum

def rglru_direction(x, wa, ba, wx, bx, lam, h0, reverse):
    b, t, _ = x.shape
    xb = x.reshape(b, t, N_REC_BLOCKS, REC_BLOCK)
    gate_a = jnp.einsum("btnc,ncd->btnd", xb, wa).reshape(b, t, D_REC) + ba
    gate_x = jnp.einsum("btnc,ncd->btnd", xb, wx).reshape(b, t, D_REC) + bx
    log_a = LRU_C * jax.nn.sigmoid(gate_a.astype(jnp.float32)) * jax.nn.log_sigmoid(lam.astype(jnp.float32))
    u = jnp.sqrt(-jnp.expm1(2.0 * log_a)) * jax.nn.sigmoid(gate_x.astype(jnp.float32)) * x.astype(jnp.float32)
    h = linear_scan(jnp.exp(log_a), u, h0, reverse)
    final = h[:, 0] if reverse else h[:, -1]
    return h, final

def rglru_group(xr, xr_ctx, conv_w, conv_b, wa, ba, wx, bx, lam, need_ctx_out):
    xl = centred_dwconv(xr, conv_w, conv_b)
    xc = centred_dwconv(xr_ctx, conv_w, conv_b)
    h0 = jnp.zeros((xc.shape[0], D_REC), jnp.float32)
    ys_lat, ys_ctx = [], []
    for d, rev in enumerate((False, True)):
        hc, h_fin = rglru_direction(xc, wa[d], ba[d], wx[d], bx[d], lam[d], h0, rev)
        hl, _ = rglru_direction(xl, wa[d], ba[d], wx[d], bx[d], lam[d], h_fin, rev)
        ys_lat.append(hl)
        ys_ctx.append(hc)
    y_lat = (ys_lat[0] + ys_lat[1]).astype(xr.dtype)
    y_ctx = (ys_ctx[0] + ys_ctx[1]).astype(xr.dtype) if need_ctx_out else None
    return y_lat, y_ctx

def neighbourhood_attention(q, k, v, k_ctx, v_ctx, rpb):
    b, l = q.shape[:2]
    rows = l // GRID_W
    win_r = min(WIN_ROWS, rows)
    scale = HEAD_DIM ** -0.5

    def to_grid(t):
        return t.reshape(b, rows, GRID_W, N_ATT_HEADS, HEAD_DIM).transpose(0, 3, 1, 2, 4)

    qg, kg, vg = to_grid(q), to_grid(k), to_grid(v)
    col = np.arange(GRID_W)
    col_start = np.clip(col - WIN_COLS // 2, 0, GRID_W - WIN_COLS)
    col_valid = (col[None, :] >= col_start[:, None]) & (col[None, :] < col_start[:, None] + WIN_COLS)
    col_off = np.clip(col[None, :] - col[:, None] + WIN_COLS - 1, 0, 2 * WIN_COLS - 2)
    rpb_cols = rpb.astype(jnp.float32)[:, :, col_off]

    def one_row(args):
        r, q_row = args
        start = jnp.clip(r - win_r // 2, 0, rows - win_r)
        k_band = lax.dynamic_slice_in_dim(kg, start, win_r, axis=2)
        v_band = lax.dynamic_slice_in_dim(vg, start, win_r, axis=2)
        s_loc = jnp.einsum("bhqd,bhjkd->bhqjk", q_row, k_band).astype(jnp.float32) * scale
        row_off = start + jnp.arange(win_r) - r + WIN_ROWS - 1
        bias = jnp.take(rpb_cols, row_off, axis=1).transpose(0, 2, 1, 3)
        s_loc = jnp.where(col_valid[:, None, :], s_loc + bias, NEG_INF)
        s_ctx = jnp.einsum("bhqd,bhkd->bhqk", q_row, k_ctx).astype(jnp.float32) * scale
        s = jnp.concatenate([s_loc.reshape(b, N_ATT_HEADS, GRID_W, win_r * GRID_W), s_ctx], axis=-1)
        p = jax.nn.softmax(s, axis=-1)
        p_loc = p[..., :win_r * GRID_W].reshape(b, N_ATT_HEADS, GRID_W, win_r, GRID_W).astype(v.dtype)
        p_ctx = p[..., win_r * GRID_W:].astype(v.dtype)
        return (jnp.einsum("bhqjk,bhjkd->bhqd", p_loc, v_band)
                + jnp.einsum("bhqk,bhkd->bhqd", p_ctx, v_ctx))

    out = lax.map(one_row, (jnp.arange(rows), qg.transpose(2, 0, 1, 3, 4)))
    return out.transpose(1, 0, 3, 2, 4).reshape(b, l, D_ATT)

def context_attention(q_ctx, k_ctx, v_ctx):
    s = jnp.einsum("bhqd,bhkd->bhqk", q_ctx, k_ctx).astype(jnp.float32) * HEAD_DIM ** -0.5
    p = jax.nn.softmax(s, axis=-1).astype(v_ctx.dtype)
    o = jnp.einsum("bhqk,bhkd->bhqd", p, v_ctx)
    b, _, t, _ = o.shape
    return o.transpose(0, 2, 1, 3).reshape(b, t, D_ATT)

def split_heads(t):
    return t.reshape(t.shape[0], t.shape[1], N_ATT_HEADS, HEAD_DIM)

def mixer(h, hc, w_in, w_out, conv_w, conv_b, wa, ba, wx, bx, lam, rpb, need_ctx_out):
    p = h @ w_in
    xr, gr, q, k, v = p[..., :C_RG], p[..., C_RG:C_Q], p[..., C_Q:C_K], p[..., C_K:C_V], p[..., C_V:]
    xr_ctx = hc @ w_in[:, :C_RG]
    kv_ctx = hc @ w_in[:, C_K:]
    k_ctx = split_heads(kv_ctx[..., :D_ATT]).transpose(0, 2, 1, 3)
    v_ctx = split_heads(kv_ctx[..., D_ATT:]).transpose(0, 2, 1, 3)

    y_rec, y_rec_ctx = rglru_group(xr, xr_ctx, conv_w, conv_b, wa, ba, wx, bx, lam, need_ctx_out)
    y_att = neighbourhood_attention(split_heads(q), split_heads(k), split_heads(v), k_ctx, v_ctx, rpb)
    y = jnp.concatenate([y_rec * jax.nn.gelu(gr), y_att], axis=-1) @ w_out
    if not need_ctx_out:
        return y, None
    g_ctx = hc @ w_in[:, C_RG:C_Q]
    q_ctx = split_heads(hc @ w_in[:, C_Q:C_K]).transpose(0, 2, 1, 3)
    y_att_ctx = context_attention(q_ctx, k_ctx, v_ctx)
    yc = jnp.concatenate([y_rec_ctx * jax.nn.gelu(g_ctx), y_att_ctx], axis=-1) @ w_out
    return y, yc

def setup_inputs(seed: int = 0) -> dict:
    key = jax.random.key(seed)
    ks = jax.random.split(key, 24)
    nrm = jax.random.normal
    f32 = jnp.float32
    lam_u = jax.random.uniform(ks[20], (DEPTH, 2, D_REC), f32, 0.9, 0.999)
    a0 = lam_u ** (1.0 / LRU_C)
    return {
        "x": nrm(ks[0], (BATCH, SEQ, D_MODEL), f32),
        "c": nrm(ks[1], (BATCH, D_MODEL), f32),
        "ctx": nrm(ks[2], (BATCH, CTX_LEN, D_MODEL), f32),
        "c_ctx": nrm(ks[3], (D_MODEL,), f32),
        "w_mod": nrm(ks[4], (DEPTH, D_MODEL, N_MOD * D_MODEL), f32) * D_MODEL ** -0.5,
        "b_mod": nrm(ks[5], (DEPTH, N_MOD * D_MODEL), f32) * 0.02,
        "norm_pre": 1.0 + 0.05 * nrm(ks[6], (DEPTH, 3, D_MODEL), f32),
        "norm_post": 1.0 + 0.05 * nrm(ks[7], (DEPTH, 3, D_MODEL), f32),
        "ffn1_w_gu": nrm(ks[8], (DEPTH, D_MODEL, 2 * D_FF), f32) * D_MODEL ** -0.5,
        "ffn1_w_down": nrm(ks[9], (DEPTH, D_FF, D_MODEL), f32) * D_FF ** -0.5,
        "ffn2_w_gu": nrm(ks[10], (DEPTH, D_MODEL, 2 * D_FF), f32) * D_MODEL ** -0.5,
        "ffn2_w_down": nrm(ks[11], (DEPTH, D_FF, D_MODEL), f32) * D_FF ** -0.5,
        "w_in": nrm(ks[12], (DEPTH, D_MODEL, D_IN), f32) * D_MODEL ** -0.5,
        "w_out": nrm(ks[13], (DEPTH, D_MIX, D_MODEL), f32) * D_MIX ** -0.5,
        "conv_w": nrm(ks[14], (DEPTH, CONV_W, D_REC), f32) * CONV_W ** -0.5,
        "conv_b": nrm(ks[15], (DEPTH, D_REC), f32) * 0.02,
        "lru_wa": nrm(ks[16], (DEPTH, 2, N_REC_BLOCKS, REC_BLOCK, REC_BLOCK), f32) * REC_BLOCK ** -0.5,
        "lru_ba": nrm(ks[17], (DEPTH, 2, D_REC), f32) * 0.02,
        "lru_wx": nrm(ks[18], (DEPTH, 2, N_REC_BLOCKS, REC_BLOCK, REC_BLOCK), f32) * REC_BLOCK ** -0.5,
        "lru_bx": nrm(ks[19], (DEPTH, 2, D_REC), f32) * 0.02,
        "lru_lambda": jnp.log(a0) - jnp.log1p(-a0),
        "na_rpb": nrm(ks[21], (DEPTH, N_ATT_HEADS, 2 * WIN_ROWS - 1, 2 * WIN_COLS - 1), f32) * 0.1,
    }

def reference(x, c, ctx, c_ctx, w_mod, b_mod, norm_pre, norm_post, ffn1_w_gu, ffn1_w_down,
              ffn2_w_gu, ffn2_w_down, w_in, w_out, conv_w, conv_b, lru_wa, lru_ba, lru_wx,
              lru_bx, lru_lambda, na_rpb):
    b = x.shape[0]
    xc = ctx
    for l in range(DEPTH):
        last = l == DEPTH - 1
        mod = (jax.nn.silu(c) @ w_mod[l] + b_mod[l]).reshape(b, N_MOD, D_MODEL)
        mod_c = (jax.nn.silu(c_ctx)[None] @ w_mod[l] + b_mod[l]).reshape(1, N_MOD, D_MODEL)
        ffn1 = lambda h: swiglu(h, ffn1_w_gu[l], ffn1_w_down[l])
        ffn2 = lambda h: swiglu(h, ffn2_w_gu[l], ffn2_w_down[l])

        x = sublayer(x, mod, 0, norm_pre[l, 0], norm_post[l, 0], ffn1, RES_W_FFN)
        xc = sublayer(xc, mod_c, 0, norm_pre[l, 0], norm_post[l, 0], ffn1, RES_W_FFN)

        h = modulated_norm(x, norm_pre[l, 1], mod, 1)
        hc = modulated_norm(xc, norm_pre[l, 1], mod_c, 1)
        y, yc = mixer(h, hc, w_in[l], w_out[l], conv_w[l], conv_b[l], lru_wa[l], lru_ba[l],
                      lru_wx[l], lru_bx[l], lru_lambda[l], na_rpb[l], need_ctx_out=not last)
        x = gated_residual(x, y, norm_post[l, 1], mod, 1, 1.0)
        if not last:
            xc = gated_residual(xc, yc, norm_post[l, 1], mod_c, 1, 1.0)

        x = sublayer(x, mod, 2, norm_pre[l, 2], norm_post[l, 2], ffn2, RES_W_FFN)
        if not last:
            xc = sublayer(xc, mod_c, 2, norm_pre[l, 2], norm_post[l, 2], ffn2, RES_W_FFN)
    return x


_drawn_inputs = setup_inputs


def setup_inputs(seed=0):
    import zlib

    import numpy as np

    out = dict(_drawn_inputs(seed))
    spreads = {}
    factors = {'conv_b': 3.67, 'lru_ba': 49.223, 'lru_bx': 8.0, 'na_rpb': 50.909}
    for name, (base, spread) in spreads.items():
        noise = np.random.default_rng([zlib.crc32(name.encode()), seed]).standard_normal(out[name].shape)
        drawn = base * np.exp(spread * noise) if base else spread * noise
        out[name] = __import__('jax').numpy.asarray(drawn.astype(out[name].dtype))
    for name, factor in factors.items():
        out[name] = (out[name] * factor).astype(out[name].dtype)
    return out
```

```python
from contextlib import ExitStack

import concourse.bass as bass
from concourse import mybir

F32 = mybir.dt.float32
F32R = mybir.dt.float32r
ALU = mybir.AluOpType
ACT = mybir.ActivationFunctionType
AX_X = mybir.AxisListType.X

P = 128
D = 1024
KC = D // P
HALF_D = D // 2
LAT, CTX = 512, 256
TOK = LAT + CTX
NLT, NCT = LAT // P, CTX // P
NTT = NLT + NCT
FF = 2816
FC = FF // P
PAIRS = FC // 2 - 1
REC = 512
RC = REC // P
GRID_W, ROWS = 64, 8
NH, DH = 8, 64
HPAIRS = NH // 2
QCOLS = 16
KCOLS = 32
NBLK = GRID_W // QCOLS
KSTART = [0, 8, 24, 32]
LOCK = ROWS * KCOLS
UNITS = 2 * NBLK
RPB_R, RPB_C = 15, 31
NEG = -1e30
EPS = 1e-6
LRU_C = 8.0
SLOTS = 6
PADW = 776
SCANW = 772
HSW = SCANW // 2
CTX0 = LAT + 3

R_BMOD, R_PRE, R_C, R_CC, N_R1 = 0, 72, 96, 104, 112
R_POST, R_CW, R_CB, R_BA, R_BX, R_LAM, N_R2 = 0, 24, 40, 44, 52, 60, 68

NM01 = 2 * KC
B1, A1, D1 = (2, 3), (0, 1), (4, 5)
MIX = (2, 3, 0, 1, 4, 5)
B2, A2, D2 = (0, 1), (4, 5), (2, 3)

N_ALT, N_IN, N_OUT = 16, 20, 8
T_GATE = 2 * N_ALT
T_OUT = T_GATE + (N_IN - N_ALT)
N_MIX = T_OUT + N_OUT
GROUPS = [0, 3, 4, 2, 1]
REC_STEP = {1: 0, 2: 1, 4: 2, 5: 3, 7: 4, 8: 5, 10: 6, 11: 7}


def slot_uses():
    u = [0] * SLOTS
    for n in range(NM01):
        u[n % SLOTS] += 1
    ffn1 = list(u)
    for s in B1 + A1 + D1:
        u[s] += FC // 2
    mix = list(u)
    for n in range(N_MIX):
        u[MIX[n % SLOTS]] += 1
    return ffn1, mix, u


U_FFN1, U_MIX, U_FFN2 = slot_uses()


def mix_use(n):
    return MIX[n % SLOTS], U_MIX[MIX[n % SLOTS]] + n // SLOTS


def step_tile(n):
    return 2 * n if n < N_ALT else T_GATE + n - N_ALT


def known(v):
    return isinstance(v, int)


def build(nc, x, c, ctx_in, c_ctx, w_mod, b_mod, norm_pre, norm_post, w_gu1, w_dn1, w_gu2, w_dn2,
          w_in, w_out, conv_w, conv_b, lru_wa, lru_ba, lru_wx, lru_bx, lru_lambda, rpb, out):
    x_t = x.rearrange("b (t p) d -> (b t) p d", p=P)
    ctx_t = ctx_in.rearrange("b (t p) d -> (b t) p d", p=P)
    out_t = out.rearrange("b (t p) d -> (b t) p d", p=P)

    def row_blocks(w):
        return w.rearrange("l (k p) n -> (l k) p n", p=P)

    def col_range(w):
        return w.rearrange("l (k p) n -> p (l k) n", p=P)

    rpb_rows = nc.dram_tensor("rpb_rows", (ROWS, NH, ROWS, GRID_W), F32, kind="Internal").ap()
    rpb_full = nc.dram_tensor("rpb_full", (3, P, NH, LOCK), F32, kind="Internal").ap()

    with ExitStack() as ctx:
        base = 16512
        ctx.enter_context(nc.sbuf_tensor("fence", [P, (229344 - base) // 4], F32))

        def at(name, off, shape, dt=F32):
            return nc.alloc_sbuf_tensor_at(name, shape, dt, offset=base + off)

        YX_O = 0
        HH_O = YX_O + 4 * NTT * D
        HL_O = HH_O + 4 * KC * TOK
        W_O = HL_O + 4 * KC * TOK
        M_O = W_O + 3 * SLOTS * 4 * D
        S_O = M_O + 62656
        YX = at("YX", YX_O, [P, NTT, D])
        HH = at("HH", HH_O, [P, KC, TOK], F32R)
        HL = at("HL", HL_O, [P, KC, TOK], F32R)
        WR = at("WR", W_O, [P, SLOTS, D])
        WH = at("WH", W_O + SLOTS * 4 * D, [P, SLOTS, D], F32R)
        WL = at("WL", W_O + 2 * SLOTS * 4 * D, [P, SLOTS, D], F32R)
        R1 = at("R1", M_O, [P, P])
        R2 = at("R2", M_O + 512, [P, P])
        ZERO = at("ZERO", M_O + 1024, [P, 256])
        LT = at("LT", M_O + 2048, [P, 6, 8])
        AH = at("AH", M_O, [P, 2, TOK], F32R)
        AL = at("AL", M_O + 6144, [P, 2, TOK], F32R)
        SG = at("SG", M_O + 12288, [P, 2, TOK])
        JUNK = at("JUNK", M_O + 12288, [P, D])
        MRAW = at("MRAW", M_O + 18432, [P, 2, 2, 512])
        MACC = at("MACC", M_O + 26624, [P, 2, 512])
        DIAG = at("DIAG", M_O + 18432, [P, 2, KC, P])
        XST = at("XST", M_O + 30720, [P, 2, D])
        GROW = at("GROW", M_O + 38912, [P, 2, D])
        XN_A = at("XN_A", M_O + 18432, [P, 3, D])
        XN_B = at("XN_B", M_O + 47104, [P, 3, D])
        ONES = at("ONES", M_O + 59392, [P, P])
        Y2 = at("Y2", M_O + 18432, [P, NLT, D])
        DIAG2 = at("DIAG2", M_O + 47104, [P, 1, KC, P])
        XR = at("XR", M_O, [P, RC, PADW])
        T = at("T", M_O + 12416, [P, 3, SCANW])
        Q = at("Q", M_O + 21696, [P, HPAIRS, LAT])
        K = at("K", M_O + 29888, [P, HPAIRS, TOK])
        V = at("V", M_O + 42176, [P, HPAIRS, TOK])
        GR = at("GR", M_O + 54464, [P, RC, LAT])
        XC = at("XC", M_O + 54464, [P, SCANW])
        T3 = at("T3", M_O + 54464 + 3104, [P, SCANW])
        GW = at("GW", YX_O + 4 * NLT * D, [P, 2, 2, RC, P])
        HHf = at("HHf", HH_O, [P, KC, TOK])
        HLf = at("HLf", HL_O, [P, KC, TOK])
        VB = HHf[:, :, 0:LAT]
        VC = HLf[:, 0:2, 0:LAT]
        BIAS3 = HHf[:, :, LAT:TOK]
        BIAS0 = HLf[:, :, LAT:TOK]
        BIASM = HLf[:, 2:6, 0:LAT]
        YR6 = at("YR6", M_O + 42176, [P, 6, LAT], F32R)
        YR7 = [at(f"YR7_{j}", HL_O + 4 * TOK * (6 + j), [P, LAT], F32R) for j in range(2)]
        YRH = [YR6[:, j, :] for j in range(4)]
        YRL = [YR6[:, 4, :], YR6[:, 5, :], YR7[0][:, :], YR7[1][:, :]]
        YAH = at("YAH", M_O, [P, HPAIRS, LAT], F32R)
        YAL = at("YAL", M_O + 54464, [P, HPAIRS, LAT], F32R)
        GROW5 = at("GROW5", M_O + 8192, [P, D])
        DIAG5 = at("DIAG5", M_O + 12416, [P, 1, KC, P])
        PR = at("PR", M_O + 12416, [P, 2, LOCK + CTX])
        PT = at("PT", M_O + 16512, [P, 2, LOCK + CTX])
        JUNK5 = at("JUNK5", M_O + 16512, [P, D])
        ONES5 = at("ONES5", M_O + 20608, [P, P])
        MASK = at("MASK", M_O + 21120, [P, 3, KCOLS])
        QS = at("QS", YX_O + 4 * NLT * D, [P, LAT])
        KS = at("KS", YX_O + 4 * NLT * D + 2048, [P, TOK])
        ON = at("ON", YX_O + 4 * NLT * D + 5120, [P, NBLK, P])
        XN5 = at("XN5", M_O + 21696, [P, NLT, D])
        H5 = at("H5", M_O + 38080, [P, 2, LAT])
        so = [S_O]

        def small(name, shape, dt=F32):
            t = at(name, so[0], shape, dt)
            n = 4
            for v in shape[1:]:
                n *= v
            so[0] += (n + 31) // 32 * 32
            assert base + so[0] <= 229344
            return t

        IDENT = small("IDENT", [P, P])
        MOD = small("MOD", [P, 72, 2])
        C1 = small("C1", [P, N_R1])
        C2 = small("C2", [P, N_R2])
        CS = small("CS", [P, 2, KC])
        C4 = small("C4", [P, KC, 4], F32R)
        APRE = small("APRE", [P, KC, 2])
        GCOL = small("GCOL", [P, KC, 2])
        LOGC = small("LOGC", [P, 8])
        SS = small("SS", [P, 32])
        MS = small("MS", [P, 8])
        RS = small("RS", [P, 32])
        MHALF = small("MHALF", [P, 1])
        NMX = small("NMX", [P, UNITS])
        DEN = small("DEN", [P, UNITS])
        RDEN = small("RDEN", [P, UNITS])

        PS = ctx.enter_context(nc.psum_tensor("PS", [P, 8, 512], F32))

        def sem(name):
            return ctx.enter_context(nc.semaphore(name))

        landed, hi_made, lo_made, used = ([sem(f"{n}{i}") for i in range(SLOTS)]
                                          for n in ("landed", "hi_made", "lo_made", "used"))
        x_in = [sem(f"x_in{i}") for i in range(NTT)]
        xst_in = [sem(f"xst_in{i}") for i in range(2)]
        mod_in = [sem(f"mod_in{i}") for i in range(2)]
        rows_in, rpb_zeroed, rpb_put, rpb_spread, bias_in, gw_in, stored = (sem(n) for n in (
            "rows_in", "rpb_zeroed", "rpb_put", "rpb_spread", "bias_in", "gw_in", "stored"))
        zero_set, ident_set, mhalf_set, y_zeroed, gw_zeroed, pads_zeroed, ones_set = (sem(n) for n in (
            "zero_set", "ident_set", "mhalf_set", "y_zeroed", "gw_zeroed", "pads_zeroed", "ones_set"))
        rows_turned, c1_made, c2_made, cs_made, c4_hi, c4_made, lam_abs, lam_exp, logc_made = (sem(n) for n in (
            "rows_turned", "c1_made", "c2_made", "cs_made", "c4_hi", "c4_made", "lam_abs", "lam_exp", "logc_made"))
        mod01_made, a_made, mod_own, mod_red, mod_made, mod78_made = (sem(n) for n in (
            "mod01_made", "a_made", "mod_own", "mod_red", "mod_made", "mod78_made"))
        sq_pre, sq_post, rstd_pre, rstd_post, pool_own, dve_own = (sem(n) for n in (
            "sq_pre", "sq_post", "rstd_pre", "rstd_post", "pool_own", "dve_own"))
        xn_made, turned, h_hi, h_32, h_lo = (sem(n) for n in ("xn_made", "turned", "h_hi", "h_32", "h_lo"))
        silu_made, au_made, a_hi, a_lo = ([sem(f"{n}{r}") for r in range(2)] for n in (
            "silu_made", "au_made", "a_hi", "a_lo"))
        y_ready, y_added, diag_made, grow_ps, grow_made, ysum, scaled, resid = (sem(n) for n in (
            "y_ready", "y_added", "diag_made", "grow_ps", "grow_made", "ysum", "scaled", "resid"))
        proj_out, gelu_out, xc_made, gates, r_sig, x_sig, r_at, om_made, root, scanned = (sem(n) for n in (
            "proj_out", "gelu_out", "xc_made", "gates", "r_sig", "x_sig", "r_at", "om_made", "root", "scanned"))
        vt, vt_act, vt_dve, mask_own, bias_made, yr_f, yr_hi, yr_lo = (sem(n) for n in (
            "vt", "vt_act", "vt_dve", "mask_own", "bias_made", "yr_f", "yr_hi", "yr_lo"))
        qs_made, ks_made, scores, biased, maxed, exps, pt_ps, pt_made, pv, inverted, on_made, ot, ya_hi, ya_lo = (
            sem(n) for n in ("qs_made", "ks_made", "scores", "biased", "maxed", "exps", "pt_ps", "pt_made", "pv",
                             "inverted", "on_made", "ot", "ya_hi", "ya_lo"))
        wo_done = sem("wo_done")

        PRE_T, POST_T = [NTT, NTT, NLT], [NTT, NLT, NLT]
        PRE_C, POST_C = [0, 12, 22], [6, 18, 26]
        PRE_N, POST_N = [0, NTT, 2 * NTT], [0, NTT, NTT + NLT]

        def xn_tile(n, t):
            return (YX[:, t, :], XN_A[:, t, :] if t < 3 else XN_B[:, t - 3, :], XN5[:, min(t, 3), :])[n]

        def h32(n, k):
            return SG[:, k % 2, :] if n < 2 else H5[:, k % 2, :]

        def y_acc(n, t):
            return YX[:, t, :] if n == 0 else Y2[:, t, :]

        def v_dst(j):
            return VB[:, j, :] if j < 8 else VC[:, j - 8, :]

        def ffn_counts(n):
            ntok = TOK if n == 0 else LAT
            return ntok, 2 * ntok // P, n * (FC // 2), n * (PAIRS + 1) * 2 * NTT

        def added_before(n):
            return n * PAIRS * 2 * NTT

        def token_halves(ntok):
            w = 384 if ntok == TOK else 512
            return [(j, slice(w * j, w * j + w), w) for j in range(ntok // w)]

        block = ctx.enter_context(nc.Block())

        @block.sync
        def _(sp):
            def load(s, u, src):
                if not (known(u) and u == 0):
                    sp.wait_ge(lo_made[s], u)
                dst = WR[:, s, :]
                if len(src.shape) == 3:
                    dst = dst.rearrange("p (k n) -> p k n", n=src.shape[2])
                sp.dma_start(dst, src).then_inc(landed[s], 16)

            def at_cols(w, off, n):
                return col_range(w)[:, :, off:off + n] if known(off) else col_range(w)[:, :, bass.ds(off, n)]

            def mix_load(t):
                s, u = mix_use(t)
                if t < T_GATE and t % 2 == 1:
                    m = t // 2
                    src = row_blocks(w_mod)[m // 2][:, (7 + m % 2) * D:(8 + m % 2) * D]
                elif t < T_OUT:
                    n = t // 2 if t < T_GATE else t - T_GATE + N_ALT
                    src = at_cols(w_in, GROUPS[n // 4] * 512 + (n % 4) * P, P)
                else:
                    src = row_blocks(w_out)[t - T_OUT]
                load(s, u, src)

            def ffn_loads(n, w_gu, w_dn, uses, B, A, Dn):
                def up(slots, use, chunk):
                    for g in range(2):
                        load(slots[g], uses[slots[g]] + use, at_cols(w_gu, chunk * P + g * FF, P))

                def down(use, first):
                    for j in range(2):
                        r = first + j
                        src = row_blocks(w_dn)[r] if known(r) else \
                            row_blocks(w_dn)[bass.ds(r, 1)].rearrange("a p n -> p (a n)")
                        load(Dn[j], uses[Dn[j]] + use, src)

                def mod_load(i, q):
                    src = at_cols(w_mod, i * 512 + 2 * D, 512)[:, 2 * q:2 * q + 2, :]
                    sp.dma_start(MRAW[:, q % 2, :, :], src).then_inc(mod_in[q % 2], 16)

                up(B, 0, 0)
                up(A, 0, 1)
                up(B, 1, 2)
                down(0, 0)
                up(A, 1, 3)
                if n == 0:
                    mod_load(0, 0)
                    mod_load(0, 1)
                    spread_bias()

                def pair(i, last):
                    if not last:
                        up(B, i + 2, i * 2 + 4)
                    elif n == 0:
                        mix_load(0)
                        mix_load(1)
                    down(i + 1, i * 2 + 2)
                    if not last:
                        up(A, i + 2, i * 2 + 5)
                    elif n == 0:
                        mix_load(2)
                        mix_load(3)
                    if n == 0:
                        for q in (2, 3):
                            sp.wait_ge(mod_own, i * 16 + 4 * q - 4)
                            mod_load(i, q)
                        if not last:
                            for q in (0, 1):
                                sp.wait_ge(mod_own, i * 16 + 4 * q + 12)
                                mod_load(i + 1, q)

                with sp.Fori(0, PAIRS - 1, 1) as i:
                    pair(i, False)
                pair(PAIRS - 1, True)

            def spread_bias():
                sp.wait_ge(rpb_put, 16 * ROWS)
                for v, first in ((0, 31), (1, 23), (2, 15)):
                    for qc in range(QCOLS):
                        s = first - qc
                        src = rpb_rows[:, :, :, s:s + KCOLS].rearrange("q h r x -> q (h r) x")
                        dst = rpb_full[v, 8 * qc:8 * qc + 8].rearrange("q h (r x) -> q (h r) x", x=KCOLS)
                        sp.dma_start(dst, src).then_inc(rpb_spread, 16)

            for n in range(NM01):
                load(n % SLOTS, n // SLOTS, row_blocks(w_mod)[n // 2][:, (n % 2) * D:(n % 2 + 1) * D])
            ffn_loads(0, w_gu1, w_dn1, U_FFN1, B1, A1, D1)
            for t in range(NTT):
                if t >= 2:
                    sp.wait_ge(resid, t - 1)
                sp.dma_start(XST[:, t % 2, :], x_t[t] if t < NLT else ctx_t[t - NLT]).then_inc(xst_in[t % 2], 16)
                if t == 1:
                    mix_load(4)
                    mix_load(5)
            sp.wait_ge(gw_zeroed, 1)
            for g, w in ((0, lru_wa), (1, lru_wx)):
                src = w.rearrange("l d (c two) i j -> (l two) i (d c) j", two=2)
                for h in range(2):
                    dst = GW[DH * h:DH * h + DH, g].rearrange("p d c n -> p (d c) n")[:, :, DH * h:DH * h + DH]
                    sp.dma_start(dst, src[h]).then_inc(gw_in, 16)
            for t in range(6, 29):
                mix_load(t)
            s, u = mix_use(step_tile(11))
            sp.wait_ge(used[s], u + 1)
            sp.wait_ge(rpb_spread, 16 * 3 * QCOLS)
            sp.dma_start(BIAS0, rpb_full[0]).then_inc(bias_in, 16)
            sp.dma_start(BIAS3, rpb_full[2]).then_inc(bias_in, 16)
            for t in range(29, N_MIX - 2):
                mix_load(t)
            s, u = mix_use(step_tile(N_IN - 1))
            sp.wait_ge(used[s], u + 1)
            sp.dma_start(BIASM, rpb_full[1].rearrange("p (a h) n -> p a (h n)", h=2)).then_inc(bias_in, 16)
            for t in range(N_MIX - 2, N_MIX):
                mix_load(t)
            ffn_loads(1, w_gu2, w_dn2, U_FFN2, B2, A2, D2)
            for t in range(NLT):
                sp.wait_ge(resid, POST_N[2] + t + 1)
                sp.dma_start(out_t[t], YX[:, t, :]).then_inc(stored, 16)
            sp.wait_ge(stored, 16 * NLT)

        @block.scalar
        def _(act):
            def make_hi(s, u):
                act.wait_ge(landed[s], u * 16 + 16)
                if not (known(u) and u == 0):
                    act.wait_ge(used[s], u)
                nc.scalar.activation(WH[:, s, :], WR[:, s, :], ACT.Copy).then_inc(hi_made[s], 1)

            squares = []

            def square(src, junk, col, done):
                if squares:
                    act.wait_ge(squares[-1], squares.count(squares[-1]))
                squares.append(done)
                nc.scalar.activation(junk, src, ACT.Square, accum_out=SS[:, col:col + 1]).then_inc(done, 1)

            def h_full(n):
                for k in range(KC):
                    b = 2 * (k % 4)
                    if k == 0:
                        act.wait_ge(a_made, n + 1)
                    act.wait_ge(turned, n * KC + k + 1)
                    if k >= 2:
                        act.wait_ge(h_lo, n * KC + k - 1)
                    m = 24 * n + k
                    ins = nc.scalar.activation(h32(n, k)[:, 0:LAT], PS[:, b, 0:LAT], ACT.Identity,
                                               bias=MOD[:, m, 0:1], scale=APRE[:, k, 0:1])
                    if PRE_T[n] == NTT:
                        ins = nc.scalar.activation(h32(n, k)[:, LAT:TOK], PS[:, b + 1, 0:CTX], ACT.Identity,
                                                   bias=MOD[:, m, 1:2], scale=APRE[:, k, 1:2])
                    ins.then_inc(h_32, 1)

            def ffn(n, uses, B, A, Dn):
                ntok, nj, cb, yb = ffn_counts(n)
                nh = len(token_halves(ntok))

                def silu(r, cnt, bank):
                    g = (A, B)[r][0]
                    act.wait_ge(used[g], cnt + uses[g] - cb)
                    if not (known(cnt) and cnt == 1):
                        act.wait_ge(a_lo[r], cnt - 1)
                    nc.scalar.activation(SG[:, r, 0:ntok].rearrange("p (h w) -> p h w", h=nh),
                                         PS[:, bank:bank + nh, 0:ntok // nh], ACT.Silu).then_inc(silu_made[r], 1)

                def high(r, cnt):
                    act.wait_ge(au_made[r], cnt)
                    nc.scalar.activation(AH[:, r, 0:ntok], SG[:, r, 0:ntok], ACT.Copy).then_inc(a_hi[r], 1)

                def tiles(slots, use):
                    for s in slots:
                        make_hi(s, uses[s] + use)

                def pair(i, whole):
                    silu(1, i + cb + 2, 0)
                    if whole:
                        tiles(B, i + 2)
                    act.wait_ge(y_ready, i * nj + yb + nj)
                    high(1, i + cb + 2)
                    tiles(Dn, i + 1)
                    silu(0, i + cb + 2, 4)
                    if whole:
                        tiles(A, i + 2)
                    high(0, i + cb + 2)

                silu(1, cb + 1, 0)
                tiles(B, 1)
                tiles(Dn, 0)
                high(1, cb + 1)
                silu(0, cb + 1, 4)
                tiles(A, 1)
                high(0, cb + 1)
                with act.Fori(0, PAIRS if n == 0 else PAIRS - 1, 1) as i:
                    pair(i, True)
                if n == 1:
                    pair(PAIRS - 1, False)

            def grow_out(n, dsts):
                act.wait_ge(grow_ps, n + 1)
                for dst, bank in dsts:
                    ins = nc.scalar.activation(dst.rearrange("p (a n) -> p a n", a=2), PS[:, bank:bank + 2, :], ACT.Copy)
                ins.then_inc(grow_made, 1)

            def post_squares(n):
                for t in range(POST_T[n] + (n < 2)):
                    if t < POST_T[n]:
                        if n == 1:
                            act.wait_ge(wo_done, t + 1)
                            src = PS[:, 2 * t:2 * t + 2, :].rearrange("p a n -> p (a n)")
                        else:
                            act.wait_ge(ysum, t + 1 + (NTT if n == 2 else 0))
                            src = y_acc(n // 2, t)
                        square(src, JUNK5[:, :] if n == 1 else JUNK[:, :], POST_C[n] + t, sq_post)
                    if n < 2 and t >= 1:
                        act.wait_ge(resid, POST_N[n] + t)
                        square(YX[:, t - 1, :], JUNK5[:, :] if n == 1 else JUNK[:, :], PRE_C[n + 1] + t - 1, sq_pre)

            def load_rows(dst, r, n, src):
                act.dma_start(dst[r:r + n, :], src).then_inc(rows_in, 16)

            def rows128(a):
                return a.rearrange("l (r p) -> (l r) p", p=P) if len(a.shape) == 2 else \
                    a.rearrange("l m (r p) -> (l m r) p", p=P)

            load_rows(R1, R_C, KC, rows128(c))
            load_rows(R1, R_CC, KC, c_ctx.rearrange("(r p) -> r p", p=P))
            load_rows(R1, R_BMOD, 72, rows128(b_mod))
            load_rows(R1, R_PRE, 24, rows128(norm_pre))
            load_rows(R2, R_POST, 24, rows128(norm_post))
            load_rows(R2, R_CW, 16, rows128(conv_w))
            load_rows(R2, R_CB, RC, rows128(conv_b))
            load_rows(R2, R_BA, 8, rows128(lru_ba))
            load_rows(R2, R_BX, 8, rows128(lru_bx))
            load_rows(R2, R_LAM, 8, rows128(lru_lambda))
            for t in range(NTT):
                act.dma_start(YX[:, t, :], x_t[t] if t < NLT else ctx_t[t - NLT]).then_inc(x_in[t], 16)
            act.wait_ge(zero_set, 1)
            act.dma_start(rpb_rows.rearrange("q h r x -> (q h r x)").rearrange("(p n) -> p n", p=P),
                          ZERO[:, :]).then_inc(rpb_zeroed, 16)
            act.wait_ge(c1_made, 1)
            nc.scalar.activation(CS[:, :, :].rearrange("p a k -> p (a k)"), C1[:, R_C:R_C + 16],
                                 ACT.Silu).then_inc(cs_made, 1)
            act.wait_ge(cs_made, 1)
            nc.scalar.activation(C4[:, :, 0:4:2], CS[:, :, :].rearrange("p a k -> p k a"), ACT.Copy).then_inc(c4_hi, 1)
            act.wait_ge(lam_abs, 1)
            nc.scalar.activation(LT[:, 1, :], LT[:, 0, :], ACT.Exp, scale=-1.0).then_inc(lam_exp, 1)
            act.wait_ge(rpb_zeroed, 16)
            for qr in range(ROWS):
                act.dma_start(rpb_rows[qr, :, :, 16:16 + RPB_C],
                              rpb[0, :, ROWS - 1 - qr:2 * ROWS - 1 - qr, :]).then_inc(rpb_put, 16)
            for n in range(NM01):
                make_hi(n % SLOTS, n // SLOTS)
                if n % 2 == 1 and n // 2 < NTT:
                    t = n // 2
                    act.wait_ge(x_in[t], 16)
                    square(YX[:, t, :], JUNK[:, :], PRE_C[0] + t, sq_pre)
            for s in B1 + A1:
                make_hi(s, U_FFN1[s])
            h_full(0)
            ffn(0, U_FFN1, B1, A1, D1)
            grow_out(0, [(GROW[:, 0, :], 0), (GROW[:, 1, :], 2)])
            post_squares(0)
            for t in (4, 5):
                make_hi(*mix_use(t))
            h_full(1)

            def rec_unit(r):
                j = (r % 2) * RC + r // 2
                act.wait_ge(gates, r + 1)
                if r:
                    act.wait_ge(scanned, r)
                nc.scalar.activation(T[:, 0, :].rearrange("p (h w) -> p h w", h=2), PS[:, 4:6, 0:HSW],
                                     ACT.Sigmoid, bias=C2[:, R_BA + j:R_BA + j + 1]).then_inc(r_sig, 1)
                nc.scalar.activation(T[:, 1, :].rearrange("p (h w) -> p h w", h=2), PS[:, 6:8, 0:HSW],
                                     ACT.Sigmoid, bias=C2[:, R_BX + j:R_BX + j + 1]).then_inc(x_sig, 1)
                act.wait_ge(r_sig, r + 1)
                nc.scalar.activation(T[:, 2, :], T[:, 0, :], ACT.Exp, scale=LOGC[:, j:j + 1])
                nc.scalar.activation(T3[:, :], T[:, 0, :], ACT.Tanh, scale=LOGC[:, j:j + 1]).then_inc(r_at, 1)
                act.wait_ge(om_made, r + 1)
                nc.scalar.activation(T[:, 0, :], T[:, 0, :], ACT.Sqrt, scale=-1.0).then_inc(root, 1)

            t_hi = 6
            act.wait_ge(logc_made, 1)
            for n in range(N_IN):
                while t_hi <= step_tile(n) + 6 and t_hi < N_MIX - 2:
                    make_hi(*mix_use(t_hi))
                    t_hi += 1
                if n in REC_STEP:
                    rec_unit(REC_STEP[n])
                if n >= N_ALT:
                    if n == N_ALT:
                        act.wait_ge(scanned, 2 * RC)
                    s, u = mix_use(step_tile(n))
                    act.wait_ge(used[s], u + 1)
                    nc.scalar.activation(GR[:, n - N_ALT, :], PS[:, 2 * (n % 2), :], ACT.Gelu_apprx_tanh).then_inc(gelu_out, 1)
            for j in range(0, 10, 2):
                act.wait_ge(vt, j + 1)
                nc.scalar.activation(v_dst(j), PS[:, j % 4, :], ACT.Copy).then_inc(vt_act, 1)
            for j in range(RC):
                act.wait_ge(yr_f, j + 1)
                nc.scalar.activation(YRH[j], XR[:, j, 2:2 + LAT], ACT.Copy).then_inc(yr_hi, 1)
            act.wait_ge(yr_lo, RC)
            grow_out(1, [(GROW5[:, :], 4)])
            with act.Fori(0, HPAIRS, 1) as p:
                nc.scalar.activation(QS[:, :], Q[:, bass.ds(p, 1), :].rearrange("p a n -> p (a n)"), ACT.Copy,
                                     scale=DH ** -0.5).then_inc(qs_made, 1)

                def exponentials(u):
                    act.wait_ge(maxed, p * UNITS + u + 1)
                    if u >= 2:
                        act.wait_ge(pt_ps, p * UNITS + u - 1)
                    nc.scalar.activation(PR[:, u % 2, :], PS[:, u % 2, :], ACT.Exp, bias=NMX[:, u:u + 1],
                                         accum_out=DEN[:, u:u + 1]).then_inc(exps, 1)

                def transposed(u):
                    act.wait_ge(pt_ps, p * UNITS + u + 1)
                    if u >= 2:
                        act.wait_ge(pv, p * UNITS + u - 1)
                    nc.scalar.activation(PT[:, u % 2, :], PS[:, 2 + u % 2, :], ACT.Copy).then_inc(pt_made, 1)

                exponentials(0)
                for u in range(1, UNITS):
                    exponentials(u)
                    transposed(u - 1)
                transposed(UNITS - 1)
                act.wait_ge(ot, p + 1)
                nc.scalar.activation(YAH[:, bass.ds(p, 1), :].rearrange("p a (r c) -> p (a c) r", r=ROWS),
                                     PS[:, 6, :].rearrange("p (c r) -> p c r", r=ROWS), ACT.Copy).then_inc(ya_hi, 1)
            for t in (N_MIX - 2, N_MIX - 1):
                make_hi(*mix_use(t))
            post_squares(1)
            for s in B2 + A2:
                make_hi(s, U_FFN2[s])
            h_full(2)
            ffn(1, U_FFN2, B2, A2, D2)
            grow_out(2, [(GROW[:, 0, :], 0)])
            post_squares(2)

        @block.gpsimd
        def _(pool):
            own = [0]

            def after_own(ins):
                own[0] += 1
                ins.then_inc(pool_own, 1)
                pool.wait_ge(pool_own, own[0])

            def make_lo(s, u):
                pool.wait_ge(hi_made[s], u + 1)
                nc.gpsimd.tensor_tensor(WL[:, s, :], WR[:, s, :], WH[:, s, :].bitcast(F32),
                                        ALU.subtract).then_inc(lo_made[s], 1)

            def rstd(col, t, ready, cnt, done):
                pool.wait_ge(ready, cnt)
                after_own(nc.gpsimd.tensor_scalar(MS[:, t:t + 1], SS[:, col:col + 1], 1.0 / D, EPS, ALU.mult, ALU.add))
                nc.gpsimd.tensor_tensor(RS[:, col:col + 1], MS[:, t:t + 1], MHALF[:, :], ALU.pow).then_inc(done, 1)

            def h_low(n):
                w = TOK if PRE_T[n] == NTT else LAT
                for k in range(KC):
                    pool.wait_ge(h_hi, n * KC + k + 1)
                    nc.gpsimd.tensor_tensor(HL[:, k, 0:w], h32(n, k)[:, 0:w], HH[:, k, 0:w].bitcast(F32),
                                            ALU.subtract).then_inc(h_lo, 1)

            def ffn(n, uses, B, A, Dn):
                def tiles(slots, use):
                    for s in slots:
                        make_lo(s, uses[s] + use)

                tiles(B, 1)
                tiles(Dn, 0)
                tiles(A, 1)
                with pool.Fori(0, PAIRS if n == 0 else PAIRS - 1, 1) as i:
                    tiles(B, i + 2)
                    tiles(Dn, i + 1)
                    tiles(A, i + 2)
                if n == 1:
                    tiles(Dn, PAIRS)

            def post(n):
                for t in range(POST_T[n] + 1):
                    if t >= 1:
                        pool.wait_ge(scaled, POST_N[n] + t)
                        if n == 0:
                            pool.wait_ge(xst_in[(t - 1) % 2], 16 * ((t - 1) // 2 + 1))
                            y, r = y_acc(0, t - 1), XST[:, (t - 1) % 2, :]
                        elif n == 1:
                            y, r = YX[:, NLT + (t - 1) % 2, :], YX[:, t - 1, :]
                        else:
                            y, r = y_acc(1, t - 1), YX[:, t - 1, :]
                        nc.gpsimd.tensor_tensor(YX[:, t - 1, :], y, r, ALU.add).then_inc(resid, 1)
                    if t < POST_T[n]:
                        rstd(POST_C[n] + t, t, sq_post, POST_N[n] + t + 1, rstd_post)
                    if n < 2 and t >= 1:
                        rstd(PRE_C[n + 1] + t - 1, t - 1, sq_pre, PRE_N[n + 1] + t, rstd_pre)

            nc.gpsimd.memset(ZERO[:, :], 0.0).then_inc(zero_set, 1)
            after_own(nc.gpsimd.memset(IDENT[:, :], 0.0))
            nc.gpsimd.affine_select(out=IDENT[:, :], in_=IDENT[:, :], compare_op=ALU.not_equal, fill=1.0, base=0,
                                    pattern=[[-1, P]], channel_multiplier=1).then_inc(ident_set, 1)
            nc.gpsimd.memset(MHALF[:, :], -0.5).then_inc(mhalf_set, 1)
            nc.gpsimd.memset(ONES[:, :], 1.0).then_inc(ones_set, 1)
            pool.wait_ge(mhalf_set, 1)
            for n in range(NM01):
                make_lo(n % SLOTS, n // SLOTS)
                if n % 2 == 1 and n // 2 < NTT:
                    rstd(PRE_C[0] + n // 2, n // 2, sq_pre, n // 2 + 1, rstd_pre)
            for s in B1 + A1:
                make_lo(s, U_FFN1[s])
            h_low(0)
            pool.wait_ge(turned, KC)
            nc.gpsimd.memset(YX[:, :, :], 0.0).then_inc(y_zeroed, 1)
            ffn(0, U_FFN1, B1, A1, D1)
            post(0)
            for t in (4, 5):
                make_lo(*mix_use(t))
            pool.wait_ge(xn_made, 2 * NTT)
            nc.gpsimd.memset(GW[:, :, :, :, :], 0.0).then_inc(gw_zeroed, 1)
            h_low(1)
            pool.wait_ge(h_lo, 2 * KC)
            for j in range(RC):
                for a, b in ((0, 2), (2 + LAT, 2 + CTX0), (2 + CTX0 + CTX, PADW)):
                    ins = nc.gpsimd.memset(XR[:, j, a:b], 0.0)
            ins.then_inc(pads_zeroed, 1)
            for t in range(6, 35):
                make_lo(*mix_use(t))
            pool.wait_ge(scanned, 2 * RC)
            nc.gpsimd.memset(ONES5[:, :], 1.0).then_inc(ones_set, 1)
            after_own(nc.gpsimd.memset(MASK[:, :, :], 0.0))

            def window(v, x0, n, base_, step, cm):
                part = MASK[:, v, x0:x0 + n]
                after_own(nc.gpsimd.affine_select(out=part, in_=part, compare_op=ALU.is_ge, fill=NEG, base=base_,
                                                  pattern=[[step, n]], channel_multiplier=cm))

            window(0, 0, 16, 64 + 7, 8, -1)
            window(0, 16, 16, 56 - 128, -8, 1)
            window(1, 0, 32, 7, 8, -1)
            window(1, 0, 32, 120, -8, 1)
            window(2, 0, 16, 7 - 64, 8, -1)
            window(2, 16, 16, 184 - 128, -8, 1)
            for t in range(35, T_OUT + 2):
                make_lo(*mix_use(t))
            pool.wait_ge(bias_in, 48)
            for v, b in ((0, BIAS0), (2, BIAS3), (1, BIASM)):
                view = b.rearrange("p a (r x) -> p a r x", x=KCOLS)
                n1, n2 = view.shape[1], view.shape[2]
                m = MASK[:, v, :].unsqueeze(1).unsqueeze(1).broadcast_to([P, n1, n2, KCOLS])
                nc.gpsimd.tensor_tensor(view, view, m, ALU.add).then_inc(bias_made, 1)
            for t in range(T_OUT + 2, T_OUT + 6):
                make_lo(*mix_use(t))
            for t in (N_MIX - 2, N_MIX - 1):
                make_lo(*mix_use(t))
            post(1)
            for s in B2 + A2:
                make_lo(s, U_FFN2[s])
            h_low(2)
            pool.wait_ge(turned, 3 * KC)
            nc.gpsimd.memset(Y2[:, :, :], 0.0).then_inc(y_zeroed, 1)
            nc.gpsimd.memset(ONES[:, :], 1.0).then_inc(ones_set, 1)
            ffn(1, U_FFN2, B2, A2, D2)
            post(2)

        @block.tensor
        def _(pe):
            def turn(n):
                for k in range(KC):
                    b = 2 * (k % 4)
                    if k == 0:
                        pe.wait_ge(xn_made, PRE_N[n] + PRE_T[n])
                    if k >= 4:
                        pe.wait_ge(h_32, n * KC + k - 3)
                    for t in range(PRE_T[n]):
                        bank, col = (b, t) if t < NLT else (b + 1, t - NLT)
                        ins = nc.tensor.transpose(PS[:, bank, col * P:col * P + P],
                                                  xn_tile(n, t)[:, k * P:k * P + P], IDENT[:, :])
                    ins.then_inc(turned, 1)

            def project(s, halves, banks, wait_k=None):
                ins = None
                for k in range(KC):
                    if wait_k is not None:
                        pe.wait_ge(h_lo, wait_k + k + 1)
                    wh, wl = WH[:, s, k * P:k * P + P], WL[:, s, k * P:k * P + P]
                    for w, h, first, last in ((wh, HH, True, False), (wh, HL, False, False), (wl, HH, False, True)):
                        for (j, sl, n), bank in zip(halves, banks):
                            ins = nc.tensor.matmul(PS[:, bank, 0:n], w, h[:, k, sl], start=(k == 0 and first),
                                                   stop=(k == KC - 1 and last))
                return ins

            def three(out_ps, lh, ll, rh, rl, first, last):
                nc.tensor.matmul(out_ps, lh, rh, start=first, stop=False)
                nc.tensor.matmul(out_ps, lh, rl, start=False, stop=False)
                return nc.tensor.matmul(out_ps, ll, rh, start=False, stop=last)

            def ffn(n, uses, B, A, Dn):
                ntok, nj, cb, yb = ffn_counts(n)
                ab = added_before(n)
                halves = token_halves(ntok)

                def up(r, use, bank, wait_k=None):
                    slots = (A, B)[r]
                    for g, s in enumerate(slots):
                        pe.wait_ge(lo_made[s], uses[s] + use + 1)
                        if g == 1 and r == 0 and not known(use):
                            pe.wait_ge(y_added, (use - 1) * nj + ab + nj)
                        bk = bank + 2 * g
                        project(s, halves, [bk, bk + 1], wait_k if g == 0 else None).then_inc(used[s], 1)
                        if g == 0 and r == 0 and not known(use):
                            release_down((use - 1) * nj + yb + nj)

                def release_down(y_count):
                    pe.wait_ge(y_ready, y_count)
                    pe.nop().then_inc(used[Dn[1]], 1)

                def down_unit(j, use, bank):
                    t, half = j // 2, j % 2
                    tk = slice(t * P, t * P + P)
                    col = slice(half * HALF_D, half * HALF_D + HALF_D)
                    for q, r in ((0, 1), (1, 0)):
                        s = Dn[q]
                        ins = three(PS[:, bank, :], AH[:, r, tk], AL[:, r, tk], WH[:, s, col], WL[:, s, col],
                                    q == 0, q == 1)
                        if j == nj - 1:
                            if q == 0:
                                ins.then_inc(used[s], 1)
                    return ins

                pe.wait_ge(h_32, n * 2 * KC + KC)
                up(1, 0, 0, wait_k=2 * n * KC)
                up(0, 0, 4)
                if n == 0:
                    pe.wait_ge(ones_set, 1)
                with pe.Fori(0, PAIRS, 1) as i:
                    pe.wait_ge(au_made[1], i + cb + 1)
                    up(1, i + 1, 0)
                    for q in range(2):
                        pe.wait_ge(lo_made[Dn[q]], i + uses[Dn[q]] + 1)
                    for r in range(2):
                        pe.wait_ge(a_lo[r], i + cb + 1)
                    if n == 0:
                        pe.wait_ge(mod_own, i * 16 + 16)
                        for m in range(4):
                            for r in range(2):
                                ins = nc.tensor.matmul(PS[:, 7, 2 * m + r:2 * m + r + 1],
                                                       MACC[:, r, m * P:m * P + P], ONES[:, 0:1], start=True, stop=True)
                        ins.then_inc(mod_red, 1)
                    for j in range(nj):
                        if n == 0 and j == 3:
                            pe.wait_ge(mod_made, i + 1)
                        if j >= 4:
                            pe.wait_ge(y_added, i * nj + ab + j - 3)
                        down_unit(j, i, 4 + j % 4).then_inc(y_ready, 1)
                    pe.wait_ge(y_added, i * nj + ab + nj - 2)
                    up(0, i + 1, 4)
                for q in range(2):
                    pe.wait_ge(lo_made[Dn[q]], uses[Dn[q]] + PAIRS + 1)
                for r in range(2):
                    pe.wait_ge(a_lo[r], cb + PAIRS + 1)
                for j in range(nj):
                    if j >= 4 and j % 2 == 0:
                        pe.wait_ge(ysum, n * NTT + j // 2 - 1)
                    down_unit(j, PAIRS, 4 + j % 4).then_inc(y_ready, 1)
                    if j == 1:
                        grow(2 * n, 2 if n == 0 else 1, 0, ONES, DIAG if n == 0 else DIAG2, (1, 3)[n])
                release_down(yb + nj * (PAIRS + 1))

            def grow(n, streams, bank, ones, diag, ones_count):
                pe.wait_ge(ones_set, ones_count)
                pe.wait_ge(diag_made, n + 1)
                for g in range(streams):
                    for k in range(KC):
                        b = bank + 2 * g + k // 4
                        ins = nc.tensor.matmul(PS[:, b, (k % 4) * P:(k % 4) * P + P], ones[:, :],
                                               diag[:, g, k, :], start=True, stop=True)
                ins.then_inc(grow_ps, 1)

            def mod_tile(s, bank, col, first, last, alone):
                k = mod_k[0]
                for m in range(KC):
                    for q, w in enumerate((WH, WL)):
                        o = PS[:, bank, col + 4 * m:col + 4 * m + 4]
                        ins = nc.tensor.matmul(o, w[:, s, m * P:m * P + P], C4[:, k, :],
                                               start=(q == 0 if alone else first and m == 0 and q == 0),
                                               stop=(q == 1 if alone else last and q == 1), skip_group_check=not alone)
                return ins

            mod_k = [0]
            pe.wait_ge(ident_set, 1)
            pe.wait_ge(rows_in, 160)
            nc.tensor.transpose(PS[:, 4, 0:N_R1], R1[0:N_R1, :], IDENT[0:N_R1, 0:N_R1])
            nc.tensor.transpose(PS[:, 5, 0:N_R2], R2[0:N_R2, :], IDENT[0:N_R2, 0:N_R2]).then_inc(rows_turned, 1)
            pe.wait_ge(c4_made, 1)
            for n in range(NM01):
                s = n % SLOTS
                pe.wait_ge(lo_made[s], n // SLOTS + 1)
                mod_k[0] = n // 2
                ins = mod_tile(s, 6, 32 * (n % 2), n == 0, n // 2 == KC - 1, False)
                ins.then_inc(used[s], 1)
            pe.wait_ge(c2_made, 1)
            pe.wait_ge(mod01_made, 1)
            turn(0)
            ffn(0, U_FFN1, B1, A1, D1)
            pe.wait_ge(grow_made, 1)
            pe.wait_ge(ysum, NTT)
            turn(1)
            pe.wait_ge(h_32, 2 * KC)
            lat = (0, slice(0, LAT), LAT)
            both = [lat, (1, slice(LAT, TOK), CTX)]
            for n in range(N_IN):
                s, u = mix_use(step_tile(n))
                pe.wait_ge(lo_made[s], u + 1)
                if 2 <= n < N_ALT + 2:
                    pe.wait_ge(proj_out, n - 1)
                elif n >= N_ALT + 2:
                    pe.wait_ge(gelu_out, n - N_ALT - 1)
                b = 2 * (n % 2)
                ins = project(s, both if n < 12 else [lat], [b, b + 1], wait_k=KC if n == 0 else None)
                ins.then_inc(used[s], 1)
                if n < N_ALT:
                    s, u = mix_use(step_tile(n) + 1)
                    pe.wait_ge(lo_made[s], u + 1)
                    done = [REC_STEP[q] for q in REC_STEP if q < n]
                    if done:
                        pe.wait_ge(x_sig, max(done) + 1)
                    if n:
                        pe.wait_ge(mod78_made, n)
                    mod_k[0] = n // 2
                    mod_tile(s, 7, 0, True, True, True).then_inc(used[s], 1)
                if n in REC_STEP:
                    r = REC_STEP[n]
                    cc, d = r // 2, r % 2
                    pe.wait_ge(xc_made, cc + 1)
                    if r == 0:
                        pe.wait_ge(gw_in, 64)
                    else:
                        pe.wait_ge(x_sig, r)
                    for g in range(2):
                        for h in range(2):
                            if g == 1 and h == 1:
                                pe.wait_ge(mod78_made, n + 1)
                            ins = nc.tensor.matmul(PS[:, 4 + 2 * g + h, 0:HSW], GW[:, g, d, cc, :],
                                                   XC[:, HSW * h:HSW * h + HSW], start=True, stop=True)
                    ins.then_inc(gates, 1)
            pe.wait_ge(gelu_out, N_IN - N_ALT)
            pe.wait_ge(mod78_made, N_ALT)
            for j in range(10):
                if j >= 4:
                    pe.wait_ge((vt_act, vt_dve)[j % 2], (j - 4) // 2 + 1)
                for t in range(HPAIRS):
                    if j < 8:
                        k0 = ROWS * KSTART[j // 2] + P * (j % 2)
                        src = V[:, t, k0:k0 + P]
                    else:
                        src = V[:, t, LAT + (j - 8) * P:LAT + (j - 7) * P]
                    ins = nc.tensor.transpose(PS[:, j % 4, t * P:t * P + P], src, IDENT[:, :])
                ins.then_inc(vt, 1)
            pe.wait_ge(r_sig, 2 * RC)
            grow(1, 1, 4, ONES5, DIAG5, 2)
            pe.wait_ge(x_sig, 2 * RC)
            pe.wait_ge(vt_act, 5)
            pe.wait_ge(vt_dve, 5)
            pe.wait_ge(bias_made, 3)
            pe.wait_ge(grow_made, 2)
            with pe.Fori(0, HPAIRS, 1) as p:
                def score(u):
                    b, h = u // 2, u % 2
                    ph = slice(DH * h, DH * h + DH)
                    if u >= 2:
                        pe.wait_ge(exps, p * UNITS + u - 1)
                    q = QS[ph, b * P:b * P + P]
                    kl = KS[ph, ROWS * KSTART[b]:ROWS * KSTART[b] + LOCK]
                    nc.tensor.matmul(PS[:, u % 2, 0:LOCK], q, kl, start=True, stop=True)
                    nc.tensor.matmul(PS[:, u % 2, LOCK:LOCK + CTX], q, KS[ph, LAT:TOK], start=True,
                                     stop=True).then_inc(scores, 1)

                def weighted_sum(u):
                    b, h = u // 2, u % 2
                    pe.wait_ge(pt_made, p * UNITS + u + 1)
                    if u >= 2:
                        pe.wait_ge(on_made, p * UNITS + u - 1)
                    for j in range(4):
                        v = (VB[:, 2 * b + j, :] if j < 2 else VC[:, j - 2, :])[:, bass.ds(p * P + DH * h, DH)]
                        ins = nc.tensor.matmul(PS[:, 4 + h, DH * b:DH * b + DH],
                                               PT[:, u % 2, j * P:j * P + P], v, start=(j == 0), stop=(j == 3))
                    ins.then_inc(pv, 1)

                pe.wait_ge(qs_made, p + 1)
                pe.wait_ge(ks_made, p + 1)
                score(0)
                score(1)
                for u in range(UNITS):
                    pe.wait_ge(exps, p * UNITS + u + 1)
                    for j in range(4):
                        ins = nc.tensor.transpose(PS[:, 2 + u % 2, j * P:j * P + P], PR[:, u % 2, j * P:j * P + P],
                                                  IDENT[:, :])
                    ins.then_inc(pt_ps, 1)
                    if u + 2 < UNITS:
                        score(u + 2)
                    if u:
                        weighted_sum(u - 1)
                weighted_sum(UNITS - 1)
                for b in range(NBLK):
                    pe.wait_ge(on_made, p * UNITS + 2 * b + 2)
                    ins = nc.tensor.transpose(PS[:, 6, b * P:b * P + P], ON[:, b, :], IDENT[:, :])
                ins.then_inc(ot, 1)
            pe.wait_ge(yr_lo, RC)
            for k in range(4):
                s, u = mix_use(T_OUT + k)
                pe.wait_ge(lo_made[s], u + 1)
                for j in (7, 5, 0, 1, 2, 3, 4, 6):
                    t, half = j // 2, j % 2
                    if k == 0 and j == 4:
                        pe.wait_ge(on_made, HPAIRS * UNITS)
                    if k == 0 and j == 6:
                        pe.wait_ge(ya_lo, HPAIRS)
                    tk = slice(t * P, t * P + P)
                    col = slice(half * HALF_D, half * HALF_D + HALF_D)
                    ins = three(PS[:, j, :], YRH[k][:, tk], YRL[k][:, tk], WH[:, s, col], WL[:, s, col], k == 0, False)
                ins.then_inc(used[s], 1)
            for t in range(NLT):
                tk = slice(t * P, t * P + P)
                for half in range(2):
                    col = slice(half * HALF_D, half * HALF_D + HALF_D)
                    for k in range(4):
                        s, u = mix_use(T_OUT + 4 + k)
                        if t == 0 and half == 0:
                            pe.wait_ge(lo_made[s], u + 1)
                        ins = three(PS[:, 2 * t + half, :], YAH[:, k, tk], YAL[:, k, tk], WH[:, s, col], WL[:, s, col],
                                    False, k == 3)
                ins.then_inc(wo_done, 1)
            pe.wait_ge(wo_done, NLT)
            for k in range(4):
                pe.nop().then_inc(used[mix_use(T_OUT + 4 + k)[0]], 1)
            turn(2)
            ffn(1, U_FFN2, B2, A2, D2)

        @block.vector
        def _(dve):
            own = [0]

            def after_own(ins):
                own[0] += 1
                ins.then_inc(dve_own, 1)
                dve.wait_ge(dve_own, own[0])

            def a_columns(n):
                g = C1[:, R_PRE + KC * n:R_PRE + KC * n + KC].unsqueeze(2).broadcast_to([P, KC, 2])
                nc.vector.scalar_tensor_tensor(out=APRE[:, :, :], in0=MOD[:, 24 * n + 8:24 * n + 16, :], scalar=1.0,
                                               in1=g, op0=ALU.add, op1=ALU.mult).then_inc(a_made, 1)

            def diagonal(n, streams, diag, res_w):
                g = C2[:, R_POST + KC * n:R_POST + KC * n + KC].unsqueeze(2).broadcast_to([P, KC, 2])
                after_own(nc.vector.scalar_tensor_tensor(out=GCOL[:, :, :], in0=MOD[:, 24 * n + 16:24 * n + 24, :],
                                                         scalar=res_w, in1=g, op0=ALU.mult, op1=ALU.mult))
                for r in range(streams):
                    for k in range(KC):
                        ins = nc.vector.tensor_scalar(diag[:, r, k, :], IDENT[:, :], GCOL[:, k, r:r + 1], None, ALU.mult)
                ins.then_inc(diag_made, 1)

            def h_high(n):
                w = TOK if PRE_T[n] == NTT else LAT
                for k in range(KC):
                    dve.wait_ge(h_32, n * KC + k + 1)
                    nc.vector.tensor_copy(HH[:, k, 0:w], h32(n, k)[:, 0:w]).then_inc(h_hi, 1)

            def ffn(n, uses, B, A):
                ntok, nj, cb, yb = ffn_counts(n)
                nh = len(token_halves(ntok))

                def times_u(r, cnt, bank):
                    dve.wait_ge(silu_made[r], cnt)
                    g = (A, B)[r][1]
                    dve.wait_ge(used[g], cnt + uses[g] - cb)
                    s = SG[:, r, 0:ntok].rearrange("p (h w) -> p h w", h=nh)
                    nc.vector.tensor_tensor(s, s, PS[:, bank:bank + nh, 0:ntok // nh], ALU.mult).then_inc(au_made[r], 1)
                    dve.wait_ge(a_hi[r], cnt)
                    nc.vector.tensor_tensor(AL[:, r, 0:ntok], SG[:, r, 0:ntok], AH[:, r, 0:ntok].bitcast(F32),
                                            ALU.subtract).then_inc(a_lo[r], 1)

                times_u(1, cb + 1, 2)
                times_u(0, cb + 1, 6)
                dve.wait_ge(y_zeroed, n + 1)
                with dve.Fori(0, PAIRS, 1) as i:
                    if n == 0:
                        for k in range(KC):
                            if k % 2 == 0:
                                dve.wait_ge(mod_in[(k // 2) % 2], i * 32 + 16 * (k // 4) + 16)
                            for r in range(2):
                                src = MRAW[:, (k // 2) % 2, k % 2, :]
                                if k == 0:
                                    ins = nc.vector.tensor_scalar(MACC[:, r, :], src, CS[:, r, 0:1], None, ALU.mult)
                                else:
                                    dve.wait_ge(mod_own, i * 16 + 2 * k + r - 1)
                                    ins = nc.vector.scalar_tensor_tensor(
                                        out=MACC[:, r, :], in0=src, scalar=CS[:, r, k:k + 1], in1=MACC[:, r, :],
                                        op0=ALU.mult, op1=ALU.add)
                                ins.then_inc(mod_own, 1)
                        dve.wait_ge(mod_red, i + 1)
                        m = bass.ds(i * 4 + 16, 4)
                        bm = C1[:, m].unsqueeze(2).broadcast_to([P, 4, 2])
                        nc.vector.tensor_tensor(MOD[:, m, :], PS[:, 7, 0:8].rearrange("p (m r) -> p m r", r=2), bm,
                                                ALU.add).then_inc(mod_made, 1)
                    for j in range(nj):
                        dve.wait_ge(y_ready, i * nj + yb + j + 1)
                        y = y_acc(n, j // 2)[:, HALF_D * (j % 2):HALF_D * (j % 2) + HALF_D]
                        nc.vector.tensor_tensor(y, y, PS[:, 4 + j % 4, :], ALU.add).then_inc(y_added, 1)
                    times_u(1, i + cb + 2, 2)
                    times_u(0, i + cb + 2, 6)

            def post(n):
                tiles = POST_T[n]
                yb = {0: PAIRS * 2 * NTT, 2: (PAIRS + 1) * 2 * NTT + PAIRS * 2 * NLT}.get(n)
                for t in range(tiles + (2 if n < 2 else 1)):
                    if n != 1 and t < tiles:
                        dve.wait_ge(y_ready, yb + 2 * t + 2)
                        b = 4 + 2 * (t % 2)
                        y = y_acc(n // 2, t).rearrange("p (a n) -> p a n", a=2)
                        nc.vector.tensor_tensor(y, y, PS[:, b:b + 2, :], ALU.add).then_inc(ysum, 1)
                    if 1 <= t <= tiles:
                        q = t - 1
                        dve.wait_ge(rstd_post, POST_N[n] + t)
                        if t == 1:
                            dve.wait_ge(grow_made, n + 1)
                        c0 = POST_C[n] + q
                        if n == 1:
                            if t >= 3:
                                dve.wait_ge(resid, POST_N[n] + t - 2)
                            dst = YX[:, NLT + q % 2, :]
                            src = PS[:, 2 * q:2 * q + 2, :].rearrange("p a n -> p (a n)")
                            g = GROW5[:, :]
                        else:
                            src = dst = y_acc(n // 2, q)
                            g = GROW[:, 0 if q < NLT else 1, :]
                        nc.vector.scalar_tensor_tensor(out=dst, in0=src, scalar=RS[:, c0:c0 + 1], in1=g, op0=ALU.mult,
                                                       op1=ALU.mult).then_inc(scaled, 1)
                    if n < 2 and t >= 2:
                        q = t - 2
                        dve.wait_ge(rstd_pre, PRE_N[n + 1] + q + 1)
                        c0 = PRE_C[n + 1] + q
                        nc.vector.tensor_scalar(xn_tile(n + 1, q), YX[:, q, :], RS[:, c0:c0 + 1], None,
                                                ALU.mult).then_inc(xn_made, 1)

            dve.wait_ge(rows_turned, 1)
            nc.vector.tensor_copy(C1[:, :], PS[:, 4, 0:N_R1]).then_inc(c1_made, 1)
            nc.vector.tensor_copy(C2[:, :], PS[:, 5, 0:N_R2]).then_inc(c2_made, 1)
            dve.wait_ge(c2_made, 1)
            lam = C2[:, R_LAM:R_LAM + 8]
            neg, e, s1, s2, acc, mn = LT[:, 0, :], LT[:, 1, :], LT[:, 2, :], LT[:, 3, :], LT[:, 4, :], LT[:, 5, :]
            after_own(nc.vector.tensor_scalar(neg, lam, -1.0, None, ALU.mult))
            nc.vector.tensor_tensor(neg, neg, lam, ALU.max).then_inc(lam_abs, 1)
            dve.wait_ge(c4_hi, 1)
            nc.vector.tensor_tensor(C4[:, :, 1:4:2], CS[:, :, :].rearrange("p a k -> p k a"),
                                    C4[:, :, 0:4:2].bitcast(F32), ALU.subtract).then_inc(c4_made, 1)
            dve.wait_ge(lam_exp, 1)
            after_own(nc.vector.tensor_scalar(s2, e, 2.0, None, ALU.add))
            after_own(nc.vector.reciprocal(s1, s2))
            after_own(nc.vector.tensor_tensor(s1, s1, e, ALU.mult))
            after_own(nc.vector.tensor_tensor(s2, s1, s1, ALU.mult))
            after_own(nc.vector.tensor_scalar(acc, s2, 1.0 / 19, None, ALU.mult))
            for d in (17, 15, 13, 11, 9, 7, 5, 3):
                after_own(nc.vector.scalar_tensor_tensor(out=acc, in0=acc, scalar=1.0 / d, in1=s2, op0=ALU.add, op1=ALU.mult))
            after_own(nc.vector.scalar_tensor_tensor(out=acc, in0=acc, scalar=1.0, in1=s1, op0=ALU.add, op1=ALU.mult))
            after_own(nc.vector.tensor_scalar(mn, lam, 0.0, LRU_C, ALU.min, ALU.mult))
            nc.vector.scalar_tensor_tensor(out=LOGC[:, :], in0=acc, scalar=-2.0 * LRU_C, in1=mn, op0=ALU.mult,
                                           op1=ALU.add).then_inc(logc_made, 1)
            for t in range(NTT):
                dve.wait_ge(rstd_pre, t + 1)
                nc.vector.tensor_scalar(YX[:, t, :], YX[:, t, :], RS[:, PRE_C[0] + t:PRE_C[0] + t + 1], None,
                                        ALU.mult).then_inc(xn_made, 1)
            dve.wait_ge(used[(NM01 - 1) % SLOTS], NM01 // SLOTS + 1)
            m01 = MOD[:, 0:2 * KC, :]
            after_own(nc.vector.tensor_reduce(m01, PS[:, 6, 0:8 * KC].rearrange("p (m a h) -> p m a h", a=2, h=2), AX_X, ALU.add))
            nc.vector.tensor_tensor(m01, m01, C1[:, 0:2 * KC].unsqueeze(2).broadcast_to([P, 2 * KC, 2]),
                                    ALU.add).then_inc(mod01_made, 1)
            dve.wait_ge(mod01_made, 1)
            a_columns(0)
            h_high(0)
            ffn(0, U_FFN1, B1, A1)
            dve.wait_ge(mod_made, PAIRS)
            diagonal(0, 2, DIAG, 0.5)
            dve.wait_ge(h_32, KC)
            a_columns(1)
            post(0)
            h_high(1)

            M8 = MOD[:, 56:72, :]

            def project_out(n):
                s, u = mix_use(step_tile(n))
                dve.wait_ge(used[s], u + 1)
                g, t, b = n // 4, n % 4, 2 * (n % 2)
                if n == 0:
                    dve.wait_ge(pads_zeroed, 1)
                if g == 0:
                    nc.vector.tensor_copy(XR[:, t, 2:2 + LAT], PS[:, b, :])
                    ins = nc.vector.tensor_copy(XR[:, t, 2 + CTX0:2 + CTX0 + CTX], PS[:, b + 1, 0:CTX])
                else:
                    dst = (K, V, Q)[g - 1]
                    ins = nc.vector.tensor_copy(dst[:, t, 0:LAT].rearrange("p (c r) -> p r c", r=ROWS),
                                                PS[:, b, :].rearrange("p (r c) -> p r c", r=ROWS))
                    if g < 3:
                        ins = nc.vector.tensor_copy(dst[:, t, LAT:TOK], PS[:, b + 1, 0:CTX])
                ins.then_inc(proj_out, 1)

            def mod78_add(n):
                s, u = mix_use(step_tile(n) + 1)
                dve.wait_ge(used[s], u + 1)
                m = M8[:, (n % 2) * KC:(n % 2) * KC + KC, :]
                p4 = PS[:, 7, 0:32].rearrange("p (m a h) -> p m a h", a=2, h=2)
                if n < 2:
                    bm = C1[:, R_BMOD + 56 + (n % 2) * KC:R_BMOD + 56 + (n % 2) * KC + KC].unsqueeze(2)
                    after_own(nc.vector.tensor_tensor(m, p4[:, :, :, 0], bm.broadcast_to([P, KC, 2]), ALU.add))
                else:
                    after_own(nc.vector.tensor_tensor(m, p4[:, :, :, 0], m, ALU.add))
                nc.vector.tensor_tensor(m, p4[:, :, :, 1], m, ALU.add).then_inc(mod78_made, 1)
                dve.wait_ge(mod78_made, n + 1)

            def conv(cc):
                w = [C2[:, R_CW + 4 * j + cc:R_CW + 4 * j + cc + 1] for j in range(4)]
                if cc:
                    dve.wait_ge(gates, 2 * cc)
                dve.wait_ge(proj_out, cc + 1)
                after_own(nc.vector.tensor_scalar(XC[:, :], XR[:, cc, 0:SCANW], w[0], C2[:, R_CB + cc:R_CB + cc + 1],
                                                  ALU.mult, ALU.add))
                for j in range(1, 4):
                    ins = nc.vector.scalar_tensor_tensor(out=XC[:, :], in0=XR[:, cc, j:j + SCANW], scalar=w[j],
                                                         in1=XC[:, :], op0=ALU.mult, op1=ALU.add)
                    if j < 3:
                        after_own(ins)
                ins.then_inc(xc_made, 1)

            def rec_unit(r):
                cc, d = r // 2, r % 2
                y = XR[:, cc, 2:2 + LAT]
                r1, a, u, hs = T[:, 1, :], T[:, 2, :], T[:, 0, :], T[:, 1, :]
                dve.wait_ge(xc_made, cc + 1)
                dve.wait_ge(x_sig, r + 1)
                after_own(nc.vector.tensor_tensor(r1, r1, XC[:, :], ALU.mult))
                dve.wait_ge(r_at, r + 1)
                after_own(nc.vector.tensor_tensor(u, a, a, ALU.mult))
                nc.vector.scalar_tensor_tensor(out=u, in0=u, scalar=1.0, in1=T3[:, :], op0=ALU.add,
                                               op1=ALU.mult).then_inc(om_made, 1)
                dve.wait_ge(root, r + 1)
                after_own(nc.vector.tensor_tensor(u, u, r1, ALU.mult))

                def part(t, lo, n):
                    v = t[:, lo:lo + n]
                    return v if d == 0 else v[:, ::-1]

                last = CTX0 + (CTX - 1 if d == 0 else 0)
                after_own(nc.vector.tensor_tensor_scan(part(hs, CTX0, CTX), part(a, CTX0, CTX), part(u, CTX0, CTX), 0.0,
                                                       ALU.mult, ALU.add))
                if d == 0:
                    nc.vector.tensor_tensor_scan(y, a[:, 0:LAT], u[:, 0:LAT], hs[:, last:last + 1],
                                                 ALU.mult, ALU.add).then_inc(scanned, 1)
                else:
                    after_own(nc.vector.tensor_tensor_scan(part(hs, 0, LAT), part(a, 0, LAT), part(u, 0, LAT),
                                                           hs[:, last:last + 1], ALU.mult, ALU.add))
                    dve.wait_ge(scanned, r)
                    nc.vector.tensor_tensor(y, y, hs[:, 0:LAT], ALU.add).then_inc(scanned, 1)

            for n in range(N_ALT):
                project_out(n)
                mod78_add(n)
                if n == 0:
                    conv(0)
                if n in REC_STEP:
                    r = REC_STEP[n]
                    rec_unit(r)
                    if r % 2 == 1 and r < 7:
                        conv(r // 2 + 1)
            diagonal(1, 1, DIAG5, 1.0)
            dve.wait_ge(h_32, 2 * KC)
            a_columns(2)
            for j in range(1, 10, 2):
                dve.wait_ge(vt, j + 1)
                nc.vector.tensor_copy(v_dst(j), PS[:, j % 4, :]).then_inc(vt_dve, 1)
            dve.wait_ge(scanned, 2 * RC)
            for j in range(RC):
                dve.wait_ge(gelu_out, j + 1)
                nc.vector.tensor_tensor(XR[:, j, 2:2 + LAT], XR[:, j, 2:2 + LAT], GR[:, j, :], ALU.mult).then_inc(yr_f, 1)
            for j in range(RC):
                dve.wait_ge(yr_hi, j + 1)
                nc.vector.tensor_tensor(YRL[j], XR[:, j, 2:2 + LAT], YRH[j].bitcast(F32), ALU.subtract).then_inc(yr_lo, 1)
            dve.wait_ge(bias_made, 3)
            with dve.Fori(0, HPAIRS, 1) as p:
                nc.vector.tensor_copy(KS[:, :], K[:, bass.ds(p, 1), :].rearrange("p a n -> p (a n)")).then_inc(ks_made, 1)

                def row_max(u):
                    b, h = u // 2, u % 2
                    dve.wait_ge(scores, p * UNITS + u + 1)
                    if b in (0, 3):
                        bias = (BIAS0 if b == 0 else BIAS3)[:, bass.ds(p * 2 + h, 1), :].rearrange("p a n -> p (a n)")
                    else:
                        bias = BIASM[:, bass.ds(p, 1), :].rearrange("p a n -> p (a n)")[:, LOCK * h:LOCK * h + LOCK]
                    s = PS[:, u % 2, 0:LOCK].rearrange("p (x r) -> p x r", r=ROWS)
                    nc.vector.tensor_tensor(s, s, bias.rearrange("p (r x) -> p x r", r=ROWS), ALU.add).then_inc(biased, 1)
                    dve.wait_ge(biased, p * UNITS + u + 1)
                    nc.vector.tensor_reduce(NMX[:, u:u + 1], PS[:, u % 2, :], AX_X, ALU.max, negate=True).then_inc(maxed, 1)

                def normed(u):
                    b, h = u // 2, u % 2
                    dve.wait_ge(pv, p * UNITS + u + 1)
                    nc.vector.reciprocal(RDEN[:, u:u + 1], DEN[:, u:u + 1]).then_inc(inverted, 1)
                    dve.wait_ge(inverted, p * UNITS + u + 1)
                    nc.vector.tensor_scalar(ON[:, b, DH * h:DH * h + DH], PS[:, 4 + h, DH * b:DH * b + DH],
                                            RDEN[:, u:u + 1], None, ALU.mult).then_inc(on_made, 1)

                for u in range(UNITS + 2):
                    if u < UNITS:
                        row_max(u)
                    if u >= 2:
                        normed(u - 2)
                dve.wait_ge(ya_hi, p + 1)
                ap = YAL[:, bass.ds(p, 1), :].rearrange("p a (r c) -> p (a c) r", r=ROWS)
                hi = YAH[:, bass.ds(p, 1), :].rearrange("p a (r c) -> p (a c) r", r=ROWS).bitcast(F32)
                nc.vector.tensor_tensor(ap, PS[:, 6, :].rearrange("p (c r) -> p c r", r=ROWS), hi,
                                        ALU.subtract).then_inc(ya_lo, 1)
            post(1)
            h_high(2)
            ffn(1, U_FFN2, B2, A2)
            diagonal(2, 1, DIAG2, 0.5)
            post(2)


_INS = ["x", "c", "ctx", "c_ctx", "w_mod", "b_mod", "norm_pre", "norm_post", "ffn1_w_gu", "ffn1_w_down", "ffn2_w_gu",
        "ffn2_w_down", "w_in", "w_out", "conv_w", "conv_b", "lru_wa", "lru_ba", "lru_wx", "lru_bx", "lru_lambda",
        "na_rpb"]


def kernel(**inputs):
    import numpy as _np
    import concourse.bacc as _bacc
    from concourse import mybir as _mybir
    from concourse.bass_utils import run_bass_kernel_spmd as _run

    nc = _bacc.Bacc("TRN2", target_bir_lowering=False, num_devices=1)
    arrays, args = {}, []
    for name in _INS:
        a = _np.ascontiguousarray(inputs[name])
        arrays[f"in_{name}"] = a
        args.append(nc.dram_tensor(f"in_{name}", a.shape, _mybir.dt.from_np(a.dtype), kind="ExternalInput").ap())
    args.append(nc.dram_tensor("out_dram", (1, LAT, D), _mybir.dt.float32, kind="ExternalOutput").ap())
    build(nc, *args)
    r = _run(nc, [arrays], core_ids=[0])
    return r.results[0]["out_dram"]
```

```python
from contextlib import ExitStack

import concourse.bass as bass
from concourse import mybir

F32 = mybir.dt.float32
F32R = mybir.dt.float32r
ALU = mybir.AluOpType
ACT = mybir.ActivationFunctionType
AX_X = mybir.AxisListType.X

P = 128
D = 1024
KC = D // P
HALF_D = D // 2
LAT, CTX = 512, 256
TOK = LAT + CTX
NLT, NCT = LAT // P, CTX // P
NTT = NLT + NCT
FF = 2816
FC = FF // P
PAIRS = FC // 2 - 1
REC = 512
RC = REC // P
GRID_W, ROWS = 64, 8
NH, DH = 8, 64
HPAIRS = NH // 2
QCOLS = 16
KCOLS = 32
NBLK = GRID_W // QCOLS
KSTART = [0, 8, 24, 32]
LOCK = ROWS * KCOLS
UNITS = 2 * NBLK
RPB_R, RPB_C = 15, 31
NEG = -1e30
EPS = 1e-6
LRU_C = 8.0
SLOTS = 6
PADW = 776
SCANW = 772
HSW = SCANW // 2
CTX0 = LAT + 3

R_C, R_CC, R_BMOD, R_PRE, N_R1 = 0, 8, 16, 88, 112
R_POST, R_CW, R_CB, R_BA, R_BX, R_LAM, N_R2 = 0, 24, 40, 44, 52, 60, 68

NM01 = 2 * KC
M01 = (2, 3, 0, 1, 4, 5) + (4, 5, 0, 1) * 2 + (4, 5)
B1, A1, D1 = (2, 3), (0, 1), (4, 5)
MIX = (2, 3, 0, 1, 4, 5)
B2, A2, D2 = (0, 1), (4, 5), (2, 3)

N_ALT, N_IN, N_OUT = 16, 20, 8
T_GATE = 2 * N_ALT
T_OUT = T_GATE + (N_IN - N_ALT)
N_MIX = T_OUT + N_OUT
GROUPS = [0, 3, 4, 2, 1]
REC_STEP = {1: 0, 2: 1, 4: 2, 5: 3, 7: 4, 8: 5, 10: 6, 11: 7}


def slot_uses():
    u = [0] * SLOTS
    for s in M01:
        u[s] += 1
    ffn1 = list(u)
    for s in B1 + A1 + D1:
        u[s] += FC // 2
    mix = list(u)
    for n in range(N_MIX):
        u[MIX[n % SLOTS]] += 1
    return ffn1, mix, u


U_FFN1, U_MIX, U_FFN2 = slot_uses()
RAW = U_FFN1


def mix_use(n):
    return MIX[n % SLOTS], U_MIX[MIX[n % SLOTS]] + n // SLOTS


def step_tile(n):
    return 2 * n if n < N_ALT else T_GATE + n - N_ALT


def known(v):
    return isinstance(v, int)


def build(nc, x, c, ctx_in, c_ctx, w_mod, b_mod, norm_pre, norm_post, w_gu1, w_dn1, w_gu2, w_dn2,
          w_in, w_out, conv_w, conv_b, lru_wa, lru_ba, lru_wx, lru_bx, lru_lambda, rpb, out):
    x_t = x.rearrange("b (t p) d -> (b t) p d", p=P)
    ctx_t = ctx_in.rearrange("b (t p) d -> (b t) p d", p=P)
    out_t = out.rearrange("b (t p) d -> (b t) p d", p=P)

    def row_blocks(w):
        return w.rearrange("l (k p) n -> (l k) p n", p=P)

    def col_range(w):
        return w.rearrange("l (k p) n -> p (l k) n", p=P)

    rpb_rows = nc.dram_tensor("rpb_rows", (ROWS, NH, ROWS, GRID_W), F32, kind="Internal").ap()
    rpb_full = nc.dram_tensor("rpb_full", (3, P, NH, LOCK), F32, kind="Internal").ap()

    with ExitStack() as ctx:
        base = 16512
        ctx.enter_context(nc.sbuf_tensor("fence", [P, (229344 - base) // 4], F32))

        def at(name, off, shape, dt=F32):
            return nc.alloc_sbuf_tensor_at(name, shape, dt, offset=base + off)

        YX_O = 0
        HH_O = YX_O + 4 * NTT * D
        HL_O = HH_O + 4 * KC * TOK
        W_O = HL_O + 4 * KC * TOK
        M_O = W_O + 3 * SLOTS * 4 * D
        S_O = M_O + 62656
        YX = at("YX", YX_O, [P, NTT, D])
        HH = at("HH", HH_O, [P, KC, TOK], F32R)
        HL = at("HL", HL_O, [P, KC, TOK], F32R)
        WR = at("WR", W_O, [P, SLOTS, D])
        WH = at("WH", W_O + SLOTS * 4 * D, [P, SLOTS, D], F32R)
        WL = at("WL", W_O + 2 * SLOTS * 4 * D, [P, SLOTS, D], F32R)
        R1 = at("R1", M_O, [P, P])
        R2 = at("R2", M_O + 512, [P, P])
        ZERO = at("ZERO", M_O + 1024, [P, 256])
        LT = at("LT", M_O + 2048, [P, 6, 8])
        AH = at("AH", M_O, [P, 2, TOK], F32R)
        AL = at("AL", M_O + 6144, [P, 2, TOK], F32R)
        SG = at("SG", M_O + 12288, [P, 2, TOK])
        H32 = at("H32", M_O + 6144, [P, 4, TOK])
        JUNK = at("JUNK", M_O + 12288, [P, D])
        MROW = at("MROW", M_O + 47104, [P, 2 * D])
        MRAW = at("MRAW", M_O + 18432, [P, 2, 2, 512])
        MACC = at("MACC", M_O + 26624, [P, 2, 512])
        MH = at("MH", M_O + 30720, [P, 2, 512], F32R)
        ML = at("ML", M_O + 34816, [P, 2, 512], F32R)
        DIAG = at("DIAG", M_O + 18432, [P, 2, KC, P])
        XST = at("XST", M_O + 30720, [P, 2, D])
        GROW = at("GROW", M_O + 38912, [P, 2, D])
        YG = at("YG", M_O + 47104, [P, 2, D])
        DG = at("DG", M_O + 55296, [P, NTT, P])
        ONES = at("ONES", M_O + 59392, [P, P])
        Y2 = at("Y2", M_O + 18432, [P, NLT, D])
        DIAG2 = at("DIAG2", M_O + 55296, [P, 1, KC, P])
        XR = at("XR", M_O, [P, RC, PADW])
        T = at("T", M_O + 12416, [P, 3, SCANW])
        Q = at("Q", M_O + 21696, [P, HPAIRS, LAT])
        K = at("K", M_O + 29888, [P, HPAIRS, TOK])
        V = at("V", M_O + 42176, [P, HPAIRS, TOK])
        GR = at("GR", M_O + 54464, [P, RC, LAT])
        XC = at("XC", M_O + 54464, [P, SCANW])
        T3 = at("T3", M_O + 54464 + 3104, [P, SCANW])
        GW = at("GW", YX_O + 4 * NLT * D, [P, 2, 2, RC, P])
        HHf = at("HHf", HH_O, [P, KC, TOK])
        HLf = at("HLf", HL_O, [P, KC, TOK])
        VCL = at("VCL", W_O + 2 * 4 * D, [P, 2, LAT], F32R)

        def v_hi(j, cols):
            return HH[:, j, cols] if j < 8 else HL[:, j - 8, cols]

        def v_lo(j, off, n):
            if j >= 8:
                return VCL[:, j - 8, off:off + n] if known(off) else VCL[:, j - 8, bass.ds(off, n)]
            w, s, o = (WH, WL)[j // 4], 4 + (j % 4) // 2, off + LAT * (j % 2)
            return w[:, s, o:o + n] if known(off) else w[:, s, bass.ds(o, n)]

        BIAS3 = HHf[:, :, LAT:TOK]
        BIAS0 = HLf[:, :, LAT:TOK]
        BIASM = HLf[:, 2:6, 0:LAT]
        YR6 = at("YR6", M_O + 42176, [P, 6, LAT], F32R)
        YR7 = [at(f"YR7_{j}", HL_O + 4 * TOK * (6 + j), [P, LAT], F32R) for j in range(2)]
        YRH = [YR6[:, j, :] for j in range(4)]
        YRL = [YR6[:, 4, :], YR6[:, 5, :], YR7[0][:, :], YR7[1][:, :]]
        YAH = at("YAH", M_O, [P, HPAIRS, LAT], F32R)
        YAL = at("YAL", M_O + 54464, [P, HPAIRS, LAT], F32R)
        GROW5T = at("GROW5T", M_O + 54464 + 4096, [P, D])
        GROW5 = at("GROW5", M_O + 8192, [P, D])
        DIAG5 = at("DIAG5", M_O + 12416, [P, 1, KC, P])
        PR = at("PR", M_O + 12416, [P, 2, LOCK + CTX])
        PTH = at("PTH", M_O + 16512, [P, 2, LOCK + CTX], F32R)
        PTL = at("PTL", W_O + 3 * 4 * D, [P, 2, LOCK + CTX], F32R)
        JUNK5 = at("JUNK5", M_O + 16512, [P, D])
        ONES5 = at("ONES5", M_O + 20608, [P, P])
        MASK = at("MASK", M_O + 21120, [P, 3, KCOLS])
        qk_at = [W_O + 4 * 4 * D, W_O]
        QH = [at(f"QH{e}", qk_at[e], [P, LAT], F32R) for e in range(2)]
        QL = [at(f"QL{e}", qk_at[e] + 2048, [P, LAT], F32R) for e in range(2)]
        KH = [at(f"KH{e}", qk_at[e] + 4096, [P, TOK], F32R) for e in range(2)]
        KL = [at(f"KL{e}", YX_O + 4 * NLT * D + 3072 * e, [P, TOK], F32R) for e in range(2)]
        ON = at("ON", YX_O + 4 * NLT * D + 6144, [P, NBLK, P])
        DG5 = at("DG5", M_O + 34816, [P, NLT, P])
        H5 = at("H5", M_O + 38080, [P, 4, LAT])
        so = [S_O]

        def small(name, shape, dt=F32):
            t = at(name, so[0], shape, dt)
            n = 4
            for v in shape[1:]:
                n *= v
            so[0] += (n + 31) // 32 * 32
            assert base + so[0] <= 229344
            return t

        IDENT = small("IDENT", [P, P])
        MOD = small("MOD", [P, 72, 2])
        C1 = small("C1", [P, N_R1])
        C2 = small("C2", [P, N_R2])
        CS = small("CS", [P, KC, 2])
        C4 = small("C4", [P, KC, 4], F32R)
        APRE = small("APRE", [P, KC, 2])
        GCOL = small("GCOL", [P, KC, 2])
        LOGC = small("LOGC", [P, 8])
        SS = small("SS", [P, 32])
        MS = small("MS", [P, 8])
        RS = small("RS", [P, 32])
        MHALF = small("MHALF", [P, 1])
        ONESR = small("ONESR", [P, 2], F32R)
        NMX = small("NMX", [P, UNITS])
        DEN = small("DEN", [P, UNITS])
        RDEN = small("RDEN", [P, UNITS])

        PS = ctx.enter_context(nc.psum_tensor("PS", [P, 8, 512], F32))

        def sem(name):
            return ctx.enter_context(nc.semaphore(name))

        landed, hi_made, lo_made, used = ([sem(f"{n}{i}") for i in range(SLOTS)]
                                          for n in ("landed", "hi_made", "lo_made", "used"))
        x_in = [sem(f"x_in{i}") for i in range(NTT)]
        xst_in = [sem(f"xst_in{i}") for i in range(2)]
        mod_in = [sem(f"mod_in{i}") for i in range(2)]
        c_in, rows_in, rpb_zeroed, rpb_put, rpb_spread, bias_in, gw_in, stored = (sem(n) for n in (
            "c_in", "rows_in", "rpb_zeroed", "rpb_put", "rpb_spread", "bias_in", "gw_in", "stored"))
        zero_set, ident_set, mhalf_set, y_zeroed, gw_zeroed, pads_zeroed, ones_set = (sem(n) for n in (
            "zero_set", "ident_set", "mhalf_set", "y_zeroed", "gw_zeroed", "pads_zeroed", "ones_set"))
        c_turned, rows_turned, c1_made, c2_made, cs_made, c4_hi, c4_made, lam_abs, lam_exp, logc_made = (sem(n) for n in (
            "c_turned", "rows_turned", "c1_made", "c2_made", "cs_made", "c4_hi", "c4_made", "lam_abs", "lam_exp", "logc_made"))
        mrow_act, mrow_dve, mod01_turned, mod01_made, a_made, mod_own, mod_hi, mod_lo, mod_red, mod_made, mod78_made = (
            sem(n) for n in ("mrow_act", "mrow_dve", "mod01_turned", "mod01_made", "a_made", "mod_own", "mod_hi",
                             "mod_lo", "mod_red", "mod_made", "mod78_made"))
        sq_pre, sq_post, rstd_pre, rstd_post, pool_own, dve_own = (sem(n) for n in (
            "sq_pre", "sq_post", "rstd_pre", "rstd_post", "pool_own", "dve_own"))
        dg_made, turned, h_hi, h_32, h_lo, h_lo_c = (sem(n) for n in (
            "dg_made", "turned", "h_hi", "h_32", "h_lo", "h_lo_c"))
        silu_made, au_made, a_hi, a_lo = ([sem(f"{n}{r}") for r in range(2)] for n in (
            "silu_made", "au_made", "a_hi", "a_lo"))
        y_ready, y_added, diag_made, grow_ps, grow_made, ysum, yg_pool, yg_dve, resid, onesr_set = (sem(n) for n in (
            "y_ready", "y_added", "diag_made", "grow_ps", "grow_made", "ysum", "yg_pool", "yg_dve", "resid",
            "onesr_set"))
        proj_out, gelu_out, xc_made, gates, r_sig, x_sig, r_at, om_made, root, scanned = (sem(n) for n in (
            "proj_out", "gelu_out", "xc_made", "gates", "r_sig", "x_sig", "r_at", "om_made", "root", "scanned"))
        vt, vt_hi, vt_lo, biasm_in, bias_made, yr_f, yr_hi, yr_lo = (sem(n) for n in (
            "vt", "vt_hi", "vt_lo", "biasm_in", "bias_made", "yr_f", "yr_hi", "yr_lo"))
        qk_hi, qk_made, scores, biased, maxed, exps, pt_ps, pt_hi, pt_lo, pv, inverted, on_made, ot, ya_hi, ya_lo = (
            sem(n) for n in ("qk_hi", "qk_made", "scores", "biased", "maxed", "exps", "pt_ps", "pt_hi", "pt_lo", "pv",
                             "inverted", "on_made", "ot", "ya_hi", "ya_lo"))
        wo_done, grow5_made = sem("wo_done"), sem("grow5_made")

        PRE_T, POST_T = [NTT, NTT, NLT], [NTT, NLT, NLT]
        PRE_C, POST_C = [0, 12, 22], [6, 18, 26]
        PRE_N, POST_N = [0, NTT, 2 * NTT], [0, NTT, NTT + NLT]

        def dg(n):
            return DG5 if n == 2 else DG

        def h32(n, k):
            return H32[:, k % 4, :] if n < 2 else H5[:, k % 4, :]

        def y_acc(n, t):
            return YX[:, t, :] if n == 0 else Y2[:, t, :]

        def ffn_counts(n):
            ntok = TOK if n == 0 else LAT
            return ntok, 2 * ntok // P, n * (FC // 2), n * (PAIRS + 1) * 2 * NTT

        def added_before(n):
            return n * PAIRS * 2 * NTT

        def token_halves(ntok):
            w = 384 if ntok == TOK else 512
            return [(j, slice(w * j, w * j + w), w) for j in range(ntok // w)]

        block = ctx.enter_context(nc.Block())

        @block.sync
        def _(sp):
            def load(s, u, src):
                if not known(u) or u > RAW[s]:
                    sp.wait_ge(lo_made[s], u - RAW[s])
                elif u:
                    sp.wait_ge(used[s], u)
                dst = WR[:, s, :]
                if len(src.shape) == 3:
                    dst = dst.rearrange("p (k n) -> p k n", n=src.shape[2])
                sp.dma_start(dst, src).then_inc(landed[s], 16)

            def at_cols(w, off, n):
                return col_range(w)[:, :, off:off + n] if known(off) else col_range(w)[:, :, bass.ds(off, n)]

            def mix_load(t):
                s, u = mix_use(t)
                if t < T_GATE and t % 2 == 1:
                    m = t // 2
                    src = row_blocks(w_mod)[m // 2][:, (7 + m % 2) * D:(8 + m % 2) * D]
                elif t < T_OUT:
                    n = t // 2 if t < T_GATE else t - T_GATE + N_ALT
                    src = at_cols(w_in, GROUPS[n // 4] * 512 + (n % 4) * P, P)
                else:
                    src = row_blocks(w_out)[t - T_OUT]
                load(s, u, src)

            def ffn_loads(n, w_gu, w_dn, uses, B, A, Dn):
                def up(slots, use, chunk):
                    for g in range(2):
                        load(slots[g], uses[slots[g]] + use, at_cols(w_gu, chunk * P + g * FF, P))

                def down(use, first):
                    for j in range(2):
                        r = first + j
                        src = row_blocks(w_dn)[r] if known(r) else \
                            row_blocks(w_dn)[bass.ds(r, 1)].rearrange("a p n -> p (a n)")
                        load(Dn[j], uses[Dn[j]] + use, src)

                def mod_load(i, q):
                    src = at_cols(w_mod, i * 512 + 2 * D, 512)[:, 2 * q:2 * q + 2, :]
                    sp.dma_start(MRAW[:, q % 2, :, :], src).then_inc(mod_in[q % 2], 16)

                up(B, 0, 0)
                up(A, 0, 1)
                up(B, 1, 2)
                down(0, 0)
                up(A, 1, 3)
                if n == 0:
                    mod_load(0, 0)
                    mod_load(0, 1)

                def pair(i, last, spread=False):
                    if not last:
                        up(B, i + 2, i * 2 + 4)
                    elif n == 0:
                        mix_load(0)
                        mix_load(1)
                    down(i + 1, i * 2 + 2)
                    if not last:
                        up(A, i + 2, i * 2 + 5)
                    elif n == 0:
                        mix_load(2)
                        mix_load(3)
                    if n == 0:
                        for q in (2, 3):
                            sp.wait_ge(mod_own, i * 16 + 4 * q - 4)
                            mod_load(i, q)
                        if not last:
                            for q in (0, 1):
                                sp.wait_ge(mod_own, i * 16 + 4 * q + 12)
                                mod_load(i + 1, q)
                    if spread:
                        spread_bias(i)

                steps = QCOLS // 2 if n == 0 else 0
                if steps:
                    with sp.Fori(0, steps, 1) as i:
                        pair(i, False, True)
                with sp.Fori(steps, PAIRS - 1, 1) as i:
                    pair(i, False)
                pair(PAIRS - 1, True)

            def spread_bias(i):
                sp.wait_ge(rpb_put, 16 * ROWS)
                for v, first in ((0, 31), (1, 23), (2, 15)):
                    for e in range(2):
                        src = rpb_rows[:, :, :, bass.ds(i * -2 + first - e, KCOLS)].rearrange("q h r x -> q (h r) x")
                        dst = rpb_full[v, bass.ds(i * 16 + 8 * e, 8)].rearrange("q h (r x) -> q (h r) x", x=KCOLS)
                        sp.dma_start(dst, src).then_inc(rpb_spread, 16)

            sp.dma_start(R1[R_C:R_C + KC, :], c.rearrange("l (r p) -> (l r) p", p=P)).then_inc(c_in, 16)
            sp.dma_start(R1[R_CC:R_CC + KC, :], c_ctx.rearrange("(r p) -> r p", p=P)).then_inc(c_in, 16)
            for n in range(NM01):
                load(M01[n], M01[:n].count(M01[n]), row_blocks(w_mod)[n // 2][:, (n % 2) * D:(n % 2 + 1) * D])
            ffn_loads(0, w_gu1, w_dn1, U_FFN1, B1, A1, D1)
            sp.wait_ge(mod_red, PAIRS)
            for t in range(NTT):
                if t >= 2:
                    sp.wait_ge(resid, t - 1)
                sp.dma_start(XST[:, t % 2, :], x_t[t] if t < NLT else ctx_t[t - NLT]).then_inc(xst_in[t % 2], 16)
                if t == 1:
                    mix_load(4)
                    mix_load(5)
            sp.wait_ge(gw_zeroed, 1)
            for g, w in ((0, lru_wa), (1, lru_wx)):
                src = w.rearrange("l d (c two) i j -> (l two) i (d c) j", two=2)
                for h in range(2):
                    dst = GW[DH * h:DH * h + DH, g].rearrange("p d c n -> p (d c) n")[:, :, DH * h:DH * h + DH]
                    sp.dma_start(dst, src[h]).then_inc(gw_in, 16)
            for t in range(6, 29):
                mix_load(t)
            s, u = mix_use(step_tile(11))
            sp.wait_ge(used[s], u + 1)
            sp.wait_ge(rpb_spread, 16 * 3 * QCOLS)
            sp.dma_start(BIAS0, rpb_full[0]).then_inc(bias_in, 16)
            sp.dma_start(BIAS3, rpb_full[2]).then_inc(bias_in, 16)
            for t in range(29, T_OUT + 4):
                mix_load(t)
            s, u = mix_use(step_tile(N_IN - 1))
            sp.wait_ge(used[s], u + 1)
            sp.dma_start(BIASM, rpb_full[1].rearrange("p (a h) n -> p a (h n)", h=2)).then_inc(biasm_in, 16)
            sp.wait_ge(pv, HPAIRS * UNITS)
            for t in range(T_OUT + 4, N_MIX):
                mix_load(t)
            ffn_loads(1, w_gu2, w_dn2, U_FFN2, B2, A2, D2)
            for t in range(NLT):
                sp.wait_ge(resid, POST_N[2] + t + 1)
                sp.dma_start(out_t[t], YX[:, t, :]).then_inc(stored, 16)
            sp.wait_ge(stored, 16 * NLT)

        @block.scalar
        def _(act):
            def make_hi(s, u):
                act.wait_ge(landed[s], u * 16 + 16)
                if not (known(u) and u == 0):
                    act.wait_ge(used[s], u)
                nc.scalar.activation(WH[:, s, :], WR[:, s, :], ACT.Copy).then_inc(hi_made[s], 1)

            squares = []

            def square(src, junk, col, done):
                if squares:
                    act.wait_ge(squares[-1], squares.count(squares[-1]))
                squares.append(done)
                nc.scalar.activation(junk, src, ACT.Square, scale=D ** -0.5, accum_out=SS[:, col:col + 1]).then_inc(done, 1)

            def h_full(n):
                for k in range(KC):
                    b = 2 * (k % 4)
                    if k == 0:
                        act.wait_ge(a_made, n + 1)
                    act.wait_ge(turned, n * KC + k + 1)
                    if k >= 4:
                        act.wait_ge(h_lo, n * KC + k - 3)
                        if PRE_T[n] == NTT:
                            act.wait_ge(h_lo_c, n * KC + k - 3)
                    m = 24 * n + k
                    ins = nc.scalar.activation(h32(n, k)[:, 0:LAT], PS[:, b, 0:LAT], ACT.Identity,
                                               bias=MOD[:, m, 0:1], scale=APRE[:, k, 0:1])
                    if PRE_T[n] == NTT:
                        ins = nc.scalar.activation(h32(n, k)[:, LAT:TOK], PS[:, b + 1, 0:CTX], ACT.Identity,
                                                   bias=MOD[:, m, 1:2], scale=APRE[:, k, 1:2])
                    ins.then_inc(h_32, 1)

            def ffn(n, uses, B, A, Dn):
                ntok, nj, cb, yb = ffn_counts(n)
                nh = len(token_halves(ntok))

                def silu(r, cnt, bank):
                    g = (A, B)[r][0]
                    act.wait_ge(used[g], cnt + uses[g] - cb)
                    if not (known(cnt) and cnt == 1):
                        act.wait_ge(a_lo[r], cnt - 1)
                    nc.scalar.activation(SG[:, r, 0:ntok].rearrange("p (h w) -> p h w", h=nh),
                                         PS[:, bank:bank + nh, 0:ntok // nh], ACT.Silu).then_inc(silu_made[r], 1)

                def high(r, cnt):
                    act.wait_ge(au_made[r], cnt)
                    nc.scalar.activation(AH[:, r, 0:ntok], SG[:, r, 0:ntok], ACT.Copy).then_inc(a_hi[r], 1)

                def tiles(slots, use):
                    for s in slots:
                        make_hi(s, uses[s] + use)

                def pair(i, whole):
                    if n == 0:
                        act.wait_ge(mod_own, i * 16 + 16)
                        nc.scalar.activation(MH[:, :, :], MACC[:, :, :], ACT.Copy).then_inc(mod_hi, 1)
                    silu(1, i + cb + 2, 0)
                    if whole:
                        tiles(B, i + 2)
                    act.wait_ge(y_ready, i * nj + yb + nj)
                    high(1, i + cb + 2)
                    tiles(Dn, i + 1)
                    silu(0, i + cb + 2, 4)
                    if whole:
                        tiles(A, i + 2)
                    high(0, i + cb + 2)

                silu(1, cb + 1, 0)
                tiles(B, 1)
                tiles(Dn, 0)
                high(1, cb + 1)
                silu(0, cb + 1, 4)
                tiles(A, 1)
                high(0, cb + 1)
                with act.Fori(0, PAIRS if n == 0 else PAIRS - 1, 1) as i:
                    pair(i, True)
                if n == 1:
                    pair(PAIRS - 1, False)

            def grow_out(n, dsts):
                act.wait_ge(grow_ps, n + 1)
                for dst, bank in dsts:
                    ins = nc.scalar.activation(dst.rearrange("p (a n) -> p a n", a=2), PS[:, bank:bank + 2, :], ACT.Copy)
                ins.then_inc(grow_made, 1)

            def post_squares(n):
                for t in range(POST_T[n] + (n < 2)):
                    if t < POST_T[n]:
                        if n == 1:
                            act.wait_ge(wo_done, t + 1)
                            src = PS[:, 2 * t:2 * t + 2, :].rearrange("p a n -> p (a n)")
                        else:
                            act.wait_ge(ysum, t + 1 + (NTT if n == 2 else 0))
                            src = y_acc(n // 2, t)
                        square(src, JUNK5[:, :] if n == 1 else JUNK[:, :], POST_C[n] + t, sq_post)
                    if n < 2 and t >= 1:
                        act.wait_ge(resid, POST_N[n] + t)
                        square(YX[:, t - 1, :], JUNK5[:, :] if n == 1 else JUNK[:, :], PRE_C[n + 1] + t - 1, sq_pre)

            def load_rows(dst, r, n, src):
                act.dma_start(dst[r:r + n, :], src).then_inc(rows_in, 16)

            def rows128(a):
                return a.rearrange("l (r p) -> (l r) p", p=P) if len(a.shape) == 2 else \
                    a.rearrange("l m (r p) -> (l m r) p", p=P)

            def load_x(t):
                act.dma_start(YX[:, t, :], x_t[t] if t < NLT else ctx_t[t - NLT]).then_inc(x_in[t], 16)

            load_x(0)
            act.wait_ge(c_turned, 1)
            nc.scalar.activation(CS[:, :, :].rearrange("p k a -> p a k"), PS[:, 3, 0:16].rearrange("p (a k) -> p a k", a=2),
                                 ACT.Silu).then_inc(cs_made, 1)
            load_rows(R1, R_BMOD, 72, rows128(b_mod))
            load_rows(R1, R_PRE, 24, rows128(norm_pre))
            load_x(1)
            small_rows = [(R_POST, 24, norm_post), (R_CW, 16, conv_w), (R_CB, RC, conv_b), (R_BA, 8, lru_ba),
                          (R_BX, 8, lru_bx), (R_LAM, 8, lru_lambda)]
            for t in range(NTT):
                if t + 2 < NTT:
                    load_x(t + 2)
                r0, cnt, src = small_rows[t]
                load_rows(R2, r0, cnt, rows128(src))
                act.wait_ge(x_in[t], 16)
                square(YX[:, t, :], JUNK[:, :], PRE_C[0] + t, sq_pre)
            act.wait_ge(used[M01[-1]], U_FFN1[M01[-1]])
            nc.scalar.activation(MROW[0:2, 0:D].rearrange("p (a n) -> p a n", a=2), PS[0:2, 4:6, :],
                                 ACT.Copy).then_inc(mrow_act, 1)
            make_hi(B1[0], U_FFN1[B1[0]])
            h_full(0)
            for s in (B1[1],) + A1:
                make_hi(s, U_FFN1[s])
            act.wait_ge(cs_made, 1)
            nc.scalar.activation(C4[:, :, 0:4:2], CS[:, :, :], ACT.Copy).then_inc(c4_hi, 1)
            act.wait_ge(ones_set, 1)
            nc.scalar.activation(ONESR[:, :], ONES[:, 0:2], ACT.Copy).then_inc(onesr_set, 1)
            act.wait_ge(zero_set, 1)
            act.dma_start(rpb_rows.rearrange("q h r x -> (q h r x)").rearrange("(p n) -> p n", p=P),
                          ZERO[:, :]).then_inc(rpb_zeroed, 16)
            act.wait_ge(lam_abs, 1)
            nc.scalar.activation(LT[:, 1, :], LT[:, 0, :], ACT.Exp, scale=-1.0).then_inc(lam_exp, 1)
            act.wait_ge(rpb_zeroed, 16)
            for qr in range(ROWS):
                act.dma_start(rpb_rows[qr, :, :, 16:16 + RPB_C],
                              rpb[0, :, ROWS - 1 - qr:2 * ROWS - 1 - qr, :]).then_inc(rpb_put, 16)
            ffn(0, U_FFN1, B1, A1, D1)
            grow_out(0, [(GROW[:, 0, :], 0), (GROW[:, 1, :], 2)])
            post_squares(0)
            for t in (4, 5):
                make_hi(*mix_use(t))
            h_full(1)

            def rec_unit(r):
                j = (r % 2) * RC + r // 2
                act.wait_ge(gates, r + 1)
                if r:
                    act.wait_ge(scanned, r)
                nc.scalar.activation(T[:, 0, :].rearrange("p (h w) -> p h w", h=2), PS[:, 4:6, 0:HSW],
                                     ACT.Sigmoid, bias=C2[:, R_BA + j:R_BA + j + 1]).then_inc(r_sig, 1)
                nc.scalar.activation(T[:, 1, :].rearrange("p (h w) -> p h w", h=2), PS[:, 6:8, 0:HSW],
                                     ACT.Sigmoid, bias=C2[:, R_BX + j:R_BX + j + 1]).then_inc(x_sig, 1)
                act.wait_ge(r_sig, r + 1)
                nc.scalar.activation(T[:, 2, :], T[:, 0, :], ACT.Exp, scale=LOGC[:, j:j + 1])
                nc.scalar.activation(T3[:, :], T[:, 0, :], ACT.Tanh, scale=LOGC[:, j:j + 1]).then_inc(r_at, 1)
                act.wait_ge(om_made, r + 1)
                nc.scalar.activation(T[:, 0, :], T[:, 0, :], ACT.Sqrt, scale=-1.0).then_inc(root, 1)

            t_hi = 6
            act.wait_ge(logc_made, 1)
            for n in range(N_IN):
                while t_hi <= step_tile(n) + 6 and t_hi < T_OUT + 4:
                    make_hi(*mix_use(t_hi))
                    t_hi += 1
                if n in REC_STEP:
                    rec_unit(REC_STEP[n])
                if n >= N_ALT:
                    if n == N_ALT:
                        act.wait_ge(scanned, 2 * RC)
                    s, u = mix_use(step_tile(n))
                    act.wait_ge(used[s], u + 1)
                    nc.scalar.activation(GR[:, n - N_ALT, :], PS[:, 2 * (n % 2), :], ACT.Gelu_apprx_tanh).then_inc(gelu_out, 1)
            for j in range(10):
                act.wait_ge(vt, j + 1)
                nc.scalar.activation(v_hi(j, slice(0, LAT)), PS[:, j % 4, :], ACT.Copy).then_inc(vt_hi, 1)
            for j in range(RC):
                act.wait_ge(yr_f, j + 1)
                nc.scalar.activation(YRH[j], XR[:, j, 2:2 + LAT], ACT.Copy).then_inc(yr_hi, 1)
            grow_out(1, [(GROW5T[:, :], 6)])
            with act.Fori(0, HPAIRS // 2, 1) as i:
                ub = i * (2 * UNITS)

                def exponentials(u):
                    act.wait_ge(maxed, ub + u + 1)
                    if u >= 2:
                        act.wait_ge(pt_ps, ub + u - 1)
                    nc.scalar.activation(PR[:, u % 2, :], PS[:, u % 2, :], ACT.Exp, bias=NMX[:, u % UNITS:u % UNITS + 1],
                                         accum_out=DEN[:, u % UNITS:u % UNITS + 1]).then_inc(exps, 1)

                def transposed_hi(u):
                    act.wait_ge(pt_ps, ub + u + 1)
                    if u >= 2:
                        act.wait_ge(pv, ub + u - 1)
                    nc.scalar.activation(PTH[:, u % 2, :], PS[:, 2 + u % 2, :], ACT.Copy).then_inc(pt_hi, 1)

                def output_hi(e):
                    act.wait_ge(ot, i * 2 + e + 1)
                    act.wait_ge(yr_lo, RC)
                    nc.scalar.activation(YAH[:, bass.ds(i * 2 + e, 1), :].rearrange("p a (r c) -> p (a c) r", r=ROWS),
                                         PS[:, 6 + e, :].rearrange("p (c r) -> p c r", r=ROWS), ACT.Copy).then_inc(ya_hi, 1)

                exponentials(0)
                exponentials(1)
                for u in range(2 * UNITS):
                    transposed_hi(u)
                    if u + 2 < 2 * UNITS:
                        exponentials(u + 2)
                    if u == UNITS + 1:
                        output_hi(0)
                output_hi(1)
            act.wait_ge(pv, HPAIRS * UNITS)
            for t in range(T_OUT + 4, N_MIX):
                make_hi(*mix_use(t))
            post_squares(1)
            for s in B2 + A2:
                make_hi(s, U_FFN2[s])
            h_full(2)
            ffn(1, U_FFN2, B2, A2, D2)
            grow_out(2, [(GROW[:, 0, :], 0)])
            post_squares(2)

        @block.gpsimd
        def _(pool):
            own = [0]

            def after_own(ins):
                own[0] += 1
                ins.then_inc(pool_own, 1)
                pool.wait_ge(pool_own, own[0])

            def make_lo(s, u):
                pool.wait_ge(hi_made[s], u - RAW[s] + 1)
                nc.gpsimd.tensor_tensor(WL[:, s, :], WR[:, s, :], WH[:, s, :].bitcast(F32),
                                        ALU.subtract).then_inc(lo_made[s], 1)

            def rstd(col, t, ready, cnt, done):
                pool.wait_ge(ready, cnt)
                after_own(nc.gpsimd.tensor_scalar(MS[:, t:t + 1], SS[:, col:col + 1], EPS, None, ALU.add))
                nc.gpsimd.tensor_tensor(RS[:, col:col + 1], MS[:, t:t + 1], MHALF[:, :], ALU.pow).then_inc(done, 1)

            def diagonal_pre(n, t):
                rstd(PRE_C[n] + t, t, sq_pre, PRE_N[n] + t + 1, rstd_pre)
                pool.wait_ge(rstd_pre, PRE_N[n] + t + 1)
                r = RS[:, PRE_C[n] + t:PRE_C[n] + t + 1].broadcast_to([P, P])
                nc.gpsimd.tensor_tensor(dg(n)[:, t, :], IDENT[:, :], r, ALU.mult).then_inc(dg_made, 1)

            def h_low(n):
                for k in range(KC):
                    pool.wait_ge(h_hi, n * KC + k + 1)
                    nc.gpsimd.tensor_tensor(HL[:, k, LAT:TOK], h32(n, k)[:, LAT:TOK], HH[:, k, LAT:TOK].bitcast(F32),
                                            ALU.subtract).then_inc(h_lo_c, 1)

            def ffn(n, uses, B, A, Dn):
                def tiles(slots, use):
                    for s in slots:
                        make_lo(s, uses[s] + use)

                tiles(B, 1)
                tiles(Dn, 0)
                tiles(A, 1)
                with pool.Fori(0, PAIRS if n == 0 else PAIRS - 1, 1) as i:
                    tiles(B, i + 2)
                    tiles(Dn, i + 1)
                    tiles(A, i + 2)
                if n == 1:
                    tiles(Dn, PAIRS)

            def post(n):
                for t in range(POST_T[n] + 1):
                    if n != 1 and t < POST_T[n] and t % 2 == 0:
                        pool.wait_ge(ysum, t + 1 + (NTT if n == 2 else 0))
                        if t == 0:
                            pool.wait_ge(grow_made, n + 1)
                        else:
                            pool.wait_ge(resid, POST_N[n] + t - 1)
                        nc.gpsimd.tensor_tensor(YG[:, 0, :], y_acc(n // 2, t), GROW[:, 0 if t < NLT else 1, :],
                                                ALU.mult).then_inc(yg_pool, 1)
                    if t < POST_T[n]:
                        rstd(POST_C[n] + t, t, sq_post, POST_N[n] + t + 1, rstd_post)
                    if n < 2 and t >= 1:
                        diagonal_pre(n + 1, t - 1)

            nc.gpsimd.memset(ZERO[:, :], 0.0).then_inc(zero_set, 1)
            after_own(nc.gpsimd.memset(IDENT[:, :], 0.0))
            nc.gpsimd.affine_select(out=IDENT[:, :], in_=IDENT[:, :], compare_op=ALU.not_equal, fill=1.0, base=0,
                                    pattern=[[-1, P]], channel_multiplier=1).then_inc(ident_set, 1)
            nc.gpsimd.memset(MHALF[:, :], -0.5).then_inc(mhalf_set, 1)
            nc.gpsimd.memset(ONES[:, :], 1.0).then_inc(ones_set, 1)
            pool.wait_ge(mhalf_set, 1)
            pool.wait_ge(ident_set, 1)
            for t in range(NTT):
                diagonal_pre(0, t)
            make_lo(B1[0], U_FFN1[B1[0]])
            h_low(0)
            for s in (B1[1],) + A1:
                make_lo(s, U_FFN1[s])
            pool.wait_ge(turned, KC)
            nc.gpsimd.memset(YX[:, :, :], 0.0).then_inc(y_zeroed, 1)
            ffn(0, U_FFN1, B1, A1, D1)
            post(0)
            h_low(1)
            for t in (4, 5):
                make_lo(*mix_use(t))
            pool.wait_ge(turned, 2 * KC)
            nc.gpsimd.memset(GW[:, :, :, :, :], 0.0).then_inc(gw_zeroed, 1)
            pool.wait_ge(h_lo, 2 * KC)
            pool.wait_ge(h_lo_c, 2 * KC)
            for j in range(RC):
                for a, b in ((0, 2), (2 + LAT, 2 + CTX0), (2 + CTX0 + CTX, PADW)):
                    ins = nc.gpsimd.memset(XR[:, j, a:b], 0.0)
            ins.then_inc(pads_zeroed, 1)
            for t in range(6, 35):
                make_lo(*mix_use(t))
            pool.wait_ge(scanned, 2 * RC)
            nc.gpsimd.memset(ONES5[:, :], 1.0).then_inc(ones_set, 1)
            after_own(nc.gpsimd.memset(MASK[:, :, :], 0.0))

            def window(v, x0, n, base_, step, cm):
                part = MASK[:, v, x0:x0 + n]
                after_own(nc.gpsimd.affine_select(out=part, in_=part, compare_op=ALU.is_ge, fill=NEG, base=base_,
                                                  pattern=[[step, n]], channel_multiplier=cm))

            window(0, 0, 16, 64 + 7, 8, -1)
            window(0, 16, 16, 56 - 128, -8, 1)
            window(1, 0, 32, 7, 8, -1)
            window(1, 0, 32, 120, -8, 1)
            window(2, 0, 16, 7 - 64, 8, -1)
            window(2, 16, 16, 184 - 128, -8, 1)
            def mask_bias(v, b):
                view = b.rearrange("p a (r x) -> p a r x", x=KCOLS)
                m = MASK[:, v, :].unsqueeze(1).unsqueeze(1).broadcast_to([P, view.shape[1], view.shape[2], KCOLS])
                nc.gpsimd.tensor_tensor(view, view, m, ALU.add).then_inc(bias_made, 1)

            pool.wait_ge(bias_in, 32)
            mask_bias(0, BIAS0)
            mask_bias(2, BIAS3)
            make_lo(*mix_use(35))

            def heads(p):
                e = p % 2
                if p >= 2:
                    pool.wait_ge(scores, UNITS * (p - 1))
                else:
                    for s in ((4, 5), (0, 1))[e]:
                        pool.wait_ge(lo_made[s], mix_use((35, T_OUT + 3)[e])[1] - RAW[s] + 1)
                nc.gpsimd.tensor_copy(QH[e][:, :], Q[:, p, :])
                nc.gpsimd.tensor_copy(KH[e][:, :], K[:, p, :]).then_inc(qk_hi, 1)
                pool.wait_ge(qk_hi, p + 1)
                nc.gpsimd.tensor_tensor(QL[e][:, :], Q[:, p, :], QH[e][:, :].bitcast(F32), ALU.subtract)
                nc.gpsimd.tensor_tensor(KL[e][:, :], K[:, p, :], KH[e][:, :].bitcast(F32), ALU.subtract).then_inc(qk_made, 1)

            pool.wait_ge(proj_out, N_ALT)
            heads(0)
            for t in range(T_OUT, T_OUT + 2):
                make_lo(*mix_use(t))
            pool.wait_ge(biasm_in, 16)
            mask_bias(1, BIASM)
            for t in range(T_OUT + 2, T_OUT + 4):
                make_lo(*mix_use(t))
            heads(1)
            for j in range(RC):
                pool.wait_ge(yr_hi, j + 1)
                nc.gpsimd.tensor_tensor(YRL[j], XR[:, j, 2:2 + LAT], YRH[j].bitcast(F32), ALU.subtract).then_inc(yr_lo, 1)
            pool.wait_ge(yr_lo, RC)
            pool.wait_ge(grow_made, 2)
            nc.gpsimd.tensor_copy(GROW5[:, :], GROW5T[:, :]).then_inc(grow5_made, 1)
            for p in range(2, HPAIRS):
                heads(p)
            for t in range(T_OUT + 4, N_MIX):
                make_lo(*mix_use(t))
            post(1)
            for s in B2 + A2:
                make_lo(s, U_FFN2[s])
            pool.wait_ge(turned, 3 * KC)
            nc.gpsimd.memset(Y2[:, :, :], 0.0).then_inc(y_zeroed, 1)
            nc.gpsimd.memset(ONES[:, :], 1.0).then_inc(ones_set, 1)
            ffn(1, U_FFN2, B2, A2, D2)
            post(2)

        @block.tensor
        def _(pe):
            def turn(n, chunks):
                last = PRE_T[n] - 1

                def part(k, tiles):
                    for t in tiles:
                        bank, col = (2 * (k % 4), t) if t < NLT else (2 * (k % 4) + 1, t - NLT)
                        pe.wait_ge(dg_made, PRE_N[n] + t + 1)
                        ins = nc.tensor.matmul(PS[:, bank, col * P:col * P + P], YX[:, t, k * P:k * P + P],
                                               dg(n)[:, t, :], start=True, stop=True)
                    return ins

                early = [k for k in chunks if k < 4] if n else []
                for k in early:
                    if n == 1 and k == 2:
                        pe.wait_ge(ysum, NTT)
                    if n == 2:
                        pe.wait_ge(yg_dve, NTT // 2 + k + 1)
                    part(k, range(last - 1))
                for k in early:
                    part(k, [last - 1])
                for k in chunks:
                    if k >= 4:
                        pe.wait_ge(h_32, n * KC + k - 3)
                    part(k, [last] if k in early else range(last + 1)).then_inc(turned, 1)

            def project(s, halves, banks, wait_k=None):
                ins = None
                for k in range(KC):
                    if wait_k is not None:
                        pe.wait_ge(h_lo, wait_k + k + 1)
                        if wait_k < 2 * KC:
                            pe.wait_ge(h_lo_c, wait_k + k + 1)
                    wh, wl = WH[:, s, k * P:k * P + P], WL[:, s, k * P:k * P + P]
                    for w, h, first, last in ((wh, HH, True, False), (wh, HL, False, False), (wl, HH, False, True)):
                        for (j, sl, n), bank in zip(halves, banks):
                            ins = nc.tensor.matmul(PS[:, bank, 0:n], w, h[:, k, sl], start=(k == 0 and first),
                                                   stop=(k == KC - 1 and last))
                return ins

            def three(out_ps, lh, ll, rh, rl, first, last):
                nc.tensor.matmul(out_ps, lh, rh, start=first, stop=False)
                nc.tensor.matmul(out_ps, lh, rl, start=False, stop=False)
                return nc.tensor.matmul(out_ps, ll, rh, start=False, stop=last)

            def ffn(n, uses, B, A, Dn):
                ntok, nj, cb, yb = ffn_counts(n)
                ab = added_before(n)
                halves = token_halves(ntok)

                def up(r, use, bank, wait_k=None):
                    slots = (A, B)[r]
                    for g, s in enumerate(slots):
                        pe.wait_ge(lo_made[s], uses[s] - RAW[s] + use + 1)
                        if g == 1 and r == 0 and not known(use):
                            pe.wait_ge(y_added, (use - 1) * nj + ab + nj)
                        bk = bank + 2 * g
                        project(s, halves, [bk, bk + 1], wait_k if g == 0 else None).then_inc(used[s], 1)
                        if g == 0 and r == 0 and not known(use):
                            release_down((use - 1) * nj + yb + nj)

                def release_down(y_count):
                    pe.wait_ge(y_ready, y_count)
                    pe.nop().then_inc(used[Dn[1]], 1)

                def down_unit(j, use, bank):
                    t, half = j // 2, j % 2
                    tk = slice(t * P, t * P + P)
                    col = slice(half * HALF_D, half * HALF_D + HALF_D)
                    for q, r in ((0, 1), (1, 0)):
                        s = Dn[q]
                        ins = three(PS[:, bank, :], AH[:, r, tk], AL[:, r, tk], WH[:, s, col], WL[:, s, col],
                                    q == 0, q == 1)
                        if j == nj - 1:
                            if q == 0:
                                ins.then_inc(used[s], 1)
                    return ins

                pe.wait_ge(h_32, n * 2 * KC + KC)
                up(1, 0, 0, wait_k=2 * n * KC)
                up(0, 0, 4)
                if n == 0:
                    pe.wait_ge(onesr_set, 1)
                with pe.Fori(0, PAIRS, 1) as i:
                    pe.wait_ge(au_made[1], i + cb + 1)
                    up(1, i + 1, 0)
                    for q in range(2):
                        pe.wait_ge(lo_made[Dn[q]], i + uses[Dn[q]] - RAW[Dn[q]] + 1)
                    for r in range(2):
                        pe.wait_ge(a_lo[r], i + cb + 1)
                    def reduce_mod():
                        pe.wait_ge(mod_lo, i + 1)
                        for m in range(4):
                            for r in range(2):
                                c0 = 4 * m + 2 * r
                                nc.tensor.matmul(PS[:, 7, c0:c0 + 2], MH[:, r, m * P:m * P + P], ONESR[:, :],
                                                 start=True, stop=False)
                                ins = nc.tensor.matmul(PS[:, 7, c0:c0 + 2], ML[:, r, m * P:m * P + P], ONESR[:, :],
                                                       start=False, stop=True)
                        ins.then_inc(mod_red, 1)
                    for j in range(nj):
                        if n == 0 and j == 3:
                            pe.wait_ge(mod_made, i + 1)
                        if j >= 4:
                            pe.wait_ge(y_added, i * nj + ab + j - 3)
                        down_unit(j, i, 4 + j % 4).then_inc(y_ready, 1)
                        if n == 0 and j == 0:
                            reduce_mod()
                    pe.wait_ge(y_added, i * nj + ab + nj - 2)
                    up(0, i + 1, 4)
                pe.wait_ge(au_made[1], cb + PAIRS + 1)
                grow(2 * n, 2 if n == 0 else 1, 0, ONES, DIAG if n == 0 else DIAG2, (1, 3)[n])
                for q in range(2):
                    pe.wait_ge(lo_made[Dn[q]], uses[Dn[q]] - RAW[Dn[q]] + PAIRS + 1)
                for r in range(2):
                    pe.wait_ge(a_lo[r], cb + PAIRS + 1)
                for j in range(nj):
                    if j >= 4 and j % 2 == 0:
                        pe.wait_ge(ysum, n * NTT + j // 2 - 1)
                    down_unit(j, PAIRS, 4 + j % 4).then_inc(y_ready, 1)
                release_down(yb + nj * (PAIRS + 1))

            def grow(n, streams, bank, ones, diag, ones_count):
                pe.wait_ge(ones_set, ones_count)
                pe.wait_ge(diag_made, n + 1)
                for g in range(streams):
                    for k in range(KC):
                        b = bank + 2 * g + k // 4
                        ins = nc.tensor.matmul(PS[:, b, (k % 4) * P:(k % 4) * P + P], ones[:, :],
                                               diag[:, g, k, :], start=True, stop=True)
                ins.then_inc(grow_ps, 1)

            def mod_tile(s, k):
                for m in range(KC):
                    for q, w in enumerate((WH, WL)):
                        ins = nc.tensor.matmul(PS[:, 7, 4 * m:4 * m + 4], w[:, s, m * P:m * P + P], C4[:, k, :],
                                               start=(q == 0), stop=(q == 1))
                return ins

            pe.wait_ge(ident_set, 1)
            pe.wait_ge(c_in, 32)
            nc.tensor.transpose(PS[:, 3, 0:2 * KC], R1[0:2 * KC, :], IDENT[0:2 * KC, 0:2 * KC]).then_inc(c_turned, 1)
            pe.wait_ge(cs_made, 1)
            for n in range(NM01):
                s = M01[n]
                pe.wait_ge(landed[s], 16 * M01[:n].count(s) + 16)
                for half in range(2):
                    ins = nc.tensor.matmul(PS[0:2, 4 + 2 * (n % 2) + half, :], CS[:, n // 2, :],
                                           WR[:, s, half * HALF_D:half * HALF_D + HALF_D], start=(n < 2),
                                           stop=(n >= NM01 - 2))
                ins.then_inc(used[s], 1)
            turn(0, (0,))
            pe.wait_ge(rows_in, 128)
            nc.tensor.transpose(PS[:, 2, 0:N_R1], R1[0:N_R1, :], IDENT[0:N_R1, 0:N_R1])
            nc.tensor.transpose(PS[:, 3, 0:N_R2], R2[0:N_R2, :], IDENT[0:N_R2, 0:N_R2]).then_inc(rows_turned, 1)
            pe.wait_ge(mrow_act, 1)
            pe.wait_ge(mrow_dve, 1)
            for m in range(2 * KC):
                ins = nc.tensor.transpose(PS[:, 4, 2 * m:2 * m + 2], MROW[0:2, m * P:m * P + P], IDENT[0:2, 0:2])
            ins.then_inc(mod01_turned, 1)
            pe.wait_ge(c2_made, 1)
            turn(0, (1,))
            pe.wait_ge(mod01_made, 1)
            turn(0, range(2, KC))
            ffn(0, U_FFN1, B1, A1, D1)
            pe.wait_ge(grow_made, 1)
            turn(1, range(KC))
            pe.wait_ge(h_32, 2 * KC)
            lat = (0, slice(0, LAT), LAT)
            both = [lat, (1, slice(LAT, TOK), CTX)]
            for n in range(N_IN):
                s, u = mix_use(step_tile(n))
                pe.wait_ge(lo_made[s], u - RAW[s] + 1)
                if 2 <= n < N_ALT + 2:
                    pe.wait_ge(proj_out, n - 1)
                elif n >= N_ALT + 2:
                    pe.wait_ge(gelu_out, n - N_ALT - 1)
                b = 2 * (n % 2)
                ins = project(s, both if n < 12 else [lat], [b, b + 1], wait_k=KC if n == 0 else None)
                ins.then_inc(used[s], 1)
                if n < N_ALT:
                    s, u = mix_use(step_tile(n) + 1)
                    pe.wait_ge(lo_made[s], u - RAW[s] + 1)
                    done = [REC_STEP[q] for q in REC_STEP if q < n]
                    if done:
                        pe.wait_ge(x_sig, max(done) + 1)
                    if n:
                        pe.wait_ge(mod78_made, n)
                    if n == 0:
                        pe.wait_ge(c4_made, 1)
                    mod_tile(s, n // 2).then_inc(used[s], 1)
                if n in REC_STEP:
                    r = REC_STEP[n]
                    cc, d = r // 2, r % 2
                    pe.wait_ge(xc_made, cc + 1)
                    if r == 0:
                        pe.wait_ge(gw_in, 64)
                    else:
                        pe.wait_ge(x_sig, r)
                    for g in range(2):
                        for h in range(2):
                            if g == 1 and h == 1:
                                pe.wait_ge(mod78_made, n + 1)
                            ins = nc.tensor.matmul(PS[:, 4 + 2 * g + h, 0:HSW], GW[:, g, d, cc, :],
                                                   XC[:, HSW * h:HSW * h + HSW], start=True, stop=True)
                    ins.then_inc(gates, 1)
            pe.wait_ge(gelu_out, N_IN - N_ALT)
            pe.wait_ge(mod78_made, N_ALT)
            for j in range(10):
                if j >= 4:
                    pe.wait_ge(vt_lo, j - 3)
                for t in range(HPAIRS):
                    if j < 8:
                        k0 = ROWS * KSTART[j // 2] + P * (j % 2)
                        src = V[:, t, k0:k0 + P]
                    else:
                        src = V[:, t, LAT + (j - 8) * P:LAT + (j - 7) * P]
                    ins = nc.tensor.transpose(PS[:, j % 4, t * P:t * P + P], src, IDENT[:, :])
                ins.then_inc(vt, 1)
            pe.wait_ge(x_sig, 2 * RC)
            grow(1, 1, 6, ONES5, DIAG5, 2)
            pe.wait_ge(x_sig, 2 * RC)
            pe.wait_ge(vt_lo, 10)
            with pe.Fori(0, HPAIRS // 2, 1) as i:
                ub = i * (2 * UNITS)

                def score(u):
                    e, b, h = u // UNITS, u % UNITS // 2, u % 2
                    ph = slice(DH * h, DH * h + DH)
                    if u % UNITS == 0:
                        pe.wait_ge(qk_made, i * 2 + e + 1)
                    if u >= 2:
                        pe.wait_ge(exps, ub + u - 1)
                    q = slice(b * P, b * P + P)
                    for dst, keys in ((0, slice(ROWS * KSTART[b], ROWS * KSTART[b] + LOCK)), (LOCK, slice(LAT, TOK))):
                        n = keys.stop - keys.start
                        ins = three(PS[:, u % 2, dst:dst + n], QH[e][ph, q], QL[e][ph, q], KH[e][ph, keys],
                                    KL[e][ph, keys], True, True)
                    ins.then_inc(scores, 1)

                def weighted_sum(u):
                    e, b, h = u // UNITS, u % UNITS // 2, u % 2
                    pe.wait_ge(pt_lo, ub + u + 1)
                    if u >= 2:
                        pe.wait_ge(on_made, ub + u - 1)
                    for j in range(4):
                        r = 2 * b + j if j < 2 else 6 + j
                        off = i * (2 * P) + P * e + DH * h
                        k = slice(j * P, j * P + P)
                        ins = three(PS[:, 4 + h, DH * b:DH * b + DH], PTH[:, u % 2, k], PTL[:, u % 2, k],
                                    v_hi(r, bass.ds(off, DH)), v_lo(r, off, DH), j == 0, j == 3)
                    ins.then_inc(pv, 1)

                def turn_output(e):
                    pe.wait_ge(on_made, ub + UNITS * (e + 1))
                    if e == 0:
                        pe.wait_ge(grow_made, 2)
                    if e == 1:
                        pe.wait_ge(ya_lo, i * 2 + 1)
                    for b in range(NBLK):
                        ins = nc.tensor.transpose(PS[:, 6 + e, b * P:b * P + P], ON[:, b, :], IDENT[:, :])
                    ins.then_inc(ot, 1)

                score(0)
                score(1)
                for u in range(2 * UNITS):
                    pe.wait_ge(exps, ub + u + 1)
                    for j in range(4):
                        ins = nc.tensor.transpose(PS[:, 2 + u % 2, j * P:j * P + P], PR[:, u % 2, j * P:j * P + P],
                                                  IDENT[:, :])
                    ins.then_inc(pt_ps, 1)
                    if u + 2 < 2 * UNITS:
                        score(u + 2)
                    if u == UNITS + 1:
                        turn_output(0)
                    if u:
                        weighted_sum(u - 1)
                weighted_sum(2 * UNITS - 1)
                turn_output(1)
            pe.wait_ge(yr_lo, RC)
            for k in range(4):
                s, u = mix_use(T_OUT + k)
                pe.wait_ge(lo_made[s], u - RAW[s] + 1)
                for j in range(8):
                    t, half = j // 2, j % 2
                    if k == 0 and j >= 6:
                        pe.wait_ge(ya_lo, HPAIRS - 7 + j)
                    tk = slice(t * P, t * P + P)
                    col = slice(half * HALF_D, half * HALF_D + HALF_D)
                    ins = three(PS[:, j, :], YRH[k][:, tk], YRL[k][:, tk], WH[:, s, col], WL[:, s, col], k == 0, False)
                ins.then_inc(used[s], 1)
            for t in range(NLT):
                tk = slice(t * P, t * P + P)
                for half in range(2):
                    col = slice(half * HALF_D, half * HALF_D + HALF_D)
                    for k in range(4):
                        s, u = mix_use(T_OUT + 4 + k)
                        if t == 0 and half == 0:
                            pe.wait_ge(lo_made[s], u - RAW[s] + 1)
                        ins = three(PS[:, 2 * t + half, :], YAH[:, k, tk], YAL[:, k, tk], WH[:, s, col], WL[:, s, col],
                                    False, k == 3)
                ins.then_inc(wo_done, 1)
            pe.wait_ge(wo_done, NLT)
            for k in range(4):
                pe.nop().then_inc(used[mix_use(T_OUT + 4 + k)[0]], 1)
            turn(2, range(KC))
            ffn(1, U_FFN2, B2, A2, D2)

        @block.vector
        def _(dve):
            own = [0]

            def after_own(ins):
                own[0] += 1
                ins.then_inc(dve_own, 1)
                dve.wait_ge(dve_own, own[0])

            def a_columns(n):
                g = C1[:, R_PRE + KC * n:R_PRE + KC * n + KC].unsqueeze(2).broadcast_to([P, KC, 2])
                nc.vector.scalar_tensor_tensor(out=APRE[:, :, :], in0=MOD[:, 24 * n + 8:24 * n + 16, :], scalar=1.0,
                                               in1=g, op0=ALU.add, op1=ALU.mult).then_inc(a_made, 1)

            def diagonal(n, streams, diag, res_w):
                g = C2[:, R_POST + KC * n:R_POST + KC * n + KC].unsqueeze(2).broadcast_to([P, KC, 2])
                after_own(nc.vector.scalar_tensor_tensor(out=GCOL[:, :, :], in0=MOD[:, 24 * n + 16:24 * n + 24, :],
                                                         scalar=res_w, in1=g, op0=ALU.mult, op1=ALU.mult))
                for r in range(streams):
                    for k in range(KC):
                        ins = nc.vector.tensor_scalar(diag[:, r, k, :], IDENT[:, :], GCOL[:, k, r:r + 1], None, ALU.mult)
                ins.then_inc(diag_made, 1)

            def h_high(n):
                w = TOK if PRE_T[n] == NTT else LAT
                for k in range(KC + 1):
                    if k < KC:
                        dve.wait_ge(h_32, n * KC + k + 1)
                        nc.vector.tensor_copy(HH[:, k, 0:w], h32(n, k)[:, 0:w]).then_inc(h_hi, 1)
                    if k:
                        q = k - 1
                        dve.wait_ge(h_hi, n * KC + q + 1)
                        nc.vector.tensor_tensor(HL[:, q, 0:LAT], h32(n, q)[:, 0:LAT], HH[:, q, 0:LAT].bitcast(F32),
                                                ALU.subtract).then_inc(h_lo, 1)

            def ffn(n, uses, B, A):
                ntok, nj, cb, yb = ffn_counts(n)
                nh = len(token_halves(ntok))

                def times_u(r, cnt, bank):
                    dve.wait_ge(silu_made[r], cnt)
                    g = (A, B)[r][1]
                    dve.wait_ge(used[g], cnt + uses[g] - cb)
                    s = SG[:, r, 0:ntok].rearrange("p (h w) -> p h w", h=nh)
                    nc.vector.tensor_tensor(s, s, PS[:, bank:bank + nh, 0:ntok // nh], ALU.mult).then_inc(au_made[r], 1)
                    dve.wait_ge(a_hi[r], cnt)
                    nc.vector.tensor_tensor(AL[:, r, 0:ntok], SG[:, r, 0:ntok], AH[:, r, 0:ntok].bitcast(F32),
                                            ALU.subtract).then_inc(a_lo[r], 1)

                times_u(1, cb + 1, 2)
                times_u(0, cb + 1, 6)
                dve.wait_ge(y_zeroed, n + 1)
                def pair(i, last=False):
                    if n == 0:
                        for k in range(KC):
                            if k % 2 == 0:
                                dve.wait_ge(mod_in[(k // 2) % 2], i * 32 + 16 * (k // 4) + 16)
                            for r in range(2):
                                src = MRAW[:, (k // 2) % 2, k % 2, :]
                                if k == 0:
                                    ins = nc.vector.tensor_scalar(MACC[:, r, :], src, CS[:, 0, r:r + 1], None, ALU.mult)
                                else:
                                    dve.wait_ge(mod_own, i * 16 + 2 * k + r - 1)
                                    ins = nc.vector.scalar_tensor_tensor(
                                        out=MACC[:, r, :], in0=src, scalar=CS[:, k, r:r + 1], in1=MACC[:, r, :],
                                        op0=ALU.mult, op1=ALU.add)
                                ins.then_inc(mod_own, 1)
                        dve.wait_ge(mod_hi, i + 1)
                        nc.vector.tensor_tensor(ML[:, :, :], MACC[:, :, :], MH[:, :, :].bitcast(F32),
                                                ALU.subtract).then_inc(mod_lo, 1)
                        dve.wait_ge(mod_lo, i + 1)
                        dve.wait_ge(mod_red, i + 1)
                        bm = C1[:, bass.ds(i * 4 + 16 + R_BMOD, 4)].unsqueeze(2).broadcast_to([P, 4, 2])
                        nc.vector.tensor_tensor(MOD[:, bass.ds(i * 4 + 16, 4), :],
                                                PS[:, 7, 0:16].rearrange("p (m r a) -> p m r a", r=2, a=2)[:, :, :, 0], bm,
                                                ALU.add).then_inc(mod_made, 1)
                    for j in range(nj):
                        dve.wait_ge(y_ready, i * nj + yb + j + 1)
                        y = y_acc(n, j // 2)[:, HALF_D * (j % 2):HALF_D * (j % 2) + HALF_D]
                        nc.vector.tensor_tensor(y, y, PS[:, 4 + j % 4, :], ALU.add).then_inc(y_added, 1)
                    times_u(1, i + cb + 2, 2)
                    if last:
                        dve.wait_ge(mod_made, PAIRS)
                        diagonal(0, 2, DIAG, 0.5)
                    times_u(0, i + cb + 2, 6)

                with dve.Fori(0, PAIRS - 1 if n == 0 else PAIRS, 1) as i:
                    pair(i)
                if n == 0:
                    pair(PAIRS - 1, True)

            def post(n):
                tiles = POST_T[n]
                yb = {0: PAIRS * 2 * NTT, 2: (PAIRS + 1) * 2 * NTT + PAIRS * 2 * NLT}.get(n)

                def rest(q):
                    dve.wait_ge(rstd_post, POST_N[n] + q + 1)
                    c0 = POST_C[n] + q
                    if n == 1:
                        yg = YX[:, NLT + q % 2, :]
                        dve.wait_ge(yg_dve, yg_b + q + 1)
                    else:
                        yg = YG[:, q % 2, :]
                        if q % 2 == 0:
                            dve.wait_ge(yg_pool, yg_pb + q // 2 + 1)
                        else:
                            dve.wait_ge(yg_dve, yg_b + q // 2 + 1)
                    x0 = YX[:, q, :]
                    if n == 0:
                        dve.wait_ge(xst_in[q % 2], 16 * (q // 2 + 1))
                        x0 = XST[:, q % 2, :]
                    nc.vector.scalar_tensor_tensor(out=YX[:, q, :], in0=yg, scalar=RS[:, c0:c0 + 1], in1=x0, op0=ALU.mult,
                                                   op1=ALU.add).then_inc(resid, 1)

                yg_b, yg_pb = (0, NTT // 2, NTT // 2 + NLT)[n], (0, 0, NTT // 2)[n]
                for t in range(tiles):
                    if n == 1:
                        if t == 0:
                            dve.wait_ge(grow5_made, 1)
                        if t >= 2:
                            dve.wait_ge(resid, POST_N[n] + t - 1)
                        dve.wait_ge(sq_post, POST_N[n] + t + 1)
                        nc.vector.tensor_tensor(YX[:, NLT + t % 2, :], PS[:, 2 * t:2 * t + 2, :].rearrange("p a n -> p (a n)"),
                                                GROW5[:, :], ALU.mult).then_inc(yg_dve, 1)
                        rest(t)
                        continue
                    dve.wait_ge(y_ready, yb + 2 * t + 2)
                    b = 4 + 2 * (t % 2)
                    y = y_acc(n // 2, t)
                    y2 = y.rearrange("p (a n) -> p a n", a=2)
                    nc.vector.tensor_tensor(y2, y2, PS[:, b:b + 2, :], ALU.add).then_inc(ysum, 1)
                    if t % 2 == 1:
                        if t >= 3:
                            dve.wait_ge(resid, POST_N[n] + t - 1)
                        else:
                            dve.wait_ge(grow_made, n + 1)
                        dve.wait_ge(ysum, t + 1 + (NTT if n == 2 else 0))
                        nc.vector.tensor_tensor(YG[:, 1, :], y, GROW[:, 0 if t < NLT else 1, :], ALU.mult).then_inc(yg_dve, 1)
                    if t >= 1:
                        rest(t - 1)
                if n != 1:
                    rest(tiles - 1)

            dve.wait_ge(used[M01[-1]], U_FFN1[M01[-1]])
            nc.vector.tensor_copy(MROW[0:2, D:2 * D].rearrange("p (a n) -> p a n", a=2), PS[0:2, 6:8, :]).then_inc(mrow_dve, 1)
            dve.wait_ge(rows_turned, 1)
            nc.vector.tensor_copy(C1[:, :], PS[:, 2, 0:N_R1]).then_inc(c1_made, 1)
            nc.vector.tensor_copy(C2[:, :], PS[:, 3, 0:N_R2]).then_inc(c2_made, 1)
            dve.wait_ge(c1_made, 1)
            dve.wait_ge(mod01_turned, 1)
            nc.vector.tensor_tensor(MOD[:, 0:2 * KC, :], PS[:, 4, 0:4 * KC].rearrange("p (m a) -> p m a", a=2),
                                    C1[:, R_BMOD:R_BMOD + 2 * KC].unsqueeze(2).broadcast_to([P, 2 * KC, 2]),
                                    ALU.add).then_inc(mod01_made, 1)
            dve.wait_ge(mod01_made, 1)
            a_columns(0)
            h_high(0)
            dve.wait_ge(c2_made, 1)
            lam = C2[:, R_LAM:R_LAM + 8]
            neg, e, s1, s2, acc, mn = LT[:, 0, :], LT[:, 1, :], LT[:, 2, :], LT[:, 3, :], LT[:, 4, :], LT[:, 5, :]
            after_own(nc.vector.tensor_scalar(neg, lam, -1.0, None, ALU.mult))
            nc.vector.tensor_tensor(neg, neg, lam, ALU.max).then_inc(lam_abs, 1)
            dve.wait_ge(c4_hi, 1)
            nc.vector.tensor_tensor(C4[:, :, 1:4:2], CS[:, :, :],
                                    C4[:, :, 0:4:2].bitcast(F32), ALU.subtract).then_inc(c4_made, 1)
            dve.wait_ge(lam_exp, 1)
            after_own(nc.vector.tensor_scalar(s2, e, 2.0, None, ALU.add))
            after_own(nc.vector.reciprocal(s1, s2))
            after_own(nc.vector.tensor_tensor(s1, s1, e, ALU.mult))
            after_own(nc.vector.tensor_tensor(s2, s1, s1, ALU.mult))
            after_own(nc.vector.tensor_scalar(acc, s2, 1.0 / 19, None, ALU.mult))
            for d in (17, 15, 13, 11, 9, 7, 5, 3):
                after_own(nc.vector.scalar_tensor_tensor(out=acc, in0=acc, scalar=1.0 / d, in1=s2, op0=ALU.add, op1=ALU.mult))
            after_own(nc.vector.scalar_tensor_tensor(out=acc, in0=acc, scalar=1.0, in1=s1, op0=ALU.add, op1=ALU.mult))
            after_own(nc.vector.tensor_scalar(mn, lam, 0.0, LRU_C, ALU.min, ALU.mult))
            nc.vector.scalar_tensor_tensor(out=LOGC[:, :], in0=acc, scalar=-2.0 * LRU_C, in1=mn, op0=ALU.mult,
                                           op1=ALU.add).then_inc(logc_made, 1)
            ffn(0, U_FFN1, B1, A1)
            dve.wait_ge(h_32, KC)
            a_columns(1)
            post(0)
            h_high(1)

            M8 = MOD[:, 56:72, :]

            def project_out(n):
                s, u = mix_use(step_tile(n))
                dve.wait_ge(used[s], u + 1)
                g, t, b = n // 4, n % 4, 2 * (n % 2)
                if n == 0:
                    dve.wait_ge(pads_zeroed, 1)
                if g == 0:
                    nc.vector.tensor_copy(XR[:, t, 2:2 + LAT], PS[:, b, :])
                    ins = nc.vector.tensor_copy(XR[:, t, 2 + CTX0:2 + CTX0 + CTX], PS[:, b + 1, 0:CTX])
                elif g == 3:
                    ins = nc.vector.tensor_scalar(Q[:, t, :].rearrange("p (c r) -> p r c", r=ROWS),
                                                  PS[:, b, :].rearrange("p (r c) -> p r c", r=ROWS), DH ** -0.5, None,
                                                  ALU.mult)
                else:
                    dst = (K, V)[g - 1]
                    ins = nc.vector.tensor_copy(dst[:, t, 0:LAT].rearrange("p (c r) -> p r c", r=ROWS),
                                                PS[:, b, :].rearrange("p (r c) -> p r c", r=ROWS))
                    ins = nc.vector.tensor_copy(dst[:, t, LAT:TOK], PS[:, b + 1, 0:CTX])
                ins.then_inc(proj_out, 1)

            def mod78_add(n):
                s, u = mix_use(step_tile(n) + 1)
                dve.wait_ge(used[s], u + 1)
                m = M8[:, (n % 2) * KC:(n % 2) * KC + KC, :]
                p4 = PS[:, 7, 0:32].rearrange("p (m a h) -> p m a h", a=2, h=2)
                if n < 2:
                    bm = C1[:, R_BMOD + 56 + (n % 2) * KC:R_BMOD + 56 + (n % 2) * KC + KC].unsqueeze(2)
                    after_own(nc.vector.tensor_tensor(m, p4[:, :, :, 0], bm.broadcast_to([P, KC, 2]), ALU.add))
                else:
                    after_own(nc.vector.tensor_tensor(m, p4[:, :, :, 0], m, ALU.add))
                nc.vector.tensor_tensor(m, p4[:, :, :, 1], m, ALU.add).then_inc(mod78_made, 1)
                dve.wait_ge(mod78_made, n + 1)

            def conv(cc):
                w = [C2[:, R_CW + 4 * j + cc:R_CW + 4 * j + cc + 1] for j in range(4)]
                if cc:
                    dve.wait_ge(gates, 2 * cc)
                dve.wait_ge(proj_out, cc + 1)
                after_own(nc.vector.tensor_scalar(XC[:, :], XR[:, cc, 0:SCANW], w[0], C2[:, R_CB + cc:R_CB + cc + 1],
                                                  ALU.mult, ALU.add))
                for j in range(1, 4):
                    ins = nc.vector.scalar_tensor_tensor(out=XC[:, :], in0=XR[:, cc, j:j + SCANW], scalar=w[j],
                                                         in1=XC[:, :], op0=ALU.mult, op1=ALU.add)
                    if j < 3:
                        after_own(ins)
                ins.then_inc(xc_made, 1)

            def rec_unit(r):
                cc, d = r // 2, r % 2
                y = XR[:, cc, 2:2 + LAT]
                r1, a, u, hs = T[:, 1, :], T[:, 2, :], T[:, 0, :], T[:, 1, :]
                dve.wait_ge(xc_made, cc + 1)
                dve.wait_ge(x_sig, r + 1)
                after_own(nc.vector.tensor_tensor(r1, r1, XC[:, :], ALU.mult))
                dve.wait_ge(r_at, r + 1)
                after_own(nc.vector.tensor_tensor(u, a, a, ALU.mult))
                nc.vector.scalar_tensor_tensor(out=u, in0=u, scalar=1.0, in1=T3[:, :], op0=ALU.add,
                                               op1=ALU.mult).then_inc(om_made, 1)
                dve.wait_ge(root, r + 1)
                after_own(nc.vector.tensor_tensor(u, u, r1, ALU.mult))

                def part(t, lo, n):
                    v = t[:, lo:lo + n]
                    return v if d == 0 else v[:, ::-1]

                last = CTX0 + (CTX - 1 if d == 0 else 0)
                after_own(nc.vector.tensor_tensor_scan(part(hs, CTX0, CTX), part(a, CTX0, CTX), part(u, CTX0, CTX), 0.0,
                                                       ALU.mult, ALU.add))
                if d == 0:
                    nc.vector.tensor_tensor_scan(y, a[:, 0:LAT], u[:, 0:LAT], hs[:, last:last + 1],
                                                 ALU.mult, ALU.add).then_inc(scanned, 1)
                else:
                    after_own(nc.vector.tensor_tensor_scan(part(hs, 0, LAT), part(a, 0, LAT), part(u, 0, LAT),
                                                           hs[:, last:last + 1], ALU.mult, ALU.add))
                    dve.wait_ge(scanned, r)
                    nc.vector.tensor_tensor(y, y, hs[:, 0:LAT], ALU.add).then_inc(scanned, 1)

            for n in range(N_ALT):
                project_out(n)
                mod78_add(n)
                if n == 0:
                    conv(0)
                if n in REC_STEP:
                    r = REC_STEP[n]
                    rec_unit(r)
                    if r % 2 == 1 and r < 7:
                        conv(r // 2 + 1)
            diagonal(1, 1, DIAG5, 1.0)
            dve.wait_ge(h_32, 2 * KC)
            a_columns(2)
            dve.wait_ge(scanned, 2 * RC)
            for j in range(RC):
                y = XR[:, j, 2:2 + LAT]
                dve.wait_ge(gelu_out, j + 1)
                nc.vector.tensor_tensor(y, y, GR[:, j, :], ALU.mult).then_inc(yr_f, 1)
            for j in range(10):
                if j == 8:
                    s, u = mix_use(T_OUT)
                    dve.wait_ge(lo_made[s], u - RAW[s] + 1)
                dve.wait_ge(vt_hi, j + 1)
                nc.vector.tensor_tensor(v_lo(j, 0, LAT), PS[:, j % 4, :], v_hi(j, slice(0, LAT)).bitcast(F32),
                                        ALU.subtract).then_inc(vt_lo, 1)
            dve.wait_ge(bias_made, 3)
            s, u = mix_use(T_OUT + 1)
            dve.wait_ge(lo_made[s], u - RAW[s] + 1)
            with dve.Fori(0, HPAIRS // 2, 1) as i:
                ub = i * (2 * UNITS)

                def row_max(u):
                    e, b, h = u // UNITS, u % UNITS // 2, u % 2
                    dve.wait_ge(scores, ub + u + 1)
                    if b in (0, 3):
                        bias = (BIAS0 if b == 0 else BIAS3)[:, bass.ds(i * 4 + 2 * e + h, 1), :].rearrange("p a n -> p (a n)")
                    else:
                        bias = BIASM[:, bass.ds(i * 2 + e, 1), :].rearrange("p a n -> p (a n)")[:, LOCK * h:LOCK * h + LOCK]
                    s = PS[:, u % 2, 0:LOCK].rearrange("p (x r) -> p x r", r=ROWS)
                    nc.vector.tensor_tensor(s, s, bias.rearrange("p (r x) -> p x r", r=ROWS), ALU.add).then_inc(biased, 1)
                    dve.wait_ge(biased, ub + u + 1)
                    c0 = u % UNITS
                    nc.vector.tensor_reduce(NMX[:, c0:c0 + 1], PS[:, u % 2, :], AX_X, ALU.max, negate=True).then_inc(maxed, 1)

                def transposed_lo(u):
                    dve.wait_ge(pt_hi, ub + u + 1)
                    nc.vector.tensor_tensor(PTL[:, u % 2, :], PS[:, 2 + u % 2, :], PTH[:, u % 2, :].bitcast(F32),
                                            ALU.subtract).then_inc(pt_lo, 1)

                def normed(u):
                    e, b, h = u // UNITS, u % UNITS // 2, u % 2
                    c0 = u % UNITS
                    dve.wait_ge(pv, ub + u + 1)
                    if u == UNITS:
                        dve.wait_ge(ot, i * 2 + 1)
                    nc.vector.reciprocal(RDEN[:, c0:c0 + 1], DEN[:, c0:c0 + 1]).then_inc(inverted, 1)
                    dve.wait_ge(inverted, ub + u + 1)
                    nc.vector.tensor_scalar(ON[:, b, DH * h:DH * h + DH], PS[:, 4 + h, DH * b:DH * b + DH],
                                            RDEN[:, c0:c0 + 1], None, ALU.mult).then_inc(on_made, 1)

                def output_lo(e):
                    dve.wait_ge(ya_hi, i * 2 + e + 1)
                    dve.wait_ge(grow5_made, 1)
                    ap = YAL[:, bass.ds(i * 2 + e, 1), :].rearrange("p a (r c) -> p (a c) r", r=ROWS)
                    hi = YAH[:, bass.ds(i * 2 + e, 1), :].rearrange("p a (r c) -> p (a c) r", r=ROWS).bitcast(F32)
                    nc.vector.tensor_tensor(ap, PS[:, 6 + e, :].rearrange("p (c r) -> p c r", r=ROWS), hi,
                                            ALU.subtract).then_inc(ya_lo, 1)

                row_max(0)
                row_max(1)
                for u in range(2 * UNITS):
                    transposed_lo(u)
                    if u + 2 < 2 * UNITS:
                        row_max(u + 2)
                    if u:
                        normed(u - 1)
                    if u == UNITS + 2:
                        output_lo(0)
                normed(2 * UNITS - 1)
                output_lo(1)
            post(1)
            h_high(2)
            diagonal(2, 1, DIAG2, 0.5)
            ffn(1, U_FFN2, B2, A2)
            post(2)


_INS = ["x", "c", "ctx", "c_ctx", "w_mod", "b_mod", "norm_pre", "norm_post", "ffn1_w_gu", "ffn1_w_down", "ffn2_w_gu",
        "ffn2_w_down", "w_in", "w_out", "conv_w", "conv_b", "lru_wa", "lru_ba", "lru_wx", "lru_bx", "lru_lambda",
        "na_rpb"]


def kernel(**inputs):
    import numpy as _np
    import concourse.bacc as _bacc
    from concourse import mybir as _mybir
    from concourse.bass_utils import run_bass_kernel_spmd as _run

    nc = _bacc.Bacc("TRN2", target_bir_lowering=False, num_devices=1)
    arrays, args = {}, []
    for name in _INS:
        a = _np.ascontiguousarray(inputs[name])
        arrays[f"in_{name}"] = a
        args.append(nc.dram_tensor(f"in_{name}", a.shape, _mybir.dt.from_np(a.dtype), kind="ExternalInput").ap())
    args.append(nc.dram_tensor("out_dram", (1, LAT, D), _mybir.dt.float32, kind="ExternalOutput").ap())
    build(nc, *args)
    r = _run(nc, [arrays], core_ids=[0])
    return r.results[0]["out_dram"]
```

```python
from contextlib import ExitStack

import concourse.bass as bass
from concourse import mybir

F32 = mybir.dt.float32
F32R = mybir.dt.float32r
ALU = mybir.AluOpType
ACT = mybir.ActivationFunctionType
AX_X = mybir.AxisListType.X

P = 128
D = 1024
KC = D // P
HALF_D = D // 2
LAT, CTX = 512, 256
TOK = LAT + CTX
NLT, NCT = LAT // P, CTX // P
NTT = NLT + NCT
FF = 2816
FC = FF // P
PAIRS = FC // 2 - 1
REC = 512
RC = REC // P
GRID_W, ROWS = 64, 8
NH, DH = 8, 64
HPAIRS = NH // 2
QCOLS = 16
KCOLS = 32
NBLK = GRID_W // QCOLS
KSTART = [0, 8, 24, 32]
LOCK = ROWS * KCOLS
UNITS = 2 * NBLK
RPB_R, RPB_C = 15, 31
NEG = -1e30
EPS = 1e-6
LRU_C = 8.0
SLOTS = 6
PADW = 776
SCANW = 772
HSW = SCANW // 2
CTX0 = LAT + 3

R_C, R_CC, R_BMOD, R_PRE, N_R1 = 0, 8, 16, 88, 112
R_POST, R_CW, R_CB, R_BA, R_BX, R_LAM, N_R2 = 0, 24, 40, 44, 52, 60, 68

NM01 = 2 * KC
M01 = (2, 3, 0, 1, 4, 5) + (4, 5, 0, 1) * 2 + (4, 5)
B1, A1, D1 = (2, 3), (0, 1), (4, 5)
MIX = (2, 3, 0, 1, 4, 5) * 3 + (0, 1) + (2, 3, 0, 1, 4, 5, 2, 3)
B2, A2, D2 = (0, 1), (4, 5), (2, 3)

N_XKVQ, N_IN, N_OUT = 16, 20, 8
T_OUT = N_IN
N_MIX = T_OUT + N_OUT
MOD_GROUPS = 8
MOD_CHUNKS = 7 * KC // MOD_GROUPS
MOD_COLS = MOD_CHUNKS * P
GROUPS = [0, 3, 4, 2, 1]
REC_STEP = {1: 0, 2: 1, 4: 2, 5: 3, 7: 4, 8: 5, 10: 6, 11: 7}


def slot_uses():
    u = [0] * SLOTS
    for s in M01:
        u[s] += 1
    ffn1 = list(u)
    for s in B1 + A1 + D1:
        u[s] += FC // 2
    mix = list(u)
    for s in MIX:
        u[s] += 1
    return ffn1, mix, u


U_FFN1, U_MIX, U_FFN2 = slot_uses()
RAW = U_FFN1


def mix_use(n):
    return MIX[n], U_MIX[MIX[n]] + MIX[:n].count(MIX[n])


def known(v):
    return isinstance(v, int)


def build(nc, x, c, ctx_in, c_ctx, w_mod, b_mod, norm_pre, norm_post, w_gu1, w_dn1, w_gu2, w_dn2,
          w_in, w_out, conv_w, conv_b, lru_wa, lru_ba, lru_wx, lru_bx, lru_lambda, rpb, out):
    x_t = x.rearrange("b (t p) d -> (b t) p d", p=P)
    ctx_t = ctx_in.rearrange("b (t p) d -> (b t) p d", p=P)
    out_t = out.rearrange("b (t p) d -> (b t) p d", p=P)

    def row_blocks(w):
        return w.rearrange("l (k p) n -> (l k) p n", p=P)

    def col_range(w):
        return w.rearrange("l (k p) n -> p (l k) n", p=P)

    rpb_rows = nc.dram_tensor("rpb_rows", (ROWS, NH, ROWS, GRID_W), F32, kind="Internal").ap()
    rpb_full = nc.dram_tensor("rpb_full", (3, P, NH, LOCK), F32, kind="Internal").ap()

    with ExitStack() as ctx:
        base = 16512
        ctx.enter_context(nc.sbuf_tensor("fence", [P, (229344 - base) // 4], F32))

        def at(name, off, shape, dt=F32):
            return nc.alloc_sbuf_tensor_at(name, shape, dt, offset=base + off)

        YX_O = 0
        HH_O = YX_O + 4 * NTT * D
        HL_O = HH_O + 4 * KC * TOK
        W_O = HL_O + 4 * KC * TOK
        M_O = W_O + 3 * SLOTS * 4 * D
        S_O = M_O + 62656
        YX = at("YX", YX_O, [P, NTT, D])
        HH = at("HH", HH_O, [P, KC, TOK], F32R)
        HL = at("HL", HL_O, [P, KC, TOK], F32R)
        WR = at("WR", W_O, [P, SLOTS, D])
        WH = at("WH", W_O + SLOTS * 4 * D, [P, SLOTS, D], F32R)
        WL = at("WL", W_O + 2 * SLOTS * 4 * D, [P, SLOTS, D], F32R)
        R1 = at("R1", M_O, [P, P])
        R2 = at("R2", M_O + 512, [P, P])
        ZERO = at("ZERO", M_O + 1024, [P, 256])
        LT = at("LT", M_O + 2048, [P, 6, 8])
        AH = at("AH", M_O, [P, 2, TOK], F32R)
        AL = at("AL", M_O + 6144, [P, 2, TOK], F32R)
        SG = at("SG", M_O + 12288, [P, 2, TOK])
        H32 = at("H32", M_O + 6144, [P, 4, TOK])
        JUNK = at("JUNK", M_O + 12288, [P, D])
        MROW = at("MROW", M_O + 47104, [P, 2 * D])
        MRAW = at("MRAW", M_O + 18432, [P, 2, 2, MOD_COLS])
        MACC = at("MACC", M_O + 32768, [P, 2, MOD_COLS])
        MH = at("MH", M_O + 39936, [P, 2, MOD_COLS], F32R)
        ML = at("ML", M_O + 47104, [P, 2, MOD_COLS], F32R)
        DIAG = at("DIAG", M_O + 18432, [P, 2, KC, P])
        XST = at("XST", M_O + 30720, [P, 2, D])
        GROW = at("GROW", M_O + 38912, [P, 2, D])
        YG = at("YG", M_O + 47104, [P, 2, D])
        DG = at("DG", M_O + 55296, [P, NTT, P])
        ONES = at("ONES", M_O + 59392, [P, P])
        Y2 = at("Y2", M_O + 18432, [P, NLT, D])
        DIAG2 = at("DIAG2", M_O + 55296, [P, 1, KC, P])
        XR = at("XR", M_O, [P, RC, PADW])
        T = at("T", M_O + 12416, [P, 3, SCANW])
        Q = at("Q", M_O + 21696, [P, HPAIRS, LAT])
        K = at("K", M_O + 29888, [P, HPAIRS, TOK])
        V = at("V", M_O + 42176, [P, HPAIRS, TOK])
        GR = at("GR", M_O + 54464, [P, RC, LAT])
        XC = at("XC", M_O + 54464, [P, SCANW])
        T3 = at("T3", M_O + 54464 + 3104, [P, SCANW])
        GW = at("GW", YX_O + 4 * NLT * D, [P, 2, 2, RC, P])
        HHf = at("HHf", HH_O, [P, KC, TOK])
        HLf = at("HLf", HL_O, [P, KC, TOK])
        VCL = at("VCL", W_O + 2 * 4 * D, [P, 2, LAT], F32R)

        def v_hi(j, cols):
            return HH[:, j, cols] if j < 8 else HL[:, j - 8, cols]

        def v_lo(j, cols):
            if j >= 8:
                return VCL[:, j - 8, cols]
            o = LAT * (j % 2)
            return (WH, WL)[j // 4][:, 4 + (j % 4) // 2, o + cols.start:o + cols.stop]

        BIAS3 = HHf[:, :, LAT:TOK]
        BIAS0 = HLf[:, :, LAT:TOK]
        BIASM = HLf[:, 2:6, 0:LAT]
        YR6 = at("YR6", M_O + 42176, [P, 6, LAT], F32R)
        YR7 = [at(f"YR7_{j}", HL_O + 4 * TOK * (6 + j), [P, LAT], F32R) for j in range(2)]
        YRH = [YR6[:, j, :] for j in range(4)]
        YRL = [YR6[:, 4, :], YR6[:, 5, :], YR7[0][:, :], YR7[1][:, :]]
        YAH = at("YAH", M_O, [P, HPAIRS, LAT], F32R)
        YAL = at("YAL", M_O + 54464, [P, HPAIRS, LAT], F32R)
        GROW5T = at("GROW5T", M_O + 54464 + 4096, [P, D])
        GROW5 = at("GROW5", M_O + 8192, [P, D])
        DIAG5 = at("DIAG5", M_O + 12416, [P, 1, KC, P])
        PR = at("PR", M_O + 12416, [P, 2, LOCK + CTX])
        PTH = WH[:, 0:2, :].rearrange("p s (a n) -> p (s a) n", a=2)
        PTL = WL[:, 0:2, :].rearrange("p s (a n) -> p (s a) n", a=2)
        JUNK5 = at("JUNK5", M_O + 16512, [P, D])
        ONES5 = at("ONES5", M_O + 20608, [P, P])
        MASK = at("MASK", M_O + 21120, [P, 3, KCOLS])
        qk_at = [W_O + 4 * 4 * D, W_O]
        QH = [at(f"QH{e}", qk_at[e], [P, LAT], F32R) for e in range(2)]
        QL = [at(f"QL{e}", qk_at[e] + 2048, [P, LAT], F32R) for e in range(2)]
        KH = [at(f"KH{e}", qk_at[e] + 4096, [P, TOK], F32R) for e in range(2)]
        KL = [at(f"KL{e}", YX_O + 4 * NLT * D + 3072 * e, [P, TOK], F32R) for e in range(2)]
        DG5 = at("DG5", M_O + 34816, [P, NLT, P])
        H5 = at("H5", M_O + 38080, [P, 4, LAT])
        so = [S_O]

        def small(name, shape, dt=F32):
            t = at(name, so[0], shape, dt)
            n = 4
            for v in shape[1:]:
                n *= v
            so[0] += (n + 31) // 32 * 32
            assert base + so[0] <= 229344
            return t

        IDENT = small("IDENT", [P, P])
        MOD = small("MOD", [P, 72, 2])
        C1 = small("C1", [P, N_R1])
        C2 = small("C2", [P, N_R2])
        CS = small("CS", [P, KC, 2])
        APRE = small("APRE", [P, KC, 2])
        GCOL = small("GCOL", [P, KC, 2])
        LOGC = small("LOGC", [P, 8])
        SS = small("SS", [P, 32])
        MS = small("MS", [P, 8])
        RS = small("RS", [P, 32])
        MHALF = small("MHALF", [P, 1])
        ONESR = small("ONESR", [P, 2], F32R)
        NMX = small("NMX", [P, UNITS])
        DEN = small("DEN", [P, UNITS])
        RDEN = small("RDEN", [P, UNITS])

        PS = ctx.enter_context(nc.psum_tensor("PS", [P, 8, 512], F32))

        def sem(name):
            return ctx.enter_context(nc.semaphore(name))

        landed, hi_made, lo_made, used = ([sem(f"{n}{i}") for i in range(SLOTS)]
                                          for n in ("landed", "hi_made", "lo_made", "used"))
        x_in = [sem(f"x_in{i}") for i in range(NTT)]
        xst_in = [sem(f"xst_in{i}") for i in range(2)]
        mod_in = [sem(f"mod_in{i}") for i in range(2)]
        c_in, rows_in, rpb_zeroed, rpb_put, rpb_spread, bias_in, gw_in, stored = (sem(n) for n in (
            "c_in", "rows_in", "rpb_zeroed", "rpb_put", "rpb_spread", "bias_in", "gw_in", "stored"))
        zero_set, ident_set, mhalf_set, y_zeroed, gw_zeroed, pads_zeroed, ones_set = (sem(n) for n in (
            "zero_set", "ident_set", "mhalf_set", "y_zeroed", "gw_zeroed", "pads_zeroed", "ones_set"))
        c_turned, rows_turned, c1_made, c2_made, cs_made, lam_abs, lam_exp, logc_made = (sem(n) for n in (
            "c_turned", "rows_turned", "c1_made", "c2_made", "cs_made", "lam_abs", "lam_exp", "logc_made"))
        mrow_act, mrow_dve, mod01_turned, mod01_made, a_made, mod_own, mod_hi, mod_lo, mod_red, mod_made = (
            sem(n) for n in ("mrow_act", "mrow_dve", "mod01_turned", "mod01_made", "a_made", "mod_own", "mod_hi",
                             "mod_lo", "mod_red", "mod_made"))
        sq_pre, sq_post, rstd_pre, rstd_post, pool_own, dve_own = (sem(n) for n in (
            "sq_pre", "sq_post", "rstd_pre", "rstd_post", "pool_own", "dve_own"))
        dg_made, turned, h_hi, h_32, h_lo, h_lo_c = (sem(n) for n in (
            "dg_made", "turned", "h_hi", "h_32", "h_lo", "h_lo_c"))
        silu_made, au_made, a_hi, a_lo = ([sem(f"{n}{r}") for r in range(2)] for n in (
            "silu_made", "au_made", "a_hi", "a_lo"))
        y_ready, y_added, diag_made, grow_ps, grow_made, ysum, yg_pool, yg_dve, resid, onesr_set = (sem(n) for n in (
            "y_ready", "y_added", "diag_made", "grow_ps", "grow_made", "ysum", "yg_pool", "yg_dve", "resid",
            "onesr_set"))
        proj_out, gelu_out, xc_made, gates, r_sig, x_sig, r_at, om_made, root, scanned = (sem(n) for n in (
            "proj_out", "gelu_out", "xc_made", "gates", "r_sig", "x_sig", "r_at", "om_made", "root", "scanned"))
        vt, vt_hi, vt_lo, biasm_in, bias_made, yr_f, yr_hi, yr_lo = (sem(n) for n in (
            "vt", "vt_hi", "vt_lo", "biasm_in", "bias_made", "yr_f", "yr_hi", "yr_lo"))
        qk_hi, qk_made, scores, biased, maxed, exps, pt_ps, pt_hi, pt_lo, pv, inverted, p_made, ya_hi, ya_lo = (
            sem(n) for n in ("qk_hi", "qk_made", "scores", "biased", "maxed", "exps", "pt_ps", "pt_hi", "pt_lo", "pv",
                             "inverted", "p_made", "ya_hi", "ya_lo"))
        wo_done, grow5_made = sem("wo_done"), sem("grow5_made")

        PRE_T, POST_T = [NTT, NTT, NLT], [NTT, NLT, NLT]
        PRE_C, POST_C = [0, 12, 22], [6, 18, 26]
        PRE_N, POST_N = [0, NTT, 2 * NTT], [0, NTT, NTT + NLT]

        def dg(n):
            return DG5 if n == 2 else DG

        def h32(n, k):
            return H32[:, k % 4, :] if n < 2 else H5[:, k % 4, :]

        def y_acc(n, t):
            return YX[:, t, :] if n == 0 else Y2[:, t, :]

        def ffn_counts(n):
            ntok = TOK if n == 0 else LAT
            return ntok, 2 * ntok // P, n * (FC // 2), n * (PAIRS + 1) * 2 * NTT

        def added_before(n):
            return n * PAIRS * 2 * NTT

        def token_halves(ntok):
            w = 384 if ntok == TOK else 512
            return [(j, slice(w * j, w * j + w), w) for j in range(ntok // w)]

        block = ctx.enter_context(nc.Block())

        NU = HPAIRS * UNITS

        def heads_out(bank, ph, h):
            v = PS[ph, bank:bank + 2, :].rearrange("p a n -> p (a n)")
            return v.rearrange("p (b h q r) -> p b h q r", h=2, q=QCOLS, r=ROWS)[:, :, h]

        def by_tokens(dst, ph, p):
            return dst[ph, p, :].rearrange("p (r b q) -> p b q r", r=ROWS, q=QCOLS)

        @block.sync
        def _(sp):
            def load(s, u, src):
                if not known(u) or u > RAW[s]:
                    sp.wait_ge(lo_made[s], u - RAW[s])
                elif u:
                    sp.wait_ge(used[s], u)
                dst = WR[:, s, :]
                if len(src.shape) == 3:
                    dst = dst.rearrange("p (k n) -> p k n", n=src.shape[2])
                sp.dma_start(dst, src).then_inc(landed[s], 16)

            def ds(off, n):
                return slice(off, off + n) if known(off) else bass.ds(off, n)

            def at_cols(w, off, n):
                return col_range(w)[:, :, off:off + n] if known(off) else col_range(w)[:, :, bass.ds(off, n)]

            def mix_load(t):
                s, u = mix_use(t)
                if t < T_OUT:
                    src = at_cols(w_in, GROUPS[t // 4] * 512 + (t % 4) * P, P)
                else:
                    src = row_blocks(w_out)[t - T_OUT]
                load(s, u, src)

            def ffn_loads(n, w_gu, w_dn, uses, B, A, Dn):
                def up(slots, use, chunk):
                    for g in range(2):
                        load(slots[g], uses[slots[g]] + use, at_cols(w_gu, chunk * P + g * FF, P))

                def down(use, first):
                    for j in range(2):
                        r = first + j
                        src = row_blocks(w_dn)[r] if known(r) else \
                            row_blocks(w_dn)[bass.ds(r, 1)].rearrange("a p n -> p (a n)")
                        load(Dn[j], uses[Dn[j]] + use, src)

                def mod_load(i, q):
                    src = at_cols(w_mod, i * MOD_COLS + 2 * D, MOD_COLS)[:, 2 * q:2 * q + 2, :]
                    sp.dma_start(MRAW[:, q % 2, :, :], src).then_inc(mod_in[q % 2], 16)

                up(B, 0, 0)
                up(A, 0, 1)
                up(B, 1, 2)
                down(0, 0)
                up(A, 1, 3)
                if n == 0:
                    mod_load(0, 0)
                    mod_load(0, 1)

                def pair(i, last, mod=False, next_mod=False):
                    if not last:
                        up(B, i + 2, i * 2 + 4)
                    elif n == 0:
                        mix_load(0)
                        mix_load(1)
                    down(i + 1, i * 2 + 2)
                    if not last:
                        up(A, i + 2, i * 2 + 5)
                    elif n == 0:
                        mix_load(2)
                        mix_load(3)
                    if mod:
                        for q in (2, 3):
                            sp.wait_ge(mod_own, i * 16 + 4 * q - 4)
                            mod_load(i, q)
                        if next_mod:
                            for q in (0, 1):
                                sp.wait_ge(mod_own, i * 16 + 4 * q + 12)
                                mod_load(i + 1, q)
                    if mod:
                        spread_bias(i)

                first = MOD_GROUPS if n == 0 else 0
                if n == 0:
                    with sp.Fori(0, MOD_GROUPS - 1, 1) as i:
                        pair(i, False, True, True)
                    pair(MOD_GROUPS - 1, False, True)
                with sp.Fori(first, PAIRS - 1, 1) as i:
                    pair(i, False)
                pair(PAIRS - 1, True)

            def spread_bias(i):
                sp.wait_ge(rpb_put, 16 * ROWS)
                for v, first in ((0, 31), (1, 23), (2, 15)):
                    for e in range(QCOLS // MOD_GROUPS):
                        src = rpb_rows[:, :, :, ds(i * -2 + first - e, KCOLS)].rearrange("q h r x -> q (h r) x")
                        dst = rpb_full[v, ds(i * 16 + 8 * e, 8)].rearrange("q h (r x) -> q (h r) x", x=KCOLS)
                        sp.dma_start(dst, src).then_inc(rpb_spread, 16)

            sp.dma_start(R1[R_C:R_C + KC, :], c.rearrange("l (r p) -> (l r) p", p=P)).then_inc(c_in, 16)
            sp.dma_start(R1[R_CC:R_CC + KC, :], c_ctx.rearrange("(r p) -> r p", p=P)).then_inc(c_in, 16)
            for n in range(NM01):
                load(M01[n], M01[:n].count(M01[n]), row_blocks(w_mod)[n // 2][:, (n % 2) * D:(n % 2 + 1) * D])
            ffn_loads(0, w_gu1, w_dn1, U_FFN1, B1, A1, D1)
            sp.wait_ge(mod_red, MOD_GROUPS)
            for t in range(NTT):
                if t >= 2:
                    sp.wait_ge(resid, t - 1)
                sp.dma_start(XST[:, t % 2, :], x_t[t] if t < NLT else ctx_t[t - NLT]).then_inc(xst_in[t % 2], 16)
                if t == 1:
                    mix_load(4)
                    mix_load(5)
            sp.wait_ge(gw_zeroed, 1)
            for g, w in ((0, lru_wa), (1, lru_wx)):
                src = w.rearrange("l d (c two) i j -> (l two) i (d c) j", two=2)
                for h in range(2):
                    dst = GW[DH * h:DH * h + DH, g].rearrange("p d c n -> p (d c) n")[:, :, DH * h:DH * h + DH]
                    sp.dma_start(dst, src[h]).then_inc(gw_in, 16)
            for t in range(6, T_OUT):
                mix_load(t)
            s, u = mix_use(11)
            sp.wait_ge(used[s], u + 1)
            sp.wait_ge(rpb_spread, 16 * 3 * QCOLS)
            sp.dma_start(BIAS0, rpb_full[0]).then_inc(bias_in, 16)
            sp.dma_start(BIAS3, rpb_full[2]).then_inc(bias_in, 16)
            for t in range(T_OUT, T_OUT + 2):
                mix_load(t)
            s, u = mix_use(N_IN - 1)
            sp.wait_ge(used[s], u + 1)
            sp.dma_start(BIASM, rpb_full[1].rearrange("p (a h) n -> p a (h n)", h=2)).then_inc(biasm_in, 16)
            sp.wait_ge(pv, NU // 2)
            for t in range(T_OUT + 2, N_MIX):
                mix_load(t)
            ffn_loads(1, w_gu2, w_dn2, U_FFN2, B2, A2, D2)
            for t in range(NLT):
                sp.wait_ge(resid, POST_N[2] + t + 1)
                sp.dma_start(out_t[t], YX[:, t, :]).then_inc(stored, 16)
            sp.wait_ge(stored, 16 * NLT)

        @block.scalar
        def _(act):
            def make_hi(s, u):
                act.wait_ge(landed[s], u * 16 + 16)
                if not (known(u) and u == 0):
                    act.wait_ge(used[s], u)
                nc.scalar.activation(WH[:, s, :], WR[:, s, :], ACT.Copy).then_inc(hi_made[s], 1)

            squares = []

            def square(src, junk, col, done):
                if squares:
                    act.wait_ge(squares[-1], squares.count(squares[-1]))
                squares.append(done)
                nc.scalar.activation(junk, src, ACT.Square, scale=D ** -0.5, accum_out=SS[:, col:col + 1]).then_inc(done, 1)

            def h_full(n):
                for k in range(KC):
                    b = 2 * (k % 4)
                    if k == 0:
                        act.wait_ge(a_made, n + 1)
                    act.wait_ge(turned, n * KC + k + 1)
                    if k >= 4:
                        act.wait_ge(h_lo, n * KC + k - 3)
                        if PRE_T[n] == NTT:
                            act.wait_ge(h_lo_c, n * KC + k - 3)
                    m = 24 * n + k
                    ins = nc.scalar.activation(h32(n, k)[:, 0:LAT], PS[:, b, 0:LAT], ACT.Identity,
                                               bias=MOD[:, m, 0:1], scale=APRE[:, k, 0:1])
                    if PRE_T[n] == NTT:
                        ins = nc.scalar.activation(h32(n, k)[:, LAT:TOK], PS[:, b + 1, 0:CTX], ACT.Identity,
                                                   bias=MOD[:, m, 1:2], scale=APRE[:, k, 1:2])
                    ins.then_inc(h_32, 1)

            def ffn(n, uses, B, A, Dn):
                ntok, nj, cb, yb = ffn_counts(n)
                nh = len(token_halves(ntok))

                def silu(r, cnt, bank):
                    g = (A, B)[r][0]
                    act.wait_ge(used[g], cnt + uses[g] - cb)
                    if not (known(cnt) and cnt == 1):
                        act.wait_ge(a_lo[r], cnt - 1)
                    nc.scalar.activation(SG[:, r, 0:ntok].rearrange("p (h w) -> p h w", h=nh),
                                         PS[:, bank:bank + nh, 0:ntok // nh], ACT.Silu).then_inc(silu_made[r], 1)

                def high(r, cnt):
                    act.wait_ge(au_made[r], cnt)
                    nc.scalar.activation(AH[:, r, 0:ntok], SG[:, r, 0:ntok], ACT.Copy).then_inc(a_hi[r], 1)

                def tiles(slots, use):
                    for s in slots:
                        make_hi(s, uses[s] + use)

                def pair(i, whole, mod=False):
                    silu(1, i + cb + 2, 0)
                    if whole:
                        tiles(B, i + 2)
                    act.wait_ge(y_ready, i * nj + yb + nj)
                    high(1, i + cb + 2)
                    tiles(Dn, i + 1)
                    if mod:
                        act.wait_ge(mod_own, i * 16 + 16)
                        nc.scalar.activation(MH[:, :, :], MACC[:, :, :], ACT.Copy).then_inc(mod_hi, 1)
                    silu(0, i + cb + 2, 4)
                    if whole:
                        tiles(A, i + 2)
                    high(0, i + cb + 2)

                silu(1, cb + 1, 0)
                tiles(B, 1)
                tiles(Dn, 0)
                high(1, cb + 1)
                silu(0, cb + 1, 4)
                tiles(A, 1)
                high(0, cb + 1)
                if n == 0:
                    with act.Fori(0, MOD_GROUPS, 1) as i:
                        pair(i, True, True)
                with act.Fori(MOD_GROUPS if n == 0 else 0, PAIRS if n == 0 else PAIRS - 1, 1) as i:
                    pair(i, True)
                if n == 1:
                    pair(PAIRS - 1, False)

            def grow_out(n, dsts):
                act.wait_ge(grow_ps, n + 1)
                for dst, bank in dsts:
                    ins = nc.scalar.activation(dst.rearrange("p (a n) -> p a n", a=2), PS[:, bank:bank + 2, :], ACT.Copy)
                ins.then_inc(grow_made, 1)

            def post_squares(n):
                for t in range(POST_T[n] + (n < 2)):
                    if t < POST_T[n]:
                        if n == 1:
                            act.wait_ge(wo_done, t + 1)
                            src = PS[:, 2 * t:2 * t + 2, :].rearrange("p a n -> p (a n)")
                        else:
                            act.wait_ge(ysum, t + 1 + (NTT if n == 2 else 0))
                            src = y_acc(n // 2, t)
                        square(src, JUNK5[:, :] if n == 1 else JUNK[:, :], POST_C[n] + t, sq_post)
                    if n < 2 and t >= 1:
                        act.wait_ge(resid, POST_N[n] + t)
                        square(YX[:, t - 1, :], JUNK5[:, :] if n == 1 else JUNK[:, :], PRE_C[n + 1] + t - 1, sq_pre)

            def load_rows(dst, r, n, src):
                act.dma_start(dst[r:r + n, :], src).then_inc(rows_in, 16)

            def rows128(a):
                return a.rearrange("l (r p) -> (l r) p", p=P) if len(a.shape) == 2 else \
                    a.rearrange("l m (r p) -> (l m r) p", p=P)

            def load_x(t):
                act.dma_start(YX[:, t, :], x_t[t] if t < NLT else ctx_t[t - NLT]).then_inc(x_in[t], 16)

            load_x(0)
            act.wait_ge(c_turned, 1)
            nc.scalar.activation(CS[:, :, :].rearrange("p k a -> p a k"), PS[:, 3, 0:16].rearrange("p (a k) -> p a k", a=2),
                                 ACT.Silu).then_inc(cs_made, 1)
            load_rows(R1, R_BMOD, 72, rows128(b_mod))
            load_rows(R1, R_PRE, 24, rows128(norm_pre))
            load_x(1)
            small_rows = [(R_POST, 24, norm_post), (R_CW, 16, conv_w), (R_CB, RC, conv_b), (R_BA, 8, lru_ba),
                          (R_BX, 8, lru_bx), (R_LAM, 8, lru_lambda)]
            for t in range(NTT):
                if t + 2 < NTT:
                    load_x(t + 2)
                r0, cnt, src = small_rows[t]
                load_rows(R2, r0, cnt, rows128(src))
                act.wait_ge(x_in[t], 16)
                square(YX[:, t, :], JUNK[:, :], PRE_C[0] + t, sq_pre)
            act.wait_ge(used[M01[-1]], U_FFN1[M01[-1]])
            nc.scalar.activation(MROW[0:2, 0:D].rearrange("p (a n) -> p a n", a=2), PS[0:2, 4:6, :],
                                 ACT.Copy).then_inc(mrow_act, 1)
            make_hi(B1[0], U_FFN1[B1[0]])
            h_full(0)
            for s in (B1[1],) + A1:
                make_hi(s, U_FFN1[s])
            act.wait_ge(ones_set, 1)
            nc.scalar.activation(ONESR[:, :], ONES[:, 0:2], ACT.Copy).then_inc(onesr_set, 1)
            act.wait_ge(zero_set, 1)
            act.dma_start(rpb_rows.rearrange("q h r x -> (q h r x)").rearrange("(p n) -> p n", p=P),
                          ZERO[:, :]).then_inc(rpb_zeroed, 16)
            act.wait_ge(lam_abs, 1)
            nc.scalar.activation(LT[:, 1, :], LT[:, 0, :], ACT.Exp, scale=-1.0).then_inc(lam_exp, 1)
            act.wait_ge(rpb_zeroed, 16)
            for qr in range(ROWS):
                act.dma_start(rpb_rows[qr, :, :, 16:16 + RPB_C],
                              rpb[0, :, ROWS - 1 - qr:2 * ROWS - 1 - qr, :]).then_inc(rpb_put, 16)
            ffn(0, U_FFN1, B1, A1, D1)
            grow_out(0, [(GROW[:, 0, :], 0), (GROW[:, 1, :], 2)])
            post_squares(0)
            for t in (4, 5):
                make_hi(*mix_use(t))
            h_full(1)

            def rec_unit(r):
                j = (r % 2) * RC + r // 2
                act.wait_ge(gates, r + 1)
                if r:
                    act.wait_ge(scanned, r)
                nc.scalar.activation(T[:, 0, :].rearrange("p (h w) -> p h w", h=2), PS[:, 4:6, 0:HSW],
                                     ACT.Sigmoid, bias=C2[:, R_BA + j:R_BA + j + 1]).then_inc(r_sig, 1)
                nc.scalar.activation(T[:, 1, :].rearrange("p (h w) -> p h w", h=2), PS[:, 6:8, 0:HSW],
                                     ACT.Sigmoid, bias=C2[:, R_BX + j:R_BX + j + 1]).then_inc(x_sig, 1)
                act.wait_ge(r_sig, r + 1)
                nc.scalar.activation(T[:, 2, :], T[:, 0, :], ACT.Exp, scale=LOGC[:, j:j + 1])
                nc.scalar.activation(T3[:, :], T[:, 0, :], ACT.Tanh, scale=LOGC[:, j:j + 1]).then_inc(r_at, 1)
                act.wait_ge(om_made, r + 1)
                nc.scalar.activation(T[:, 0, :], T[:, 0, :], ACT.Sqrt, scale=-1.0).then_inc(root, 1)

            t_hi = 6
            act.wait_ge(logc_made, 1)
            for n in range(N_IN):
                while t_hi <= n + 6 and t_hi < T_OUT + 2:
                    make_hi(*mix_use(t_hi))
                    t_hi += 1
                if n in REC_STEP:
                    rec_unit(REC_STEP[n])
                if n >= N_XKVQ:
                    if n == N_XKVQ:
                        act.wait_ge(scanned, 2 * RC)
                    s, u = mix_use(n)
                    act.wait_ge(used[s], u + 1)
                    nc.scalar.activation(GR[:, n - N_XKVQ, :], PS[:, 2 * (n % 2), :], ACT.Gelu_apprx_tanh).then_inc(gelu_out, 1)
            for j in range(10):
                act.wait_ge(vt, j + 1)
                nc.scalar.activation(v_hi(j, slice(0, LAT)), PS[:, j % 4, :], ACT.Copy).then_inc(vt_hi, 1)
            for j in range(RC):
                act.wait_ge(yr_f, j + 1)
                nc.scalar.activation(YRH[j], XR[:, j, 2:2 + LAT], ACT.Copy).then_inc(yr_hi, 1)
            grow_out(1, [(GROW5T[:, :], 6)])
            def exponentials(u):
                act.wait_ge(maxed, u + 1)
                if u >= 2:
                    act.wait_ge(pt_ps, u - 1)
                c0 = u % UNITS
                nc.scalar.activation(PR[:, u % 2, :], PS[:, u % 2, :], ACT.Exp, bias=NMX[:, c0:c0 + 1],
                                     accum_out=DEN[:, c0:c0 + 1]).then_inc(exps, 1)

            def probabilities(u):
                act.wait_ge(exps, u + 1)
                act.wait_ge(inverted, u + 1)
                c0 = u % UNITS
                nc.scalar.activation(PR[:, u % 2, :], PR[:, u % 2, :], ACT.Copy, scale=RDEN[:, c0:c0 + 1]).then_inc(p_made, 1)

            def transposed_hi(u):
                act.wait_ge(pt_ps, u + 1)
                if u >= 4:
                    act.wait_ge(pv, u // 2 - 1)
                nc.scalar.activation(PTH[:, u % 4, :], PS[:, 2 + u % 2, :], ACT.Copy).then_inc(pt_hi, 1)

            def output_hi(p):
                act.wait_ge(pv, NBLK * (p + 1))
                act.wait_ge(yr_lo, RC)
                for h in range(2):
                    ph = slice(DH * h, DH * h + DH)
                    ins = nc.scalar.activation(by_tokens(YAH, ph, p), heads_out(4 + 2 * (p % 2), ph, h), ACT.Copy)
                ins.then_inc(ya_hi, 1)

            exponentials(0)
            for u in range(NU):
                if u:
                    transposed_hi(u - 1)
                probabilities(u)
                if u + 1 < NU:
                    exponentials(u + 1)
                if u % UNITS == 3 and u > UNITS:
                    output_hi(u // UNITS - 1)
            transposed_hi(NU - 1)
            output_hi(HPAIRS - 1)
            act.wait_ge(pv, NU // 2)
            for t in range(T_OUT + 2, N_MIX):
                make_hi(*mix_use(t))
            post_squares(1)
            for s in B2 + A2:
                make_hi(s, U_FFN2[s])
            h_full(2)
            ffn(1, U_FFN2, B2, A2, D2)
            grow_out(2, [(GROW[:, 0, :], 0)])
            post_squares(2)

        @block.gpsimd
        def _(pool):
            own = [0]

            def after_own(ins):
                own[0] += 1
                ins.then_inc(pool_own, 1)
                pool.wait_ge(pool_own, own[0])

            def make_lo(s, u):
                pool.wait_ge(hi_made[s], u - RAW[s] + 1)
                nc.gpsimd.tensor_tensor(WL[:, s, :], WR[:, s, :], WH[:, s, :].bitcast(F32),
                                        ALU.subtract).then_inc(lo_made[s], 1)

            def rstd(col, t, ready, cnt, done):
                pool.wait_ge(ready, cnt)
                after_own(nc.gpsimd.tensor_scalar(MS[:, t:t + 1], SS[:, col:col + 1], EPS, None, ALU.add))
                nc.gpsimd.tensor_tensor(RS[:, col:col + 1], MS[:, t:t + 1], MHALF[:, :], ALU.pow).then_inc(done, 1)

            def diagonal_pre(n, t):
                rstd(PRE_C[n] + t, t, sq_pre, PRE_N[n] + t + 1, rstd_pre)
                pool.wait_ge(rstd_pre, PRE_N[n] + t + 1)
                r = RS[:, PRE_C[n] + t:PRE_C[n] + t + 1].broadcast_to([P, P])
                nc.gpsimd.tensor_tensor(dg(n)[:, t, :], IDENT[:, :], r, ALU.mult).then_inc(dg_made, 1)

            def h_low(n):
                for k in range(KC):
                    pool.wait_ge(h_hi, n * KC + k + 1)
                    nc.gpsimd.tensor_tensor(HL[:, k, LAT:TOK], h32(n, k)[:, LAT:TOK], HH[:, k, LAT:TOK].bitcast(F32),
                                            ALU.subtract).then_inc(h_lo_c, 1)

            def ffn(n, uses, B, A, Dn):
                def tiles(slots, use):
                    for s in slots:
                        make_lo(s, uses[s] + use)

                tiles(B, 1)
                tiles(Dn, 0)
                tiles(A, 1)
                with pool.Fori(0, PAIRS if n == 0 else PAIRS - 1, 1) as i:
                    tiles(B, i + 2)
                    tiles(Dn, i + 1)
                    tiles(A, i + 2)
                if n == 1:
                    tiles(Dn, PAIRS)

            def post(n):
                for t in range(POST_T[n] + 1):
                    if n != 1 and t < POST_T[n] and t % 2 == 0:
                        pool.wait_ge(ysum, t + 1 + (NTT if n == 2 else 0))
                        if t == 0:
                            pool.wait_ge(grow_made, n + 1)
                        else:
                            pool.wait_ge(resid, POST_N[n] + t - 1)
                        nc.gpsimd.tensor_tensor(YG[:, 0, :], y_acc(n // 2, t), GROW[:, 0 if t < NLT else 1, :],
                                                ALU.mult).then_inc(yg_pool, 1)
                    if t < POST_T[n]:
                        rstd(POST_C[n] + t, t, sq_post, POST_N[n] + t + 1, rstd_post)
                    if n < 2 and t >= 1:
                        diagonal_pre(n + 1, t - 1)

            nc.gpsimd.memset(ZERO[:, :], 0.0).then_inc(zero_set, 1)
            after_own(nc.gpsimd.memset(IDENT[:, :], 0.0))
            nc.gpsimd.affine_select(out=IDENT[:, :], in_=IDENT[:, :], compare_op=ALU.not_equal, fill=1.0, base=0,
                                    pattern=[[-1, P]], channel_multiplier=1).then_inc(ident_set, 1)
            nc.gpsimd.memset(MHALF[:, :], -0.5).then_inc(mhalf_set, 1)
            nc.gpsimd.memset(ONES[:, :], 1.0).then_inc(ones_set, 1)
            pool.wait_ge(mhalf_set, 1)
            pool.wait_ge(ident_set, 1)
            for t in range(NTT):
                diagonal_pre(0, t)
            make_lo(B1[0], U_FFN1[B1[0]])
            h_low(0)
            for s in (B1[1],) + A1:
                make_lo(s, U_FFN1[s])
            pool.wait_ge(turned, KC)
            nc.gpsimd.memset(YX[:, :, :], 0.0).then_inc(y_zeroed, 1)
            ffn(0, U_FFN1, B1, A1, D1)
            post(0)
            h_low(1)
            for t in (4, 5):
                make_lo(*mix_use(t))
            pool.wait_ge(turned, 2 * KC)
            nc.gpsimd.memset(GW[:, :, :, :, :], 0.0).then_inc(gw_zeroed, 1)
            pool.wait_ge(h_lo, 2 * KC)
            pool.wait_ge(h_lo_c, 2 * KC)
            for j in range(RC):
                for a, b in ((0, 2), (2 + LAT, 2 + CTX0), (2 + CTX0 + CTX, PADW)):
                    ins = nc.gpsimd.memset(XR[:, j, a:b], 0.0)
            ins.then_inc(pads_zeroed, 1)
            for t in range(6, T_OUT - 1):
                make_lo(*mix_use(t))
            pool.wait_ge(scanned, 2 * RC)
            nc.gpsimd.memset(ONES5[:, :], 1.0).then_inc(ones_set, 1)
            after_own(nc.gpsimd.memset(MASK[:, :, :], 0.0))

            def window(v, x0, n, base_, step, cm):
                part = MASK[:, v, x0:x0 + n]
                after_own(nc.gpsimd.affine_select(out=part, in_=part, compare_op=ALU.is_ge, fill=NEG, base=base_,
                                                  pattern=[[step, n]], channel_multiplier=cm))

            window(0, 0, 16, 64 + 7, 8, -1)
            window(0, 16, 16, 56 - 128, -8, 1)
            window(1, 0, 32, 7, 8, -1)
            window(1, 0, 32, 120, -8, 1)
            window(2, 0, 16, 7 - 64, 8, -1)
            window(2, 16, 16, 184 - 128, -8, 1)
            def mask_bias(v, b):
                view = b.rearrange("p a (r x) -> p a r x", x=KCOLS)
                m = MASK[:, v, :].unsqueeze(1).unsqueeze(1).broadcast_to([P, view.shape[1], view.shape[2], KCOLS])
                nc.gpsimd.tensor_tensor(view, view, m, ALU.add).then_inc(bias_made, 1)

            pool.wait_ge(bias_in, 32)
            mask_bias(0, BIAS0)
            mask_bias(2, BIAS3)
            make_lo(*mix_use(T_OUT - 1))

            def heads(p):
                e = p % 2
                if p >= 2:
                    pool.wait_ge(scores, UNITS * (p - 1))
                else:
                    for s in ((4, 5), (0, 1))[e]:
                        pool.wait_ge(lo_made[s], mix_use((17, T_OUT - 1)[e])[1] - RAW[s] + 1)
                nc.gpsimd.tensor_copy(QH[e][:, :], Q[:, p, :])
                nc.gpsimd.tensor_copy(KH[e][:, :], K[:, p, :]).then_inc(qk_hi, 1)
                pool.wait_ge(qk_hi, p + 1)
                nc.gpsimd.tensor_tensor(QL[e][:, :], Q[:, p, :], QH[e][:, :].bitcast(F32), ALU.subtract)
                nc.gpsimd.tensor_tensor(KL[e][:, :], K[:, p, :], KH[e][:, :].bitcast(F32), ALU.subtract).then_inc(qk_made, 1)

            pool.wait_ge(proj_out, N_XKVQ)
            heads(0)
            for t in range(T_OUT, T_OUT + 2):
                make_lo(*mix_use(t))
            pool.wait_ge(biasm_in, 16)
            mask_bias(1, BIASM)
            heads(1)
            for j in range(RC):
                pool.wait_ge(yr_hi, j + 1)
                nc.gpsimd.tensor_tensor(YRL[j], XR[:, j, 2:2 + LAT], YRH[j].bitcast(F32), ALU.subtract).then_inc(yr_lo, 1)
            pool.wait_ge(yr_lo, RC)
            pool.wait_ge(grow_made, 2)
            nc.gpsimd.tensor_copy(GROW5[:, :], GROW5T[:, :]).then_inc(grow5_made, 1)
            for p in range(2, HPAIRS):
                heads(p)
            for t in range(T_OUT + 2, N_MIX):
                make_lo(*mix_use(t))
            post(1)
            for s in B2 + A2:
                make_lo(s, U_FFN2[s])
            pool.wait_ge(turned, 3 * KC)
            nc.gpsimd.memset(Y2[:, :, :], 0.0).then_inc(y_zeroed, 1)
            nc.gpsimd.memset(ONES[:, :], 1.0).then_inc(ones_set, 1)
            ffn(1, U_FFN2, B2, A2, D2)
            post(2)

        @block.tensor
        def _(pe):
            def turn(n, chunks):
                last = PRE_T[n] - 1

                def part(k, tiles):
                    for t in tiles:
                        bank, col = (2 * (k % 4), t) if t < NLT else (2 * (k % 4) + 1, t - NLT)
                        pe.wait_ge(dg_made, PRE_N[n] + t + 1)
                        ins = nc.tensor.matmul(PS[:, bank, col * P:col * P + P], YX[:, t, k * P:k * P + P],
                                               dg(n)[:, t, :], start=True, stop=True)
                    return ins

                early = [k for k in chunks if k < 4] if n else []
                for k in early:
                    if n == 1 and k == 2:
                        pe.wait_ge(ysum, NTT)
                    if n == 2:
                        pe.wait_ge(yg_dve, NTT // 2 + k + 1)
                    part(k, range(last - 1))
                for k in early:
                    part(k, [last - 1])
                for k in chunks:
                    if k >= 4:
                        pe.wait_ge(h_32, n * KC + k - 3)
                    part(k, [last] if k in early else range(last + 1)).then_inc(turned, 1)

            def project(s, halves, banks, wait_k=None):
                ins = None
                for k in range(KC):
                    if wait_k is not None:
                        pe.wait_ge(h_lo, wait_k + k + 1)
                        if wait_k < 2 * KC:
                            pe.wait_ge(h_lo_c, wait_k + k + 1)
                    wh, wl = WH[:, s, k * P:k * P + P], WL[:, s, k * P:k * P + P]
                    for w, h, first, last in ((wh, HH, True, False), (wh, HL, False, False), (wl, HH, False, True)):
                        for (j, sl, n), bank in zip(halves, banks):
                            ins = nc.tensor.matmul(PS[:, bank, 0:n], w, h[:, k, sl], start=(k == 0 and first),
                                                   stop=(k == KC - 1 and last))
                return ins

            def three(out_ps, lh, ll, rh, rl, first, last):
                nc.tensor.matmul(out_ps, lh, rh, start=first, stop=False)
                nc.tensor.matmul(out_ps, lh, rl, start=False, stop=False)
                return nc.tensor.matmul(out_ps, ll, rh, start=False, stop=last)

            def ffn(n, uses, B, A, Dn):
                ntok, nj, cb, yb = ffn_counts(n)
                ab = added_before(n)
                halves = token_halves(ntok)

                def up(r, use, bank, wait_k=None):
                    slots = (A, B)[r]
                    for g, s in enumerate(slots):
                        pe.wait_ge(lo_made[s], uses[s] - RAW[s] + use + 1)
                        if g == 1 and r == 0 and not (known(use) and use == 0):
                            pe.wait_ge(y_added, (use - 1) * nj + ab + nj)
                        bk = bank + 2 * g
                        project(s, halves, [bk, bk + 1], wait_k if g == 0 else None).then_inc(used[s], 1)
                        if g == 0 and r == 0 and not (known(use) and use == 0):
                            release_down((use - 1) * nj + yb + nj)

                def release_down(y_count):
                    pe.wait_ge(y_ready, y_count)
                    pe.nop().then_inc(used[Dn[1]], 1)

                def down_unit(j, use, bank):
                    t, half = j // 2, j % 2
                    tk = slice(t * P, t * P + P)
                    col = slice(half * HALF_D, half * HALF_D + HALF_D)
                    for q, r in ((0, 1), (1, 0)):
                        s = Dn[q]
                        ins = three(PS[:, bank, :], AH[:, r, tk], AL[:, r, tk], WH[:, s, col], WL[:, s, col],
                                    q == 0, q == 1)
                        if j == nj - 1:
                            if q == 0:
                                ins.then_inc(used[s], 1)
                    return ins

                pe.wait_ge(h_32, n * 2 * KC + KC)
                up(1, 0, 0, wait_k=2 * n * KC)
                up(0, 0, 4)
                if n == 0:
                    pe.wait_ge(onesr_set, 1)

                def pair(i, mod):
                    pe.wait_ge(au_made[1], i + cb + 1)
                    up(1, i + 1, 0)
                    for q in range(2):
                        pe.wait_ge(lo_made[Dn[q]], i + uses[Dn[q]] - RAW[Dn[q]] + 1)
                    for r in range(2):
                        pe.wait_ge(a_lo[r], i + cb + 1)
                    def reduce_mod(chunks):
                        for m in chunks:
                            for r in range(2):
                                c0 = 4 * m + 2 * r
                                nc.tensor.matmul(PS[:, 7, c0:c0 + 2], MH[:, r, m * P:m * P + P], ONESR[:, :],
                                                 start=True, stop=False)
                                ins = nc.tensor.matmul(PS[:, 7, c0:c0 + 2], ML[:, r, m * P:m * P + P], ONESR[:, :],
                                                       start=False, stop=True)
                        return ins

                    for j in range(nj):
                        if mod and j == 3:
                            pe.wait_ge(mod_made, i)
                        if j >= 4:
                            pe.wait_ge(y_added, i * nj + ab + j - 3)
                        down_unit(j, i, 4 + j % 4).then_inc(y_ready, 1)
                        if mod and j < 3:
                            if j == 0:
                                pe.wait_ge(mod_lo, i)
                            ins = reduce_mod(range((0, 3, 5)[j], (3, 5, MOD_CHUNKS)[j]))
                            if j == 2:
                                ins.then_inc(mod_red, 1)
                    pe.wait_ge(y_added, i * nj + ab + nj - 2)
                    up(0, i + 1, 4)

                if n == 0:
                    pair(0, False)
                    with pe.Fori(1, MOD_GROUPS + 1, 1) as i:
                        pair(i, True)
                with pe.Fori(MOD_GROUPS + 1 if n == 0 else 0, PAIRS, 1) as i:
                    pair(i, False)
                pe.wait_ge(au_made[1], cb + PAIRS + 1)
                grow(2 * n, 2 if n == 0 else 1, 0, ONES, DIAG if n == 0 else DIAG2, (1, 3)[n])
                for q in range(2):
                    pe.wait_ge(lo_made[Dn[q]], uses[Dn[q]] - RAW[Dn[q]] + PAIRS + 1)
                for r in range(2):
                    pe.wait_ge(a_lo[r], cb + PAIRS + 1)
                for j in range(nj):
                    if j >= 4 and j % 2 == 0:
                        pe.wait_ge(ysum, n * NTT + j // 2 - 1)
                    down_unit(j, PAIRS, 4 + j % 4).then_inc(y_ready, 1)
                release_down(yb + nj * (PAIRS + 1))

            def grow(n, streams, bank, ones, diag, ones_count):
                pe.wait_ge(ones_set, ones_count)
                pe.wait_ge(diag_made, n + 1)
                for g in range(streams):
                    for k in range(KC):
                        b = bank + 2 * g + k // 4
                        ins = nc.tensor.matmul(PS[:, b, (k % 4) * P:(k % 4) * P + P], ones[:, :],
                                               diag[:, g, k, :], start=True, stop=True)
                ins.then_inc(grow_ps, 1)

            pe.wait_ge(ident_set, 1)
            pe.wait_ge(c_in, 32)
            nc.tensor.transpose(PS[:, 3, 0:2 * KC], R1[0:2 * KC, :], IDENT[0:2 * KC, 0:2 * KC]).then_inc(c_turned, 1)
            pe.wait_ge(cs_made, 1)
            for n in range(NM01):
                s = M01[n]
                pe.wait_ge(landed[s], 16 * M01[:n].count(s) + 16)
                for half in range(2):
                    ins = nc.tensor.matmul(PS[0:2, 4 + 2 * (n % 2) + half, :], CS[:, n // 2, :],
                                           WR[:, s, half * HALF_D:half * HALF_D + HALF_D], start=(n < 2),
                                           stop=(n >= NM01 - 2))
                ins.then_inc(used[s], 1)
            turn(0, (0,))
            pe.wait_ge(rows_in, 128)
            nc.tensor.transpose(PS[:, 2, 0:N_R1], R1[0:N_R1, :], IDENT[0:N_R1, 0:N_R1])
            nc.tensor.transpose(PS[:, 3, 0:N_R2], R2[0:N_R2, :], IDENT[0:N_R2, 0:N_R2]).then_inc(rows_turned, 1)
            pe.wait_ge(mrow_act, 1)
            pe.wait_ge(mrow_dve, 1)
            for m in range(2 * KC):
                ins = nc.tensor.transpose(PS[:, 4, 2 * m:2 * m + 2], MROW[0:2, m * P:m * P + P], IDENT[0:2, 0:2])
            ins.then_inc(mod01_turned, 1)
            pe.wait_ge(c2_made, 1)
            turn(0, (1,))
            pe.wait_ge(mod01_made, 1)
            turn(0, range(2, KC))
            ffn(0, U_FFN1, B1, A1, D1)
            pe.wait_ge(grow_made, 1)
            turn(1, range(KC))
            pe.wait_ge(h_32, 2 * KC)
            lat = (0, slice(0, LAT), LAT)
            both = [lat, (1, slice(LAT, TOK), CTX)]
            for n in range(N_IN):
                s, u = mix_use(n)
                pe.wait_ge(lo_made[s], u - RAW[s] + 1)
                if 2 <= n < N_XKVQ + 2:
                    pe.wait_ge(proj_out, n - 1)
                elif n >= N_XKVQ + 2:
                    pe.wait_ge(gelu_out, n - N_XKVQ - 1)
                b = 2 * (n % 2)
                ins = project(s, both if n < 12 else [lat], [b, b + 1], wait_k=KC if n == 0 else None)
                ins.then_inc(used[s], 1)
                if n in REC_STEP:
                    r = REC_STEP[n]
                    cc, d = r // 2, r % 2
                    pe.wait_ge(xc_made, cc + 1)
                    if r == 0:
                        pe.wait_ge(gw_in, 64)
                    else:
                        pe.wait_ge(x_sig, r)
                    for g in range(2):
                        for h in range(2):
                            ins = nc.tensor.matmul(PS[:, 4 + 2 * g + h, 0:HSW], GW[:, g, d, cc, :],
                                                   XC[:, HSW * h:HSW * h + HSW], start=True, stop=True)
                    ins.then_inc(gates, 1)
            pe.wait_ge(gelu_out, N_IN - N_XKVQ)
            for j in range(10):
                if j >= 4:
                    pe.wait_ge(vt_lo, j - 3)
                for t in range(HPAIRS):
                    if j < 8:
                        k0 = ROWS * KSTART[j // 2] + P * (j % 2)
                        src = V[:, t, k0:k0 + P]
                    else:
                        src = V[:, t, LAT + (j - 8) * P:LAT + (j - 7) * P]
                    ins = nc.tensor.transpose(PS[:, j % 4, t * P:t * P + P], src, IDENT[:, :])
                ins.then_inc(vt, 1)
            pe.wait_ge(x_sig, 2 * RC)
            grow(1, 1, 6, ONES5, DIAG5, 2)
            pe.wait_ge(x_sig, 2 * RC)
            pe.wait_ge(vt_lo, 10)
            def score(u):
                p, b, h = u // UNITS, u % UNITS // 2, u % 2
                ph = slice(DH * h, DH * h + DH)
                if u % UNITS == 0:
                    pe.wait_ge(qk_made, p + 1)
                if u >= 2:
                    pe.wait_ge(exps, u - 1)
                q, e = slice(b * P, b * P + P), p % 2
                for dst, keys in ((0, slice(ROWS * KSTART[b], ROWS * KSTART[b] + LOCK)), (LOCK, slice(LAT, TOK))):
                    n = keys.stop - keys.start
                    ins = three(PS[:, u % 2, dst:dst + n], QH[e][ph, q], QL[e][ph, q], KH[e][ph, keys],
                                KL[e][ph, keys], True, True)
                ins.then_inc(scores, 1)

            def weighted_sums(blk):
                p, b = blk // NBLK, blk % NBLK
                pe.wait_ge(pt_lo, 2 * blk + 2)
                if b == 0 and p == 1:
                    pe.wait_ge(grow_made, 2)
                if b == 0 and p >= 2:
                    pe.wait_ge(ya_lo, p - 1)
                bank, col = 4 + 2 * (p % 2) + b // 2, 2 * P * (b % 2)
                r0 = 2 * (blk % 2)
                for j in range(4):
                    r = 2 * b + j if j < 2 else 6 + j
                    feats, k = slice(p * P, p * P + P), slice(j * P, j * P + P)
                    ins = three(PS[:, bank, col:col + 2 * P], v_hi(r, feats), v_lo(r, feats), PTH[:, r0:r0 + 2, k],
                                PTL[:, r0:r0 + 2, k], j == 0, j == 3)
                ins.then_inc(pv, 1)

            score(0)
            score(1)
            for u in range(NU):
                if u + 2 < NU:
                    score(u + 2)
                pe.wait_ge(p_made, u + 1)
                if u >= 2:
                    pe.wait_ge(pt_lo, u - 1)
                for j in range(4):
                    ins = nc.tensor.transpose(PS[:, 2 + u % 2, j * P:j * P + P], PR[:, u % 2, j * P:j * P + P],
                                              IDENT[:, :])
                ins.then_inc(pt_ps, 1)
                if u % 2 == 1 and u >= 3:
                    weighted_sums(u // 2 - 1)
            weighted_sums(NU // 2 - 1)
            pe.wait_ge(yr_lo, RC)
            for k in range(4):
                s, u = mix_use(T_OUT + k)
                pe.wait_ge(lo_made[s], u - RAW[s] + 1)
                for j in range(8):
                    t, half = j // 2, j % 2
                    if k == 0 and j == 2:
                        pe.wait_ge(pt_lo, NU)
                    if k == 0 and j in (4, 6):
                        pe.wait_ge(ya_lo, HPAIRS - 1 + (j - 4) // 2)
                    tk = slice(t * P, t * P + P)
                    col = slice(half * HALF_D, half * HALF_D + HALF_D)
                    ins = three(PS[:, j, :], YRH[k][:, tk], YRL[k][:, tk], WH[:, s, col], WL[:, s, col], k == 0, False)
                ins.then_inc(used[s], 1)
            for t in range(NLT):
                tk = slice(t * P, t * P + P)
                for half in range(2):
                    col = slice(half * HALF_D, half * HALF_D + HALF_D)
                    for k in range(4):
                        s, u = mix_use(T_OUT + 4 + k)
                        if t == 0 and half == 0:
                            pe.wait_ge(lo_made[s], u - RAW[s] + 1)
                        ins = three(PS[:, 2 * t + half, :], YAH[:, k, tk], YAL[:, k, tk], WH[:, s, col], WL[:, s, col],
                                    False, k == 3)
                ins.then_inc(wo_done, 1)
            pe.wait_ge(wo_done, NLT)
            for k in range(4):
                pe.nop().then_inc(used[mix_use(T_OUT + 4 + k)[0]], 1)
            turn(2, range(KC))
            ffn(1, U_FFN2, B2, A2, D2)

        @block.vector
        def _(dve):
            own = [0]

            def after_own(ins):
                own[0] += 1
                ins.then_inc(dve_own, 1)
                dve.wait_ge(dve_own, own[0])

            def a_columns(n):
                g = C1[:, R_PRE + KC * n:R_PRE + KC * n + KC].unsqueeze(2).broadcast_to([P, KC, 2])
                nc.vector.scalar_tensor_tensor(out=APRE[:, :, :], in0=MOD[:, 24 * n + 8:24 * n + 16, :], scalar=1.0,
                                               in1=g, op0=ALU.add, op1=ALU.mult).then_inc(a_made, 1)

            def diagonal(n, streams, diag, res_w):
                g = C2[:, R_POST + KC * n:R_POST + KC * n + KC].unsqueeze(2).broadcast_to([P, KC, 2])
                after_own(nc.vector.scalar_tensor_tensor(out=GCOL[:, :, :], in0=MOD[:, 24 * n + 16:24 * n + 24, :],
                                                         scalar=res_w, in1=g, op0=ALU.mult, op1=ALU.mult))
                for r in range(streams):
                    for k in range(KC):
                        ins = nc.vector.tensor_scalar(diag[:, r, k, :], IDENT[:, :], GCOL[:, k, r:r + 1], None, ALU.mult)
                ins.then_inc(diag_made, 1)

            def h_high(n):
                w = TOK if PRE_T[n] == NTT else LAT
                for k in range(KC + 1):
                    if k < KC:
                        dve.wait_ge(h_32, n * KC + k + 1)
                        nc.vector.tensor_copy(HH[:, k, 0:w], h32(n, k)[:, 0:w]).then_inc(h_hi, 1)
                    if k:
                        q = k - 1
                        dve.wait_ge(h_hi, n * KC + q + 1)
                        nc.vector.tensor_tensor(HL[:, q, 0:LAT], h32(n, q)[:, 0:LAT], HH[:, q, 0:LAT].bitcast(F32),
                                                ALU.subtract).then_inc(h_lo, 1)

            def ffn(n, uses, B, A):
                ntok, nj, cb, yb = ffn_counts(n)
                nh = len(token_halves(ntok))

                def times_u(r, cnt, bank):
                    dve.wait_ge(silu_made[r], cnt)
                    g = (A, B)[r][1]
                    dve.wait_ge(used[g], cnt + uses[g] - cb)
                    s = SG[:, r, 0:ntok].rearrange("p (h w) -> p h w", h=nh)
                    nc.vector.tensor_tensor(s, s, PS[:, bank:bank + nh, 0:ntok // nh], ALU.mult).then_inc(au_made[r], 1)
                    dve.wait_ge(a_hi[r], cnt)
                    nc.vector.tensor_tensor(AL[:, r, 0:ntok], SG[:, r, 0:ntok], AH[:, r, 0:ntok].bitcast(F32),
                                            ALU.subtract).then_inc(a_lo[r], 1)

                times_u(1, cb + 1, 2)
                times_u(0, cb + 1, 6)
                dve.wait_ge(y_zeroed, n + 1)
                def mod_products(i, blocks):
                    for k in blocks:
                        if k % 2 == 0:
                            dve.wait_ge(mod_in[(k // 2) % 2], i * 32 + 16 * (k // 4) + 16)
                        for r in range(2):
                            src = MRAW[:, (k // 2) % 2, k % 2, :]
                            if k == 0:
                                ins = nc.vector.tensor_scalar(MACC[:, r, :], src, CS[:, 0, r:r + 1], None, ALU.mult)
                            else:
                                dve.wait_ge(mod_own, i * 16 + 2 * k + r - 1)
                                ins = nc.vector.scalar_tensor_tensor(
                                    out=MACC[:, r, :], in0=src, scalar=CS[:, k, r:r + 1], in1=MACC[:, r, :],
                                    op0=ALU.mult, op1=ALU.add)
                            ins.then_inc(mod_own, 1)

                def pair(i, mod=False, reduced=False, last=False):
                    if mod:
                        mod_products(i, range(KC // 2))
                    def finish_mod():
                        dve.wait_ge(mod_red, i)
                        cols = bass.ds(i * MOD_CHUNKS + 16 - MOD_CHUNKS, MOD_CHUNKS)
                        bm = C1[:, bass.ds(i * MOD_CHUNKS + 16 + R_BMOD - MOD_CHUNKS, MOD_CHUNKS)]
                        nc.vector.tensor_tensor(MOD[:, cols, :],
                                                PS[:, 7, 0:4 * MOD_CHUNKS].rearrange("p (m r a) -> p m r a", r=2, a=2)[:, :, :, 0],
                                                bm.unsqueeze(2).broadcast_to([P, MOD_CHUNKS, 2]), ALU.add).then_inc(mod_made, 1)
                    for j in range(nj):
                        dve.wait_ge(y_ready, i * nj + yb + j + 1)
                        y = y_acc(n, j // 2)[:, HALF_D * (j % 2):HALF_D * (j % 2) + HALF_D]
                        nc.vector.tensor_tensor(y, y, PS[:, 4 + j % 4, :], ALU.add).then_inc(y_added, 1)
                        if reduced and j == 1:
                            finish_mod()
                    times_u(1, i + cb + 2, 2)
                    if mod:
                        mod_products(i, range(KC // 2, KC))
                        dve.wait_ge(mod_hi, i + 1)
                        nc.vector.tensor_tensor(ML[:, :, :], MACC[:, :, :], MH[:, :, :].bitcast(F32),
                                                ALU.subtract).then_inc(mod_lo, 1)
                        dve.wait_ge(mod_lo, i + 1)
                    if last:
                        dve.wait_ge(mod_made, MOD_GROUPS)
                        diagonal(0, 2, DIAG, 0.5)
                    times_u(0, i + cb + 2, 6)

                assert MOD_GROUPS == PAIRS - 2
                if n == 0:
                    pair(0, mod=True)
                    with dve.Fori(1, MOD_GROUPS, 1) as i:
                        pair(i, mod=True, reduced=True)
                    pair(MOD_GROUPS, reduced=True)
                    pair(PAIRS - 1, last=True)
                else:
                    with dve.Fori(0, PAIRS, 1) as i:
                        pair(i)

            def post(n):
                tiles = POST_T[n]
                yb = {0: PAIRS * 2 * NTT, 2: (PAIRS + 1) * 2 * NTT + PAIRS * 2 * NLT}.get(n)

                def rest(q):
                    dve.wait_ge(rstd_post, POST_N[n] + q + 1)
                    c0 = POST_C[n] + q
                    if n == 1:
                        yg = YX[:, NLT + q % 2, :]
                        dve.wait_ge(yg_dve, yg_b + q + 1)
                    else:
                        yg = YG[:, q % 2, :]
                        if q % 2 == 0:
                            dve.wait_ge(yg_pool, yg_pb + q // 2 + 1)
                        else:
                            dve.wait_ge(yg_dve, yg_b + q // 2 + 1)
                    x0 = YX[:, q, :]
                    if n == 0:
                        dve.wait_ge(xst_in[q % 2], 16 * (q // 2 + 1))
                        x0 = XST[:, q % 2, :]
                    nc.vector.scalar_tensor_tensor(out=YX[:, q, :], in0=yg, scalar=RS[:, c0:c0 + 1], in1=x0, op0=ALU.mult,
                                                   op1=ALU.add).then_inc(resid, 1)

                yg_b, yg_pb = (0, NTT // 2, NTT // 2 + NLT)[n], (0, 0, NTT // 2)[n]
                for t in range(tiles):
                    if n == 1:
                        if t == 0:
                            dve.wait_ge(grow5_made, 1)
                        if t >= 2:
                            dve.wait_ge(resid, POST_N[n] + t - 1)
                        dve.wait_ge(sq_post, POST_N[n] + t + 1)
                        nc.vector.tensor_tensor(YX[:, NLT + t % 2, :], PS[:, 2 * t:2 * t + 2, :].rearrange("p a n -> p (a n)"),
                                                GROW5[:, :], ALU.mult).then_inc(yg_dve, 1)
                        rest(t)
                        continue
                    dve.wait_ge(y_ready, yb + 2 * t + 2)
                    b = 4 + 2 * (t % 2)
                    y = y_acc(n // 2, t)
                    y2 = y.rearrange("p (a n) -> p a n", a=2)
                    nc.vector.tensor_tensor(y2, y2, PS[:, b:b + 2, :], ALU.add).then_inc(ysum, 1)
                    if t % 2 == 1:
                        if t >= 3:
                            dve.wait_ge(resid, POST_N[n] + t - 1)
                        else:
                            dve.wait_ge(grow_made, n + 1)
                        dve.wait_ge(ysum, t + 1 + (NTT if n == 2 else 0))
                        nc.vector.tensor_tensor(YG[:, 1, :], y, GROW[:, 0 if t < NLT else 1, :], ALU.mult).then_inc(yg_dve, 1)
                    if t >= 1:
                        rest(t - 1)
                if n != 1:
                    rest(tiles - 1)

            dve.wait_ge(used[M01[-1]], U_FFN1[M01[-1]])
            nc.vector.tensor_copy(MROW[0:2, D:2 * D].rearrange("p (a n) -> p a n", a=2), PS[0:2, 6:8, :]).then_inc(mrow_dve, 1)
            dve.wait_ge(rows_turned, 1)
            nc.vector.tensor_copy(C1[:, :], PS[:, 2, 0:N_R1]).then_inc(c1_made, 1)
            nc.vector.tensor_copy(C2[:, :], PS[:, 3, 0:N_R2]).then_inc(c2_made, 1)
            dve.wait_ge(c1_made, 1)
            dve.wait_ge(mod01_turned, 1)
            nc.vector.tensor_tensor(MOD[:, 0:2 * KC, :], PS[:, 4, 0:4 * KC].rearrange("p (m a) -> p m a", a=2),
                                    C1[:, R_BMOD:R_BMOD + 2 * KC].unsqueeze(2).broadcast_to([P, 2 * KC, 2]),
                                    ALU.add).then_inc(mod01_made, 1)
            dve.wait_ge(mod01_made, 1)
            a_columns(0)
            h_high(0)
            dve.wait_ge(c2_made, 1)
            lam = C2[:, R_LAM:R_LAM + 8]
            neg, e, s1, s2, acc, mn = LT[:, 0, :], LT[:, 1, :], LT[:, 2, :], LT[:, 3, :], LT[:, 4, :], LT[:, 5, :]
            after_own(nc.vector.tensor_scalar(neg, lam, -1.0, None, ALU.mult))
            nc.vector.tensor_tensor(neg, neg, lam, ALU.max).then_inc(lam_abs, 1)
            dve.wait_ge(lam_exp, 1)
            after_own(nc.vector.tensor_scalar(s2, e, 2.0, None, ALU.add))
            after_own(nc.vector.reciprocal(s1, s2))
            after_own(nc.vector.tensor_tensor(s1, s1, e, ALU.mult))
            after_own(nc.vector.tensor_tensor(s2, s1, s1, ALU.mult))
            after_own(nc.vector.tensor_scalar(acc, s2, 1.0 / 19, None, ALU.mult))
            for d in (17, 15, 13, 11, 9, 7, 5, 3):
                after_own(nc.vector.scalar_tensor_tensor(out=acc, in0=acc, scalar=1.0 / d, in1=s2, op0=ALU.add, op1=ALU.mult))
            after_own(nc.vector.scalar_tensor_tensor(out=acc, in0=acc, scalar=1.0, in1=s1, op0=ALU.add, op1=ALU.mult))
            after_own(nc.vector.tensor_scalar(mn, lam, 0.0, LRU_C, ALU.min, ALU.mult))
            nc.vector.scalar_tensor_tensor(out=LOGC[:, :], in0=acc, scalar=-2.0 * LRU_C, in1=mn, op0=ALU.mult,
                                           op1=ALU.add).then_inc(logc_made, 1)
            ffn(0, U_FFN1, B1, A1)
            dve.wait_ge(h_32, KC)
            a_columns(1)
            post(0)
            h_high(1)

            def project_out(n):
                s, u = mix_use(n)
                dve.wait_ge(used[s], u + 1)
                g, t, b = n // 4, n % 4, 2 * (n % 2)
                if n == 0:
                    dve.wait_ge(pads_zeroed, 1)
                if g == 0:
                    nc.vector.tensor_copy(XR[:, t, 2:2 + LAT], PS[:, b, :])
                    ins = nc.vector.tensor_copy(XR[:, t, 2 + CTX0:2 + CTX0 + CTX], PS[:, b + 1, 0:CTX])
                elif g == 3:
                    ins = nc.vector.tensor_scalar(Q[:, t, :].rearrange("p (c r) -> p r c", r=ROWS),
                                                  PS[:, b, :].rearrange("p (r c) -> p r c", r=ROWS), DH ** -0.5, None,
                                                  ALU.mult)
                else:
                    dst = (K, V)[g - 1]
                    ins = nc.vector.tensor_copy(dst[:, t, 0:LAT].rearrange("p (c r) -> p r c", r=ROWS),
                                                PS[:, b, :].rearrange("p (r c) -> p r c", r=ROWS))
                    ins = nc.vector.tensor_copy(dst[:, t, LAT:TOK], PS[:, b + 1, 0:CTX])
                ins.then_inc(proj_out, 1)

            def conv(cc):
                w = [C2[:, R_CW + 4 * j + cc:R_CW + 4 * j + cc + 1] for j in range(4)]
                if cc:
                    dve.wait_ge(gates, 2 * cc)
                dve.wait_ge(proj_out, cc + 1)
                after_own(nc.vector.tensor_scalar(XC[:, :], XR[:, cc, 0:SCANW], w[0], C2[:, R_CB + cc:R_CB + cc + 1],
                                                  ALU.mult, ALU.add))
                for j in range(1, 4):
                    ins = nc.vector.scalar_tensor_tensor(out=XC[:, :], in0=XR[:, cc, j:j + SCANW], scalar=w[j],
                                                         in1=XC[:, :], op0=ALU.mult, op1=ALU.add)
                    if j < 3:
                        after_own(ins)
                ins.then_inc(xc_made, 1)

            def rec_unit(r):
                cc, d = r // 2, r % 2
                y = XR[:, cc, 2:2 + LAT]
                r1, a, u, hs = T[:, 1, :], T[:, 2, :], T[:, 0, :], T[:, 1, :]
                dve.wait_ge(xc_made, cc + 1)
                dve.wait_ge(x_sig, r + 1)
                after_own(nc.vector.tensor_tensor(r1, r1, XC[:, :], ALU.mult))
                dve.wait_ge(r_at, r + 1)
                after_own(nc.vector.tensor_tensor(u, a, a, ALU.mult))
                nc.vector.scalar_tensor_tensor(out=u, in0=u, scalar=1.0, in1=T3[:, :], op0=ALU.add,
                                               op1=ALU.mult).then_inc(om_made, 1)
                dve.wait_ge(root, r + 1)
                after_own(nc.vector.tensor_tensor(u, u, r1, ALU.mult))

                def part(t, lo, n):
                    v = t[:, lo:lo + n]
                    return v if d == 0 else v[:, ::-1]

                last = CTX0 + (CTX - 1 if d == 0 else 0)
                after_own(nc.vector.tensor_tensor_scan(part(hs, CTX0, CTX), part(a, CTX0, CTX), part(u, CTX0, CTX), 0.0,
                                                       ALU.mult, ALU.add))
                if d == 0:
                    nc.vector.tensor_tensor_scan(y, a[:, 0:LAT], u[:, 0:LAT], hs[:, last:last + 1],
                                                 ALU.mult, ALU.add).then_inc(scanned, 1)
                else:
                    after_own(nc.vector.tensor_tensor_scan(part(hs, 0, LAT), part(a, 0, LAT), part(u, 0, LAT),
                                                           hs[:, last:last + 1], ALU.mult, ALU.add))
                    dve.wait_ge(scanned, r)
                    nc.vector.tensor_tensor(y, y, hs[:, 0:LAT], ALU.add).then_inc(scanned, 1)

            for n in range(N_XKVQ):
                project_out(n)
                if n == 0:
                    conv(0)
                if n in REC_STEP:
                    r = REC_STEP[n]
                    rec_unit(r)
                    if r % 2 == 1 and r < 7:
                        conv(r // 2 + 1)
            diagonal(1, 1, DIAG5, 1.0)
            dve.wait_ge(h_32, 2 * KC)
            a_columns(2)
            dve.wait_ge(scanned, 2 * RC)
            for j in range(RC):
                y = XR[:, j, 2:2 + LAT]
                dve.wait_ge(gelu_out, j + 1)
                nc.vector.tensor_tensor(y, y, GR[:, j, :], ALU.mult).then_inc(yr_f, 1)
            for j in range(10):
                if j == 8:
                    s, u = mix_use(T_OUT)
                    dve.wait_ge(lo_made[s], u - RAW[s] + 1)
                dve.wait_ge(vt_hi, j + 1)
                nc.vector.tensor_tensor(v_lo(j, slice(0, LAT)), PS[:, j % 4, :], v_hi(j, slice(0, LAT)).bitcast(F32),
                                        ALU.subtract).then_inc(vt_lo, 1)
            dve.wait_ge(bias_made, 3)

            def row_max(u):
                p, b, h = u // UNITS, u % UNITS // 2, u % 2
                dve.wait_ge(scores, u + 1)
                if b in (0, 3):
                    bias = (BIAS0 if b == 0 else BIAS3)[:, 2 * p + h, :]
                else:
                    bias = BIASM[:, p, LOCK * h:LOCK * h + LOCK]
                s = PS[:, u % 2, 0:LOCK].rearrange("p (x r) -> p x r", r=ROWS)
                nc.vector.tensor_tensor(s, s, bias.rearrange("p (r x) -> p x r", r=ROWS), ALU.add).then_inc(biased, 1)
                dve.wait_ge(biased, u + 1)
                c0 = u % UNITS
                nc.vector.tensor_reduce(NMX[:, c0:c0 + 1], PS[:, u % 2, :], AX_X, ALU.max, negate=True).then_inc(maxed, 1)

            def transposed_lo(u):
                dve.wait_ge(pt_hi, u + 1)
                nc.vector.tensor_tensor(PTL[:, u % 4, :], PS[:, 2 + u % 2, :], PTH[:, u % 4, :].bitcast(F32),
                                        ALU.subtract).then_inc(pt_lo, 1)

            def invert(u):
                c0 = u % UNITS
                dve.wait_ge(exps, u + 1)
                nc.vector.reciprocal(RDEN[:, c0:c0 + 1], DEN[:, c0:c0 + 1]).then_inc(inverted, 1)

            def output_lo(p):
                dve.wait_ge(ya_hi, p + 1)
                dve.wait_ge(grow5_made, 1)
                for h in range(2):
                    ph = slice(DH * h, DH * h + DH)
                    ins = nc.vector.tensor_tensor(by_tokens(YAL, ph, p), heads_out(4 + 2 * (p % 2), ph, h),
                                                  by_tokens(YAH, ph, p).bitcast(F32), ALU.subtract)
                ins.then_inc(ya_lo, 1)

            row_max(0)
            for u in range(NU):
                invert(u)
                if u + 1 < NU:
                    row_max(u + 1)
                if u:
                    transposed_lo(u - 1)
                if u % UNITS == 4 and u > UNITS:
                    output_lo(u // UNITS - 1)
            transposed_lo(NU - 1)
            output_lo(HPAIRS - 1)
            post(1)
            h_high(2)
            diagonal(2, 1, DIAG2, 0.5)
            ffn(1, U_FFN2, B2, A2)
            post(2)


_INS = ["x", "c", "ctx", "c_ctx", "w_mod", "b_mod", "norm_pre", "norm_post", "ffn1_w_gu", "ffn1_w_down", "ffn2_w_gu",
        "ffn2_w_down", "w_in", "w_out", "conv_w", "conv_b", "lru_wa", "lru_ba", "lru_wx", "lru_bx", "lru_lambda",
        "na_rpb"]


def kernel(**inputs):
    import numpy as _np
    import concourse.bacc as _bacc
    from concourse import mybir as _mybir
    from concourse.bass_utils import run_bass_kernel_spmd as _run

    nc = _bacc.Bacc("TRN2", target_bir_lowering=False, num_devices=1)
    arrays, args = {}, []
    for name in _INS:
        a = _np.ascontiguousarray(inputs[name])
        arrays[f"in_{name}"] = a
        args.append(nc.dram_tensor(f"in_{name}", a.shape, _mybir.dt.from_np(a.dtype), kind="ExternalInput").ap())
    args.append(nc.dram_tensor("out_dram", (1, LAT, D), _mybir.dt.float32, kind="ExternalOutput").ap())
    build(nc, *args)
    r = _run(nc, [arrays], core_ids=[0])
    return r.results[0]["out_dram"]
```
